# Optimizing a Trainium2 kernel written in Bass

```python
import math
import jax, jax.numpy as jnp
from jax import lax
import numpy as np

D_MODEL = 1024
BATCH = 1
SEQ = 512
DEPTH = 1

ATTN_HEADS = 8
ATTN_HEAD_DIM = 64
ATTN_V_DIM = 2 * ATTN_HEAD_DIM
ATTN_QK_WIDTH = ATTN_HEADS * 2 * ATTN_HEAD_DIM
ATTN_V_WIDTH = ATTN_HEADS * ATTN_V_DIM
ROPE_THETA = 10000.0
Q_BLOCK = 128
SSD_D_INNER = 2 * D_MODEL
SSD_HEAD_DIM = 64
SSD_HEADS = SSD_D_INNER // SSD_HEAD_DIM
SSD_GROUPS = 4
SSD_HEADS_PER_GROUP = SSD_HEADS // SSD_GROUPS
SSD_D_STATE = 128
SSD_CONV = 4
SSD_CHUNK = 128
SSD_CONV_DIM = SSD_D_INNER + 2 * SSD_GROUPS * SSD_D_STATE
IN_SIZES = (ATTN_QK_WIDTH, ATTN_QK_WIDTH, ATTN_V_WIDTH, D_MODEL, D_MODEL, SSD_D_INNER, SSD_CONV_DIM, SSD_HEADS)
IN_WIDTH = ATTN_QK_WIDTH * 2 + ATTN_V_WIDTH + 2 * D_MODEL + SSD_D_INNER + SSD_CONV_DIM + SSD_HEADS
N_EXPERTS = 64
TOP_K = 8
N_EXPERT_GROUPS = 8
TOPK_GROUPS = 4
EXPERT_DIM = 256
SHARED_DIM = 256
ROUTED_SCALE = 2.5
MOE_TOKEN_BLOCK = 128
EPS = 1e-6

kernel_name = "hybrid_diffattn_ssd_moe_adaln"

def rmsnorm(x, g):
    x32 = x.astype(jnp.float32)
    r = x32 * lax.rsqrt(jnp.mean(x32 * x32, axis=-1, keepdims=True) + EPS)
    return (r * g.astype(jnp.float32)).astype(x.dtype)

def rope(x, positions):
    d = x.shape[-1]
    half = d // 2
    inv_freq = ROPE_THETA ** (-jnp.arange(half, dtype=jnp.float32) * 2.0 / d)
    ang = positions.astype(jnp.float32)[..., None] * inv_freq
    ang = ang.reshape(ang.shape[:2] + (1,) * (x.ndim - 3) + (half,))
    cos, sin = jnp.cos(ang), jnp.sin(ang)
    x32 = x.astype(jnp.float32)
    x1, x2 = x32[..., :half], x32[..., half:]
    return jnp.concatenate([x1 * cos - x2 * sin, x2 * cos + x1 * sin], axis=-1).astype(x.dtype)

def diff_attention(q, k, v, positions, qn_g, kn_g, lam_vecs, subln_g, lambda_init):
    b, s, h, _, d = q.shape
    q = rope(rmsnorm(q, qn_g), positions) * (d ** -0.5)
    k = rope(rmsnorm(k, kn_g), positions)
    lv = lam_vecs.astype(jnp.float32)
    lam = jnp.exp(jnp.sum(lv[0] * lv[1])) - jnp.exp(jnp.sum(lv[2] * lv[3])) + lambda_init
    nblk = s // Q_BLOCK
    qb = q.reshape(b, nblk, Q_BLOCK, h, 2, d).transpose(1, 0, 2, 3, 4, 5)
    key_idx = jnp.arange(s)

    def block(args):
        q_blk, i = args
        scores = jnp.einsum('bqhmd,bkhmd->bhmqk', q_blk, k).astype(jnp.float32)
        q_idx = i * Q_BLOCK + jnp.arange(Q_BLOCK)
        mask = key_idx[None, :] <= q_idx[:, None]
        p = jax.nn.softmax(jnp.where(mask, scores, -jnp.inf), axis=-1)
        w = p[:, :, 0] - lam * p[:, :, 1]
        return jnp.einsum('bhqk,bkhe->bqhe', w.astype(v.dtype), v)

    o = lax.map(block, (qb, jnp.arange(nblk)))
    o = o.transpose(1, 0, 2, 3, 4).reshape(b, s, h, ATTN_V_DIM)
    o = rmsnorm(o, subln_g) * (1.0 - lambda_init)
    return o.reshape(b, s, h * ATTN_V_DIM)

def causal_depthwise_conv(u, w, bias):
    ch = u.shape[-1]
    out = lax.conv_general_dilated(u, w[:, None, :].astype(u.dtype), window_strides=(1,),
                                   padding=[(SSD_CONV - 1, 0)],
                                   dimension_numbers=('NWC', 'WIO', 'NWC'),
                                   feature_group_count=ch)
    return out + bias

def segsum_exp(a_cum):
    l = a_cum.shape[-1]
    diff = a_cum[..., :, None] - a_cum[..., None, :]
    mask = jnp.tril(jnp.ones((l, l), dtype=bool))
    return jnp.exp(jnp.where(mask, diff, -jnp.inf))

def ssd_chunked(x, a, bm, cm):
    b, s, g, j, p = x.shape
    n = bm.shape[-1]
    c, l = s // SSD_CHUNK, SSD_CHUNK
    x = x.reshape(b, c, l, g, j, p)
    bm = bm.reshape(b, c, l, g, n)
    cm = cm.reshape(b, c, l, g, n)
    a = a.reshape(b, c, l, g, j).transpose(0, 3, 4, 1, 2).astype(jnp.float32)
    a_cum = jnp.cumsum(a, axis=-1)
    lmat = segsum_exp(a_cum)
    cb = jnp.einsum('bclgn,bcsgn->bgcls', cm, bm)
    y_diag = jnp.einsum('bgcls,bgjcls,bcsgjp->bclgjp', cb, lmat, x)
    decay_states = jnp.exp(a_cum[..., -1:] - a_cum)
    states = jnp.einsum('bclgn,bgjcl,bclgjp->bcgjpn', bm, decay_states, x)
    chunk_decay = jnp.exp(a_cum[..., -1])

    def step(hstate, inp):
        st, dec = inp
        return hstate * dec[..., None, None] + st, hstate

    h0 = jnp.zeros((b, g, j, p, n), jnp.float32)
    _, prev = lax.scan(step, h0, (states.transpose(1, 0, 2, 3, 4, 5).astype(jnp.float32),
                                  chunk_decay.transpose(3, 0, 1, 2)))
    y_off = jnp.einsum('bclgn,cbgjpn,bgjcl->bclgjp', cm, prev, jnp.exp(a_cum))
    return (y_diag + y_off).reshape(b, s, g, j, p)

def ssd_mixer(z, xbc, dt, conv_w, conv_b, dt_bias, a_log, d_skip, norm_g):
    b, s, _ = z.shape
    xbc = jax.nn.silu(causal_depthwise_conv(xbc, conv_w, conv_b))
    gn = SSD_GROUPS * SSD_D_STATE
    xs = xbc[..., :SSD_D_INNER].reshape(b, s, SSD_GROUPS, SSD_HEADS_PER_GROUP, SSD_HEAD_DIM)
    bm = xbc[..., SSD_D_INNER:SSD_D_INNER + gn].reshape(b, s, SSD_GROUPS, SSD_D_STATE)
    cm = xbc[..., SSD_D_INNER + gn:].reshape(b, s, SSD_GROUPS, SSD_D_STATE)
    dtp = jax.nn.softplus(dt.astype(jnp.float32) + dt_bias.astype(jnp.float32))
    dtp = dtp.reshape(b, s, SSD_GROUPS, SSD_HEADS_PER_GROUP)
    a_neg = -jnp.exp(a_log.astype(jnp.float32)).reshape(SSD_GROUPS, SSD_HEADS_PER_GROUP)
    y = ssd_chunked(xs * dtp[..., None], dtp * a_neg, bm, cm)
    y = y + xs * d_skip.reshape(SSD_GROUPS, SSD_HEADS_PER_GROUP)[..., None]
    y = y.reshape(b, s, SSD_D_INNER).astype(z.dtype) * jax.nn.silu(z)
    y = rmsnorm(y.reshape(b, s, SSD_GROUPS, SSD_D_INNER // SSD_GROUPS),
                norm_g.reshape(SSD_GROUPS, SSD_D_INNER // SSD_GROUPS))
    return y.reshape(b, s, SSD_D_INNER)

def moe_ffn(h, w_router, router_bias, w_eg, w_eu, w_ed, w_sg, w_su, w_sd):
    b, s, d = h.shape
    t = h.reshape(b * s, d)
    ntok = b * s
    scores = jax.nn.sigmoid((t @ w_router).astype(jnp.float32))
    choice = scores + router_bias.astype(jnp.float32)
    per_group = N_EXPERTS // N_EXPERT_GROUPS
    grp_score = lax.top_k(choice.reshape(ntok, N_EXPERT_GROUPS, per_group), 2)[0].sum(-1)
    _, top_grp = lax.top_k(grp_score, TOPK_GROUPS)
    grp_mask = jax.nn.one_hot(top_grp, N_EXPERT_GROUPS, dtype=jnp.float32).sum(-2)
    expert_mask = jnp.repeat(grp_mask, per_group, axis=-1) > 0
    _, idx = lax.top_k(jnp.where(expert_mask, choice, -jnp.inf), TOP_K)
    w = jnp.take_along_axis(scores, idx, axis=-1)
    w = w / jnp.sum(w, axis=-1, keepdims=True) * ROUTED_SCALE
    gates = jnp.einsum('tk,tke->te', w, jax.nn.one_hot(idx, N_EXPERTS, dtype=jnp.float32))
    nb = ntok // MOE_TOKEN_BLOCK

    def block(args):
        tb, gb = args
        g = jnp.einsum('td,edf->tef', tb, w_eg)
        u = jnp.einsum('td,edf->tef', tb, w_eu)
        act = jax.nn.silu(g) * u * gb[:, :, None].astype(tb.dtype)
        return jnp.einsum('tef,efd->td', act, w_ed)

    routed = lax.map(block, (t.reshape(nb, MOE_TOKEN_BLOCK, d),
                             gates.reshape(nb, MOE_TOKEN_BLOCK, N_EXPERTS))).reshape(ntok, d)
    shared = (jax.nn.silu(t @ w_sg) * (t @ w_su)) @ w_sd
    return (routed + shared).reshape(b, s, d)

def setup_inputs(seed: int = 0) -> dict:
    key = jax.random.key(seed)
    ks = jax.random.split(key, 32)
    f32 = jnp.float32
    L, D = DEPTH, D_MODEL

    def nrm(k, shape, scale):
        return jax.random.normal(k, shape, f32) * scale

    x = jax.random.normal(ks[0], (BATCH, SEQ, D), f32)
    c = jax.random.normal(ks[1], (BATCH, D), f32)
    offs = jax.random.randint(ks[2], (BATCH, 1), 0, 1024, dtype=jnp.int32)
    positions = offs + jnp.arange(SEQ, dtype=jnp.int32)[None, :]
    dt0 = jnp.exp(jax.random.uniform(ks[12], (L, SSD_HEADS), f32, math.log(1e-3), math.log(1e-1)))
    return {
        "x": x,
        "c": c,
        "positions": positions,
        "w_ada": nrm(ks[3], (L, D, 6 * D), 0.5 * D ** -0.5),
        "b_ada": nrm(ks[4], (L, 6 * D), 0.02),
        "norm1_g": 1.0 + nrm(ks[5], (L, D), 0.1),
        "w_in": nrm(ks[6], (L, D, IN_WIDTH), D ** -0.5),
        "q_norm_g": 1.0 + nrm(ks[7], (L, ATTN_HEAD_DIM), 0.1),
        "k_norm_g": 1.0 + nrm(ks[8], (L, ATTN_HEAD_DIM), 0.1),
        "lambda_qk": nrm(ks[9], (L, 4, ATTN_HEAD_DIM), 0.1),
        "subln_g": 1.0 + nrm(ks[10], (L, ATTN_V_DIM), 0.1),
        "conv_w": nrm(ks[11], (L, SSD_CONV, SSD_CONV_DIM), 0.5),
        "conv_b": nrm(ks[13], (L, SSD_CONV_DIM), 0.02),
        "dt_bias": dt0 + jnp.log(-jnp.expm1(-dt0)),
        "a_log": jnp.log(jax.random.uniform(ks[14], (L, SSD_HEADS), f32, 1.0, 16.0)),
        "d_skip": 1.0 + nrm(ks[15], (L, SSD_HEADS), 0.1),
        "ssd_norm_g": 1.0 + nrm(ks[16], (L, SSD_D_INNER), 0.1),
        "w_branch_a": nrm(ks[17], (L, ATTN_V_WIDTH, D), ATTN_V_WIDTH ** -0.5),
        "w_branch_b": nrm(ks[18], (L, SSD_D_INNER, D), SSD_D_INNER ** -0.5),
        "w_out": nrm(ks[19], (L, D, D), D ** -0.5),
        "norm2_g": 1.0 + nrm(ks[20], (L, D), 0.1),
        "w_router": nrm(ks[21], (L, D, N_EXPERTS), D ** -0.5),
        "router_bias": nrm(ks[22], (L, N_EXPERTS), 0.01),
        "w_exp_gate": nrm(ks[23], (L, N_EXPERTS, D, EXPERT_DIM), D ** -0.5),
        "w_exp_up": nrm(ks[24], (L, N_EXPERTS, D, EXPERT_DIM), D ** -0.5),
        "w_exp_down": nrm(ks[25], (L, N_EXPERTS, EXPERT_DIM, D), EXPERT_DIM ** -0.5),
        "w_sh_gate": nrm(ks[26], (L, D, SHARED_DIM), D ** -0.5),
        "w_sh_up": nrm(ks[27], (L, D, SHARED_DIM), D ** -0.5),
        "w_sh_down": nrm(ks[28], (L, SHARED_DIM, D), SHARED_DIM ** -0.5),
    }

def reference(x, c, positions, w_ada, b_ada, norm1_g, w_in, q_norm_g, k_norm_g, lambda_qk, subln_g,
              conv_w, conv_b, dt_bias, a_log, d_skip, ssd_norm_g, w_branch_a, w_branch_b, w_out,
              norm2_g, w_router, router_bias, w_exp_gate, w_exp_up, w_exp_down,
              w_sh_gate, w_sh_up, w_sh_down):
    b, s, _ = x.shape
    offsets = [int(o) for o in np.cumsum(IN_SIZES)[:-1]]
    for layer in range(DEPTH):
        lambda_init = 0.8 - 0.6 * math.exp(-0.3 * layer)
        mod = jax.nn.silu(c) @ w_ada[layer] + b_ada[layer]
        sh1, sc1, g1, sh2, sc2, g2 = jnp.split(mod[:, None, :], 6, axis=-1)
        h = rmsnorm(x, norm1_g[layer]) * (1.0 + sc1) + sh1
        proj = h @ w_in[layer]
        q, k, v, ga, gb, z, xbc, dt = jnp.split(proj, offsets, axis=-1)
        q = q.reshape(b, s, ATTN_HEADS, 2, ATTN_HEAD_DIM)
        k = k.reshape(b, s, ATTN_HEADS, 2, ATTN_HEAD_DIM)
        v = v.reshape(b, s, ATTN_HEADS, ATTN_V_DIM)
        ya = diff_attention(q, k, v, positions, q_norm_g[layer], k_norm_g[layer],
                            lambda_qk[layer], subln_g[layer], lambda_init)
        yb = ssd_mixer(z, xbc, dt, conv_w[layer], conv_b[layer], dt_bias[layer],
                       a_log[layer], d_skip[layer], ssd_norm_g[layer])
        merged = (jax.nn.sigmoid(ga) * (ya @ w_branch_a[layer])
                  + jax.nn.sigmoid(gb) * (yb @ w_branch_b[layer]))
        x = x + g1 * (merged @ w_out[layer])
        h2 = rmsnorm(x, norm2_g[layer]) * (1.0 + sc2) + sh2
        x = x + g2 * moe_ffn(h2, w_router[layer], router_bias[layer], w_exp_gate[layer],
                             w_exp_up[layer], w_exp_down[layer], w_sh_gate[layer],
                             w_sh_up[layer], w_sh_down[layer])
    return x


_drawn_inputs = setup_inputs


def setup_inputs(seed=0):
    import zlib

    import numpy as np

    out = dict(_drawn_inputs(seed))
    spreads = {}
    factors = {'q_norm_g': 3.375, 'k_norm_g': 4.108, 'lambda_qk': 8.0, 'conv_b': 3.33, 'd_skip': 3.03}
    for name, (base, spread) in spreads.items():
        noise = np.random.default_rng([zlib.crc32(name.encode()), seed]).standard_normal(out[name].shape)
        drawn = base * np.exp(spread * noise) if base else spread * noise
        out[name] = __import__('jax').numpy.asarray(drawn.astype(out[name].dtype))
    for name, factor in factors.items():
        out[name] = (out[name] * factor).astype(out[name].dtype)
    return out
```

```python
from contextlib import ExitStack

import numpy as np

import concourse.bass as bass
from concourse import mybir

F32 = mybir.dt.float32
F32R = mybir.dt.float32r
I32 = mybir.dt.int32
ALU = mybir.AluOpType
ACT = mybir.ActivationFunctionType
AX = mybir.AxisListType.X

P = 128
T = 512
NT = T // P
D = 1024
KD = D // P
HEADS, HD, VD = 8, 64, 128
HALF = 4
G4, GH, HP, NS = 4, 8, 64, 128
DI = 2048
NE, FE = 64, 256
TOPK, NG, PG = 8, 8, 8
EPS = 1e-6
LAMBDA_INIT = 0.2
ROUTED_SCALE = 2.5
OQ, OK, OV, OGA, OGB, OZ, OX = 0, 1024, 2048, 3072, 4096, 5120, 7168
OB = OX + DI
OC = OB + G4 * NS
ODT = OC + G4 * NS
UNIT = 2048
RAW, HL = 3, 3
FAR = 1 << 20
NEG = -1.0e30
TWO_PI = 2.0 * np.pi


def wait(eng, sem, value):
    if isinstance(value, int) and value <= 0:
        return
    eng.wait_ge(sem, value)


def line(eng, sem):
    n = [0]

    def run(ins):
        n[0] += 1
        ins.then_inc(sem, 1)
        eng.wait_ge(sem, n[0])
    run.count = n
    return run


class Map:

    def __init__(self, nc):
        self.nc = nc
        self.at = (nc.sbuf_base + 63) // 64 * 64
        self.end = nc.sbuf_usable_end

    def __call__(self, name, shape, dt=F32):
        size = int(np.prod(shape[1:])) * 4
        t = self.nc.alloc_sbuf_tensor_at(name, shape, dt, offset=self.at)
        self.at += (size + 31) // 32 * 32
        assert self.at <= self.end, (name, self.at, self.end)
        return t


def plan_steps(w):
    steps = []

    def cols(src, r0, nk, c0, n=512):
        return src[r0:r0 + nk * P, c0:c0 + n].rearrange("(k p) n -> p k n", p=P)

    def halves(src, c0):
        return [[(0, 512, 0, 4, cols(src, h * 512, 4, c0))] for h in range(2)]

    def add(kind, tag, units=(), nout=0, ks=4):
        steps.append(dict(kind=kind, tag=tag, units=list(units), nout=nout, ks=ks))

    for j in range(4):
        add("mod", j, halves(w["w_ada"], j * 512))
    add("h", 0)
    for hf in range(2):
        add("row", ("q", hf), halves(w["w_in"], OQ + hf * 512), 4)
        add("row", ("k", hf), halves(w["w_in"], OK + hf * 512), 4)
        add("row", ("v", hf), halves(w["w_in"], OV + hf * 512), 4)
        add("attn", hf)
        for b in range(2):
            add("branch", ("a", hf, b), [[(0, 512, 0, 4, cols(w["w_a"], hf * 512, 4, b * 512))]], 4)
    for b in range(2):
        add("col", ("ga", b), halves(w["w_in"], OGA + b * 512), 4)
    for g in range(G4):
        add("col", ("xs", g), halves(w["w_in"], OX + g * 512), 4)
        add("mod", 4 + 2 * g, halves(w["w_ada"], (4 + 2 * g) * 512))
        add("col", ("bc", g), [[(0, 128, 0, 8, cols(w["w_in"], 0, 8, OB + g * NS, NS)),
                               (128, 256, 0, 8, cols(w["w_in"], 0, 8, OC + g * NS, NS))]], 2, 8)
        add("mod", 5 + 2 * g, halves(w["w_ada"], (5 + 2 * g) * 512))
        add("row", ("z", g), halves(w["w_in"], OZ + g * 512), 4)
        add("ssd", g)
        for b in range(2):
            add("branch", ("b", g, b), [[(0, 512, 0, 4, cols(w["w_b"], g * 512, 4, b * 512))]], 4)
    for b in range(2):
        add("col", ("gb", b), halves(w["w_in"], OGB + b * 512), 4)
    add("merge", 0)
    for b in range(2):
        add("row", ("out", b), halves(w["w_out"], b * 512), 4)
    add("h2", 0)
    add("row", ("sgu", 0), [[(0, 256, 0, 4, cols(w["w_sg"], h * 512, 4, 0, 256)),
                            (256, 512, 0, 4, cols(w["w_su"], h * 512, 4, 0, 256))] for h in range(2)], 4)
    add("sact", 0)
    add("row", ("sdn", 0), [[(0, 1024, 0, 2, cols(w["w_sd"], 0, 2, 0, 1024))]], 8, 2)

    n = m = mods = outs = mids = 0
    for s in steps:
        s["out0"] = outs
        s["u"] = []
        for i, dmas in enumerate(s["units"]):
            u = dict(n=n, dmas=dmas)
            n += 1
            if s["kind"] == "mod":
                mods += 1
                u.update(mod=mods)
            else:
                u.update(m=m)
                m += 1
                if i == len(s["units"]) - 1:
                    u["freed"] = ("proj_done", outs + s["nout"])
                else:
                    mids += 1
                    u["freed"] = ("half_done", mids)
            s["u"].append(u)
        outs += s["nout"]
    return steps


def build(nc, x, c, positions, w_ada, b_ada, norm1_g, w_in, q_norm_g, k_norm_g, lambda_qk, subln_g,
          conv_w, conv_b, dt_bias, a_log, d_skip, ssd_norm_g, w_branch_a, w_branch_b, w_out,
          norm2_g, w_router, router_bias, w_exp_gate, w_exp_up, w_exp_down,
          w_sh_gate, w_sh_up, w_sh_down, out, stop_after=None, dbg=None):
    w = dict(w_ada=w_ada[0], w_in=w_in[0], w_a=w_branch_a[0], w_b=w_branch_b[0], w_out=w_out[0],
             w_sg=w_sh_gate[0], w_su=w_sh_up[0], w_sd=w_sh_down[0])
    steps = plan_steps(w)
    if stop_after is not None:
        steps = steps[:stop_after]
    units = [u for s in steps for u in s["u"]]
    splits = [u for u in units if "m" in u]
    landed, per = {}, [0] * RAW
    for u in units:
        per[u["n"] % RAW] += 16 * len(u["dmas"])
        landed[u["n"]] = per[u["n"] % RAW]

    def unit_view(buf, dma):
        c0, c1, k0, ks, src = dma
        width = UNIT // ks
        return buf.rearrange("p (k n) -> p k n", n=width)[:, :, c0:c1]

    dram = lambda n, s, dt=F32: nc.dram_tensor(n, s, dt, kind="Internal").ap()
    gated_a = dram("gated_a", (P, KD * T))
    h2_rows = dram("h2_rows", (T, D))
    y_rows = dram("y_rows", (T * TOPK, D))
    x2_dram = dram("x2_dram", (P, NT * D))
    g2_dram = dram("g2_dram", (P, D))
    slot_table = dram("slot_table", (P * NE * NT, 1), I32)

    sb = Map(nc)
    ident = sb("ident", [P, P])
    upper = sb("upper", [P, P])
    later = sb("later", [P, P])
    before = sb("before", [P, P])
    ones = sb("ones", [P, P])
    causal = sb("causal", [P, P])
    colp = sb("colp", [P, 113])
    convw = sb("convw", [P, 96])
    shT = sb("shT", [P, 16])
    a1T = sb("a1T", [P, KD])
    silc = sb("silc", [P, KD])
    stat = sb("stat", [P, 5, 32])
    modacc_at = sb.at
    modacc = sb("modacc", [P, T])
    tok_of = nc.alloc_sbuf_tensor_at("tok_of", [P, NE * NT], I32, offset=modacc_at)
    row_of = nc.alloc_sbuf_tensor_at("row_of", [P, NE * NT], I32, offset=modacc_at + NE * NT * 4)
    stage_at = sb.at
    stage = sb("stage", [P, 2, T])
    dtp = sb("dtp", [P, NT, 32])
    aa = sb("aa", [P, NT, 32])
    expo = sb("expo", [P, 3, NT, 32])
    dtdec = sb("dtdec", [P, NT, 32])
    dskip = sb("dskip", [P, 32])
    w8 = sb("w8", [P, NT, TOPK])
    cnt = sb("cnt", [P, 2, NE], I32)
    hT_at = sb.at
    hT = sb("hT", [P, KD, 2, T], F32R)
    rings = sb.at
    raw = sb("raw", [P, RAW, UNIT])
    hl = sb("hl", [P, HL, 2, UNIT], F32R)
    late = sb.at
    g1b = sb("g1b", [P, D])
    g2b = sb("g2b", [P, D])
    sh2b = sb("sh2b", [P, D])
    a2b = sb("a2b", [P, D])
    after_late = sb.at
    sb.at = late
    tabs = sb("tabs", [P, 2, 2, NT, HD])
    wT = sb("wT", [P, NT, P])
    o_rows = sb("o_rows", [P, NT, VD])
    o_sq = sb("o_sq", [P, NT, VD])
    lamt = sb("lamt", [P, 4, HD])
    lam = sb("lam", [P, 8])
    sm = sb("sm", [P, 2, 8])
    gqk = sb("gqk", [P, 2, HD])
    assert sb.at <= after_late
    sb.at = after_late
    acc = sb("acc", [P, KD, T])
    work = sb.at
    x_rows = sb("x_rows", [P, NT, D])
    hsplit = sb("hsplit", [P, 2, T])
    pr1 = sb("pr1", [P, P])
    pr2 = sb("pr2", [P, P])
    wdt = sb("wdt", [P, KD, 32])
    wdt_hl = sb("wdt_hl", [P, KD, 2, 32], F32R)
    dtb = sb("dtb", [P, 2, 32])
    dwk = sb("dwk", [P, 6, NT * 32])
    trig = sb("trig", [P, 5, NT * 32])
    freq = sb("freq", [P, 32])
    posi = sb("posi", [P, NT], I32)
    posf = sb("posf", [P, NT])
    sb.at = work
    q_rows = sb("q_rows", [P, 2, NT, HALF * P])
    sb.at = work
    ya_hl = sb("ya_hl", [P, HALF, 2, T], F32R)
    v_rows = sb("v_rows", [P, NT, HALF * P])
    qkT = sb("qkT", [P, 2, HALF, T])
    probs = sb("probs", [P, 2, 2, T])
    wgt = sb("wgt", [P, 2, T])
    sb.at = work
    xbc = sb("xbc", [P, 6, T + 3])
    under = sb.at
    cv = sb("cv", [P, 6, T])
    b_rows = sb("b_rows", [P, NT, NS])
    cbm = sb("cbm", [P, NT, P])
    z_rows = sb("z_rows", [P, NT, 512])
    xs_rows = sb("xs_rows", [P, NT, 512])
    ua = sb("ua", [P, GH, P])
    lm = sb("lm", [P, GH, P])
    xdt, state, skip = cv[:, 0:2], cv[:, 2], cv[:, 3]
    ssd_end = sb.at
    sb.at = under
    yb_hl = sb("yb_hl", [P, 4, 2, T], F32R)
    sb.at = work
    ga_back = sb("ga_back", [P, KD, T])
    x2 = sb("x2", [P, NT, D])
    sb.at = work
    h2r = sb("h2r", [P, NT, D])
    sb.at = after_late
    wr = sb("wr", [P, KD, NE])
    wr_hl = sb("wr_hl", [P, KD, 2, NE], F32R)
    rt = sb("rt", [P, 6, NT, NE])
    assert sb.at <= work
    sb.at = work + 32768
    n2b = sb("n2b", [P, D])
    sb.at = work + 32768
    sgu = sb("sgu", [P, NT, T])
    sactT = sb("sactT", [P, 2, 2, T], F32R)
    rbias = sb("rbias", [P, NE])
    rk = sb("rk", [P, 3, 64])
    jlt = sb("jlt", [P, 8, 8])
    e4 = sb("e4", [P, NE])
    top = sb("top", [P, 16])
    grp = sb("grp", [P, NT, NG, 8])
    addr8 = sb("addr8", [P, NT, TOPK])
    addr8i = sb("addr8i", [P, NT, TOPK], I32)
    tokid = sb("tokid", [P, NT, TOPK], I32)
    eq8 = sb("eq8", [P, TOPK, NE])
    farow = sb("farow", [P, NE * NT], I32)
    sb.at = rings
    rawm = sb("rawm", [P, 6, UNIT])
    hlm = sb("hlm", [P, 6, 2, UNIT], F32R)
    yb = sb("yb", [P, 2, D])
    aT = sb("aT", [P, 2, 2, 2, P], F32R)
    sb.at = hT_at
    xT = sb("xT", [P, 2, KD, 2, P], F32R)
    xg = sb("xg", [P, 2, D])
    xo = sb("xo", [P, D])
    yo = sb("yo", [P, D])
    assert sb.at <= rings
    act = nc.alloc_sbuf_tensor_at("act", [P, 2, FE], F32, offset=stage_at)
    gix = nc.alloc_sbuf_tensor_at("gix", [P, 4], I32, offset=stage_at + 2048)
    oix = nc.alloc_sbuf_tensor_at("oix", [P, 2], I32, offset=stage_at + 2112)
    sb.at = rings
    ysum = sb("ysum", [P, 2, 4, D])
    xfin = sb("xfin", [P, NT, D])
    g2f = sb("g2f", [P, D])
    ofin = sb("ofin", [P, 2, D])

    with ExitStack() as ctx:
        psum = ctx.enter_context(nc.psum_tensor("psum", [P, 8, 512], F32))
        S = {}

        def sem(*names):
            for n in names:
                S[n] = ctx.enter_context(nc.semaphore(n))
        sem("vec_line", "act_line", "pool_line", "consts", "params", "x_in", "half_done", "proj_done",
            "proj_free", "hi_done", "lo_done", "mod_used", "mod_ps", "mod_ev", "par_T", "par_ev",
            "silu_c", "rs_in", "rs_out", "xr_ready", "xT_ps", "h_tmp", "h_hi", "h_lo", "wdt_hi", "wdt_lo", "dt_ps",
            "dt_exp", "dt_dve", "dt_a", "cum_ps", "cum_exp", "trig_in", "trig_out", "sq_done")
        sem(*[f"raw_in{i}" for i in range(RAW)])
        sem("qk_ready", "qkT_ps", "qkT_ev", "sc_ps", "nmax", "p_exp", "w_ready", "wT_ps", "wT_ev", "o_ps", "o_ev",
            "o_ready", "yT_ps", "yT_hi", "yT_lo", "stage_used")
        sem("conv_done", "conv_silu", "tr_ps", "tr_ev", "b_ev", "cb_ps", "ua_ready", "seg_ps",
            "seg_exp", "m_ready", "xd_ready", "ys_ps", "st_ready", "y_ready", "yn_ready", "skipped",
            "g_in", "spilled", "ga_in", "x2_in", "merged", "m_hi", "m_lo")
        sem("x2_ready", "h2_row", "h2T_ps", "h2T_hi", "h2T_lo", "h2_out", "wr_in", "wr_hi", "wr_lo", "lg_ps", "lg_ev",
            "sel_ready", "pos_ps", "addr_ready", "table_far", "table_set", "table_in", "tok_ready",
            "sa_ready", "sT_ps", "sT_hi", "sT_lo", "x2_out", "cnt_ready", "rp_in", "jlt_ready")
        sem(*[f"m_raw{i}" for i in range(6)])
        sem("m_hi2", "m_lo2", "m_x0", "m_x1", "m_y0", "m_y1", "xt_ps", "xt_hi", "xt_lo", "gu_ps", "gu_silu", "act_ready",
            "at_ps", "at_hi", "at_lo", "dn_ps", "y_ev", "m_idx", "held")
        sem(*[f"more_{n}" for n in ("x", "t", "xh", "xl", "g", "sg", "act", "t2", "t2h", "t2l", "d", "y", "s", "idx")])
        sem("fin_x", "fin_y0", "fin_y1", "fin_used", "fin_out", "fin_line", "out_done0", "out_done1")
        blk = ctx.enter_context(nc.Block())
        bank = lambda b: psum[:, b]
        ring_rule = {}

        def free_split(eng, m):
            if m >= HL:
                name, value = splits[m - HL]["freed"]
                eng.wait_ge(S[name], value)

        def raw_wait(eng, u):
            eng.wait_ge(S[f"raw_in{u['n'] % RAW}"], landed[u["n"]])

        def ahead(i):
            if i not in ring_rule:
                done = 0
                for j in range(-1, len(steps)):
                    k = j + 1
                    while k < len(steps) and not (steps[k]["u"] and steps[k]["kind"] != "mod"):
                        k += 1
                    stop = steps[k]["u"][-1]["n"] + 1 if k < len(steps) else len(units)
                    ring_rule[j] = units[done:max(stop, done)]
                    done = max(stop, done)
            return ring_rule[i]

        out_index = {s["tag"]: s["out0"] for s in steps if s["nout"]}

        flat = lambda ap: ap.rearrange("p a b -> p (a b)")
        USED = sum(s["nout"] for s in steps if s["tag"] and isinstance(s["tag"], tuple) and (
            s["tag"][0] in ("out", "sdn", "ga", "gb") or (s["kind"] == "branch" and s["tag"][1] > 0)))
        OUTS = sum(s["nout"] for s in steps)

        def route(v, L):
            V = nc.vector
            TS, TT, STT = V.tensor_scalar, V.tensor_tensor, V.scalar_tensor_tensor
            v.wait_ge(S["lg_ev"], 1)
            v.wait_ge(S["rp_in"], 16)
            over_t = lambda ap: ap.unsqueeze(1).to_broadcast([P, NT, NE])
            L(TT(rt[:, 1], rt[:, 0], over_t(rbias[:]), ALU.add))
            for t in range(NT):
                for g in range(NG):
                    ins = V.max(grp[:, t, g, :], rt[:, 1, t, g * PG:(g + 1) * PG])
            L(ins)
            gs = addr8
            L(TT(gs[:], grp[:, :, :, 0], grp[:, :, :, 1], ALU.add))
            v.wait_ge(S["jlt_ready"], 1)
            sq = lambda n: rk[:, n].rearrange("p (g j) -> p g j", j=8)
            for t in range(NT):
                as_j = gs[:, t, :].unsqueeze(1).to_broadcast([P, 8, 8])
                as_g = gs[:, t, :].unsqueeze(2).to_broadcast([P, 8, 8])
                L(TT(sq(0), as_j, as_g, ALU.is_gt))
                L(TT(sq(1), as_j, as_g, ALU.is_equal))
                L(TT(sq(1), sq(1), jlt[:], ALU.mult))
                L(TT(sq(0), sq(0), sq(1), ALU.add))
                L(V.tensor_reduce(top[:, 0:8], sq(0), AX, ALU.add))
                L(TS(top[:, 0:8], top[:, 0:8], 4.0, None, ALU.is_lt))
                L(TS(top[:, 8:16], top[:, 0:8], -NEG, NEG, ALU.mult, ALU.add))
                m = rt[:, 1, t, :]
                by_g = lambda ap: ap.rearrange("p (g e) -> p g e", e=PG)
                L(TT(by_g(m), by_g(m), top[:, 0:8].unsqueeze(2).to_broadcast([P, 8, 8]), ALU.mult))
                L(TT(by_g(m), by_g(m), top[:, 8:16].unsqueeze(2).to_broadcast([P, 8, 8]), ALU.add))
                L(V.max(top[:, 0:8], m))
                L(V.match_replace(rt[:, 2, t, :], top[:, 0:8], m, -3.0e38))
                TS(rt[:, 3, t, :], rt[:, 2, t, :], -2.0e30, None, ALU.is_lt).then_inc(S["sel_ready"], 1)
            v.wait_ge(S["sel_ready"], NT)
            L(TT(rt[:, 5], rt[:, 0], rt[:, 3], ALU.mult))
            L(V.tensor_reduce(top[:, 0:NT], rt[:, 5], AX, ALU.add))
            L(V.reciprocal(top[:, 0:NT], top[:, 0:NT]))
            L(TS(top[:, 0:NT], top[:, 0:NT], ROUTED_SCALE, None, ALU.mult))
            L(TT(rt[:, 5], rt[:, 5], top[:, 0:NT].unsqueeze(2).to_broadcast([P, NT, NE]), ALU.mult))

        def slots(v, L):
            V = nc.vector
            TS, TT, STT = V.tensor_scalar, V.tensor_tensor, V.scalar_tensor_tensor
            v.wait_ge(S["pos_ps"], 1)
            pos, j_ = flat(rt[:, 4]), flat(rt[:, 1])
            L(V.tensor_copy(pos, psum[:, 7, 0:NT * NE]))
            L(V.tensor_copy(rk[:, 2], psum[:, 7, NT * NE:(NT + 1) * NE]))
            L(TS(j_, pos, 128.0, None, ALU.is_ge))
            L(STT(out=j_, in0=pos, scalar=256.0, in1=j_, op0=ALU.is_ge, op1=ALU.add))
            L(STT(out=j_, in0=pos, scalar=384.0, in1=j_, op0=ALU.is_ge, op1=ALU.add))
            L(TS(pos, pos, 256.0, 1.0, ALU.mult, ALU.add))
            L(TT(rt[:, 4], rt[:, 4], e4[:].unsqueeze(1).to_broadcast([P, NT, NE]), ALU.add))
            L(STT(out=pos, in0=j_, scalar=-32767.0, in1=pos, op0=ALU.mult, op1=ALU.add))
            L(TT(pos, pos, flat(rt[:, 3]), ALU.mult))
            L(TS(pos, pos, 1.0, None, ALU.subtract))
            for t in range(NT):
                L(V.max(addr8[:, t, :], rt[:, 4, t, :]))
            V.tensor_copy(addr8i[:], addr8[:]).then_inc(S["addr_ready"], 1)
            for t in range(NT):
                over_k = lambda ap: ap.unsqueeze(1).to_broadcast([P, TOPK, NE])
                L(TT(eq8[:], over_k(rt[:, 4, t, :]), addr8[:, t, :].unsqueeze(2).to_broadcast([P, TOPK, NE]),
                     ALU.is_equal))
                L(TT(eq8[:], eq8[:], over_k(rt[:, 5, t, :]), ALU.mult))
                L(V.tensor_reduce(w8[:, t, :], eq8[:], AX, ALU.add))
            L(V.tensor_copy(cnt[:, 0, :], rk[:, 2]))
            own = eq8[:, 0]
            L(TS(own, rk[:, 2], P + 0.5, None, ALU.is_gt))
            L(TS(eq8[:, 1], rk[:, 2], 2 * P + 0.5, 2.0, ALU.is_gt, ALU.mult))
            L(TT(own, own, eq8[:, 1], ALU.add))
            L(V.tensor_copy(eq8[:, 1], own))
            at = 1
            for step in (1, 2, 4, 8, 16, 32):
                nxt = 3 - at
                V.tensor_copy(eq8[:, nxt, 0:step], eq8[:, at, 0:step])
                L(TT(eq8[:, nxt, step:], eq8[:, at, step:], eq8[:, at, 0:NE - step], ALU.add))
                at = nxt
            L(TT(eq8[:, at], eq8[:, at], own, ALU.subtract))
            V.tensor_copy(cnt[:, 1, :], eq8[:, at]).then_inc(S["cnt_ready"], 1)

        def pool_route(pool, L):
            pool.wait_ge(S["h2_row"], 1)
            for t in range(NT):
                pool.dma_start(h2_rows[t * P:(t + 1) * P, :], h2r[:, t, :]).then_inc(S["h2_out"], 16)
            pool.wait_ge(S["table_far"], 16)
            pool.wait_ge(S["addr_ready"], 1)
            for t in range(NT):
                for k in range(TOPK):
                    pool.indirect_dma_start(slot_table, bass.IndirectOffsetOnAxis(ap=addr8i[:, t, k:k + 1], axis=0),
                                            tokid[:, t, k:k + 1], None).then_inc(S["table_set"], 16)
            pool.wait_ge(S["table_set"], 16 * NT * TOPK)
            pool.dma_start(row_of[:], slot_table.rearrange("(p n) o -> p (n o)", p=P)).then_inc(S["table_in"], 16)

        PAIRS = NE // 2

        def hold(eng, sem, value):
            eng.wait_ge(sem, value).then_inc(S["held"], 1)

        def read_counts(eng, e):
            return [eng.value_load(cnt[0:1, q, bass.ds(e, 1)], min_val=0, max_val=T) for q in range(2)]

        def extra(eng, e, body):
            count, n = read_counts(eng, e)
            with eng.If(count > P):
                body(1, n)
            with eng.If(count > 2 * P):
                for j in (2, 3):
                    body(j, n + (j - 1))

        def iterations(eng, it, last):
            for e in range(3):
                it(e, e % 2)
            with eng.Fori(0, PAIRS - 2) as i:
                it(i * 2 + 3, 1)
                it(i * 2 + 4, 0)
            for e in range(NE - 1, last):
                it(e, e % 2)

        def sp_moe(sp):
            gate = w_exp_gate[0].rearrange("e (k p) n -> e p k n", p=P)
            up = w_exp_up[0].rearrange("e (k p) n -> e p k n", p=P)
            down = w_exp_down[0].rearrange("e (k p) n -> e p k n", p=P)
            sp.wait_ge(S["proj_done"], OUTS)

            def load(e, par, first=False):
                at = bass.ds(e, 1)
                for u in range(3):
                    slot = 3 * par + u
                    if not first:
                        sp.wait_ge(S["m_lo2"], e * 3 + (u - 5))
                    buf = rawm[:, slot]
                    if u < 2:
                        b_ = buf.rearrange("p (k n) -> p k n", n=512)
                        for half, src in enumerate((gate, up)):
                            sp.dma_start(b_[:, :, half * FE:(half + 1) * FE],
                                         src[at, :, u * 4:u * 4 + 4, :].rearrange("o p k n -> (o p) k n")).then_inc(
                                S[f"m_raw{slot}"], 16)
                    else:
                        sp.dma_start(buf.rearrange("p (k n) -> p k n", n=D),
                                     down[at].rearrange("o p k n -> (o p) k n")).then_inc(S[f"m_raw{slot}"], 16)
            load(0, 0, True)
            load(1, 1, True)
            with sp.Fori(1, PAIRS) as i:
                load(i * 2, 0)
                load(i * 2 + 1, 1)
            for t in range(NT):
                sp.wait_ge(S["fin_out"], t + 1)
                sp.dma_start(out[0, t * P:(t + 1) * P, :], ofin[:, t % 2, :]).then_inc(S[f"out_done{t % 2}"], 16)
            sp.wait_ge(S["out_done0"], 16 * NT // 2)
            sp.wait_ge(S["out_done1"], 16 * NT // 2)

        def pool_moe(pool, L):
            if OUTS == 0:
                return
            pool.wait_ge(S["stage_used"], USED)
            pool.dma_start(x2_dram, flat(x2[:])).then_inc(S["x2_out"], 16)
            pool.dma_start(g2_dram, g2b[:]).then_inc(S["x2_out"], 16)
            pool.wait_ge(S["tok_ready"], 1)
            pool.wait_ge(S["x2_out"], 32)
            pool.wait_ge(S["h2_out"], 16 * NT)
            pool.wait_ge(S["cnt_ready"], 1)
            L(nc.gpsimd.memset(xg[:], 0.0))
            L(nc.gpsimd.memset(xo[:], 0.0))

            def gather(e, par, copies):
                nc.gpsimd.tensor_copy(gix[:, par:par + 1], tok_of[:, bass.ds(e * NT, 1)]).then_inc(S["m_idx"], 1)
                hold(pool, S["m_idx"], copies)
                pool.indirect_dma_start(xg[:, par, :], None, h2_rows,
                                        bass.IndirectOffsetOnAxis(ap=gix[:, par:par + 1], axis=0),
                                        bounds_check=T - 1, oob_is_err=False).then_inc(S[f"m_x{par}"], 16)

            def scatter(e, par, copies):
                nc.gpsimd.tensor_copy(gix[:, 2 + par:3 + par], row_of[:, bass.ds(e * NT, 1)]).then_inc(S["m_idx"], 1)
                hold(pool, S["m_idx"], copies)
                pool.indirect_dma_start(y_rows, bass.IndirectOffsetOnAxis(ap=gix[:, 2 + par:3 + par], axis=0),
                                        yb[:, par, :], None, bounds_check=T * TOPK - 1,
                                        oob_is_err=False).then_inc(S[f"m_y{par}"], 16)

            def more(e):
                def body(j, x_):
                    o = lambda n: S[f"more_{n}"]
                    nc.gpsimd.tensor_copy(oix[:, 0:1], tok_of[:, bass.ds(e * NT + j, 1)]).then_inc(o("idx"), 1)
                    hold(pool, o("idx"), x_ * 2 + 1)
                    pool.indirect_dma_start(xo[:], None, h2_rows, bass.IndirectOffsetOnAxis(ap=oix[:, 0:1], axis=0),
                                            bounds_check=T - 1, oob_is_err=False).then_inc(o("x"), 16)
                    nc.gpsimd.tensor_copy(oix[:, 1:2], row_of[:, bass.ds(e * NT + j, 1)]).then_inc(o("idx"), 1)
                    hold(pool, o("idx"), x_ * 2 + 2)
                    hold(pool, o("y"), x_ + 1)
                    pool.indirect_dma_start(y_rows, bass.IndirectOffsetOnAxis(ap=oix[:, 1:2], axis=0), yo[:], None,
                                            bounds_check=T * TOPK - 1, oob_is_err=False).then_inc(o("s"), 16)
                    hold(pool, o("s"), x_ * 16 + 16)
                extra(pool, e, body)

            def step(e, par, copies, last=False):
                if not isinstance(e, int) or e > 0:
                    hold(pool, S["y_ev"], e)
                    scatter(e - 1, 1 - par, copies + 1)
                    copies = copies + 1
                if not last:
                    hold(pool, S["xt_ps"], e + 1)
                    gather(e + 2, par, copies + 1)
                if not isinstance(e, int) or e < NE:
                    more(e)
            gather(0, 0, 1)
            gather(1, 1, 2)
            step(0, 0, 2)
            with pool.Fori(0, (NE - 4) // 2) as i:
                step(i * 2 + 1, 1, i * 4 + 3)
                step(i * 2 + 2, 0, i * 4 + 5)
            step(NE - 3, 1, 2 * NE - 5)
            step(NE - 2, 0, 2 * NE - 3, last=True)
            step(NE - 1, 1, 2 * NE - 2, last=True)
            step(NE, 0, 2 * NE - 1, last=True)
            fin_pool(pool)

        def pe_moe(pe, M, tr, three):
            if OUTS == 0:
                return
            xt_dst = lambda k: psum[:, k // 4, (k % 4) * P:(k % 4 + 1) * P]

            def to_T(src):
                for k in range(KD):
                    ins = tr(xt_dst(k), src[:, k * P:(k + 1) * P], ident[:])
                return ins

            def gate_up(par):
                for k in range(KD):
                    wv = lambda q: hlm[:, 3 * par + k // 4, q, :].rearrange("p (k n) -> p k n", n=512)[:, k % 4, :]
                    ins = three(bank(2 + par), lambda q: xT[:, par, k, q, :], wv, k == 0, k == KD - 1)
                return ins

            def act_to_T(src):
                for k in range(2):
                    ins = tr(psum[:, 4, k * P:(k + 1) * P], src[:, k * P:(k + 1) * P], ident[:])
                return ins

            def down_(par):
                wv = lambda q: hlm[:, 3 * par + 2, q, :].rearrange("p (k n) -> p k n", n=D)
                for half in range(2):
                    for k in range(2):
                        ins = three(bank(5 + half), lambda q: aT[:, par, k, q, :],
                                    lambda q: wv(q)[:, k, half * 512:(half + 1) * 512], k == 0, k == 1)
                return ins

            pe.wait_ge(S["cnt_ready"], 1)
            pe.wait_ge(S["stage_used"], USED)
            pe.wait_ge(S["m_x0"], 16)
            to_T(xg[:, 0, :]).then_inc(S["xt_ps"], 1)

            def it(e, par):
                whole = not isinstance(e, int) or e < NE
                if not isinstance(e, int) or e > 0:
                    pe.wait_ge(S["act_ready"], e)
                    wait(pe, S["at_lo"], e - 1)
                    act_to_T(act[:, 1 - par, :]).then_inc(S["at_ps"], 1)
                if whole:
                    pe.wait_ge(S["m_lo2"], e * 3 + 2)
                    pe.wait_ge(S["xt_lo"], e + 1)
                    wait(pe, S["act_ready"], e - 1)
                    gate_up(par).then_inc(S["gu_ps"], 1)
                if not isinstance(e, int) or e + 1 < NE:
                    pe.wait_ge(S[f"m_x{1 - par}"], (e + 1 - (1 - par)) * 8 + 16)
                    pe.wait_ge(S["xt_lo"], e + 1)
                    to_T(xg[:, 1 - par, :]).then_inc(S["xt_ps"], 1)
                if not isinstance(e, int) or e > 0:
                    pe.wait_ge(S["at_lo"], e)
                    pe.wait_ge(S["m_lo2"], e * 3)
                    wait(pe, S["y_ev"], e - 1)
                    down_(1 - par).then_inc(S["dn_ps"], 1)
                if whole:
                    def body(j, x_):
                        o = lambda n: S[f"more_{n}"]
                        pe.wait_ge(S["act_ready"], e + 1)
                        pe.wait_ge(S["m_lo2"], e * 3 + 3)
                        if not isinstance(e, int) or e > 0:
                            pe.wait_ge(S["y_ev"], e)
                        if not isinstance(e, int) or e + 1 < NE:
                            pe.wait_ge(S["xt_lo"], e + 2)
                        pe.wait_ge(o("x"), x_ * 16 + 16)
                        to_T(xo[:]).then_inc(o("t"), 1)
                        pe.wait_ge(o("xl"), x_ + 1)
                        gate_up(par).then_inc(o("g"), 1)
                        pe.wait_ge(o("act"), x_ + 1)
                        act_to_T(xo[:, 0:FE]).then_inc(o("t2"), 1)
                        pe.wait_ge(o("t2l"), x_ + 1)
                        down_(par).then_inc(o("d"), 1)
                        pe.wait_ge(o("y"), x_ + 1)
                    extra(pe, e, body)
            iterations(pe, it, NE + 1)

        def act_moe(a, A, L):
            if OUTS == 0:
                return
            a.wait_ge(S["x2_out"], 32)
            a.wait_ge(S["h2_out"], 16 * NT)
            a.wait_ge(S["cnt_ready"], 1)
            a.wait_ge(S["tok_ready"], 1)

            def split(e, par, us):
                for u in us:
                    slot = 3 * par + u
                    a.wait_ge(S[f"m_raw{slot}"], (e - par) * (16 if u < 2 else 8) + (32 if u < 2 else 16))
                    A(hlm[:, slot, 0, :], rawm[:, slot], ACT.Copy).then_inc(S["m_hi2"], 1)

            def x_hi(par):
                return A(xT[:, par, :, 0, :], psum[:, 0:2].rearrange("p b (k t) -> p (b k) t", t=P), ACT.Copy)

            def a_hi(par):
                return A(aT[:, par, :, 0, :], psum[:, 4, 0:2 * P].rearrange("p (k t) -> p k t", t=P), ACT.Copy)

            split(0, 0, range(3))
            a.wait_ge(S["xt_ps"], 1)
            x_hi(0).then_inc(S["xt_hi"], 1)

            def it(e, par):
                whole = not isinstance(e, int) or e < NE
                more_ = not isinstance(e, int) or e + 1 < NE
                prev = not isinstance(e, int) or e > 0
                if prev:
                    a.wait_ge(S["at_ps"], e)
                    wait(a, S["dn_ps"], e - 2)
                    a_hi(1 - par).then_inc(S["at_hi"], 1)
                    a.wait_ge(S["gu_ps"], e)
                if more_:
                    split(e + 1, 1 - par, range(2))
                if whole:
                    a.wait_ge(S["gu_ps"], e + 1)
                    wait(a, S["at_ps"], e - 1)
                    A(act[:, par, :], psum[:, 2 + par, 0:FE], ACT.Silu).then_inc(S["gu_silu"], 1)
                if more_:
                    a.wait_ge(S["xt_ps"], e + 2)
                    x_hi(1 - par).then_inc(S["xt_hi"], 1)
                if prev:
                    a.wait_ge(S["dn_ps"], e)
                    if not isinstance(e, int) or e > 2:
                        a.wait_ge(S[f"m_y{1 - par}"], (e - 1 - (1 - par)) * 8)
                    A(yb[:, 1 - par, :], psum[:, 5:7].rearrange("p b n -> p (b n)"), ACT.Copy).then_inc(S["y_ev"], 1)
                if more_:
                    split(e + 1, 1 - par, [2])
                if whole:
                    def body(j, x_):
                        o = lambda n: S[f"more_{n}"]
                        a.wait_ge(o("t"), x_ + 1)
                        x_hi(par).then_inc(o("xh"), 1)
                        a.wait_ge(o("g"), x_ + 1)
                        A(xo[:, 0:FE], psum[:, 2 + par, 0:FE], ACT.Silu).then_inc(o("sg"), 1)
                        a.wait_ge(o("t2"), x_ + 1)
                        a_hi(par).then_inc(o("t2h"), 1)
                        a.wait_ge(o("d"), x_ + 1)
                        A(yo[:], psum[:, 5:7].rearrange("p b n -> p (b n)"), ACT.Copy).then_inc(o("y"), 1)
                        hold(a, o("s"), x_ * 16 + 16)
                    extra(a, e, body)
            iterations(a, it, NE + 1)
            fin_act(a)

        def vec_moe(v, L):
            if OUTS == 0:
                return
            V = nc.vector
            TT = V.tensor_tensor
            v.wait_ge(S["table_in"], 16)
            V.tensor_single_scalar(tok_of[:], row_of[:], 3, ALU.arith_shift_right).then_inc(S["tok_ready"], 1)
            v.wait_ge(S["cnt_ready"], 1)

            def split(par, e, us):
                for u in us:
                    slot = 3 * par + u
                    v.wait_ge(S["m_hi2"], e * 3 + (u + 1))
                    TT(hlm[:, slot, 1, :], rawm[:, slot], hlm[:, slot, 0, :].bitcast(F32), ALU.subtract).then_inc(
                        S["m_lo2"], 1)

            def x_lo(par):
                return TT(xT[:, par, :, 1, :], psum[:, 0:2].rearrange("p b (k t) -> p (b k) t", t=P),
                          xT[:, par, :, 0, :].bitcast(F32), ALU.subtract)

            def a_lo(par):
                return TT(aT[:, par, :, 1, :], psum[:, 4, 0:2 * P].rearrange("p (k t) -> p k t", t=P),
                          aT[:, par, :, 0, :].bitcast(F32), ALU.subtract)

            split(0, 0, range(3))
            v.wait_ge(S["xt_hi"], 1)
            x_lo(0).then_inc(S["xt_lo"], 1)

            def it(e, par):
                whole = not isinstance(e, int) or e < NE
                more_ = not isinstance(e, int) or e + 1 < NE
                prev = not isinstance(e, int) or e > 0
                if prev:
                    v.wait_ge(S["at_hi"], e)
                    a_lo(1 - par).then_inc(S["at_lo"], 1)
                if more_:
                    split(1 - par, e + 1, range(2))
                if whole:
                    v.wait_ge(S["gu_silu"], e + 1)
                    TT(act[:, par, :], act[:, par, :], psum[:, 2 + par, FE:], ALU.mult).then_inc(S["act_ready"], 1)
                if more_:
                    v.wait_ge(S["xt_hi"], e + 2)
                    x_lo(1 - par).then_inc(S["xt_lo"], 1)
                    split(1 - par, e + 1, [2])
                if whole:
                    def body(j, x_):
                        o = lambda n: S[f"more_{n}"]
                        v.wait_ge(o("xh"), x_ + 1)
                        x_lo(par).then_inc(o("xl"), 1)
                        v.wait_ge(o("sg"), x_ + 1)
                        TT(xo[:, 0:FE], xo[:, 0:FE], psum[:, 2 + par, FE:], ALU.mult).then_inc(o("act"), 1)
                        v.wait_ge(o("t2h"), x_ + 1)
                        a_lo(par).then_inc(o("t2l"), 1)
                        hold(v, o("s"), x_ * 16 + 16)
                    extra(v, e, body)
            iterations(v, it, NE + 1)
            fin_vec(v)

        def fin_pool(pool):
            pool.wait_ge(S["m_y0"], 16 * NE // 2)
            pool.wait_ge(S["m_y1"], 16 * NE // 2)
            pool.wait_ge(S["dn_ps"], NE)
            pool.dma_start(flat(xfin[:]), x2_dram).then_inc(S["fin_x"], 16)
            pool.dma_start(g2f[:], g2_dram).then_inc(S["fin_x"], 16)

        def fin_act(a):
            a.wait_ge(S["m_y0"], 16 * NE // 2)
            a.wait_ge(S["m_y1"], 16 * NE // 2)
            a.wait_ge(S["dn_ps"], NE)
            ys = y_rows.rearrange("(t p k) d -> t p k d", p=P, k=TOPK)
            for t in range(NT):
                for half in range(2):
                    n = 2 * t + half
                    wait(a, S["fin_used"], n - 1)
                    a.dma_start(ysum[:, half], ys[t, :, half * 4:half * 4 + 4, :]).then_inc(S[f"fin_y{half}"], 16)

        def fin_vec(v):
            V = nc.vector
            L = line(v, S["fin_line"])
            v.wait_ge(S["fin_x"], 32)
            for t in range(NT):
                o_ = ofin[:, t % 2, :]
                if t >= 2:
                    v.wait_ge(S[f"out_done{t % 2}"], 16 * (t // 2))
                for k in range(TOPK):
                    half = k // 4
                    if k % 4 == 0:
                        v.wait_ge(S[f"fin_y{half}"], 16 * (t + 1))
                    gate_ = w8[:, t, k:k + 1]
                    row = ysum[:, half, k % 4, :]
                    if k == 0:
                        ins = V.tensor_scalar(o_, row, gate_, None, ALU.mult)
                    else:
                        ins = V.scalar_tensor_tensor(out=o_, in0=row, scalar=gate_, in1=o_, op0=ALU.mult, op1=ALU.add)
                    if k % 4 == 3:
                        ins.then_inc(S["fin_used"], 1)
                        v.wait_ge(S["fin_used"], 2 * t + half + 1)
                    else:
                        L(ins)
                L(V.tensor_tensor(o_, o_, g2f[:], ALU.mult))
                V.tensor_tensor(o_, o_, xfin[:, t, :], ALU.add).then_inc(S["fin_out"], 1)

        @blk.sync
        def _(sp):
            for t in range(NT):
                sp.dma_start(x_rows[:, t, :], x[0, t * P:(t + 1) * P, :]).then_inc(S["x_in"], 16)
            for u in units:
                if u["n"] >= RAW:
                    old = units[u["n"] - RAW]
                    if "m" in old:
                        sp.wait_ge(S["lo_done"], old["m"] + 1)
                    else:
                        sp.wait_ge(S["mod_used"], old["mod"])
                for dma in u["dmas"]:
                    sp.dma_start(unit_view(raw[:, u["n"] % RAW], dma), dma[4]).then_inc(
                        S[f"raw_in{u['n'] % RAW}"], 16)
            sp_moe(sp)

        @blk.gpsimd
        def _(pool):
            L = line(pool, S["pool_line"])
            for dst, rows, src in (
                    (pr1, 0, b_ada[0].rearrange("(r p) -> r p", p=P)),
                    (pr1, 48, norm1_g[0].rearrange("(r p) -> r p", p=P)),
                    (pr1, 56, norm2_g[0].rearrange("(r p) -> r p", p=P)),
                    (pr1, 64, c[0].rearrange("(r p) -> r p", p=P)),
                    (pr1, 72, conv_b[0].rearrange("(r p) -> r p", p=P)),
                    (pr1, 96, subln_g[0].rearrange("(r p) -> r p", p=P)),
                    (pr1, 97, ssd_norm_g[0].rearrange("(r p) -> r p", p=P)),
                    (pr2, 0, conv_w[0].rearrange("k (r p) -> (k r) p", p=P))):
                pool.dma_start(dst[rows:rows + src.shape[0], :], src).then_inc(S["params"], 16)
            for dst, src, n in ((gqk[:, 0], q_norm_g, HD), (gqk[:, 1], k_norm_g, HD), (dtb[:, 0], dt_bias, 32),
                                (dtb[:, 1], a_log, 32), (dskip[:], d_skip, 32),
                                (lamt.rearrange("p a d -> p (a d)"), lambda_qk.rearrange("o a d -> o (a d)"), 4 * HD)):
                pool.dma_start(dst, src.to_broadcast([P, n])).then_inc(S["params"], 16)
            pool.dma_start(posi[:], positions.rearrange("o (t p) -> p (o t)", p=P),
                           allow_slow_non_contiguous=True).then_inc(S["params"], 16)
            pool.dma_start(wdt[:], w["w_in"][:, ODT:ODT + 32].rearrange("(k p) n -> p k n", p=P)).then_inc(S["params"], 16)
            L(nc.gpsimd.memset(ones[:], 1.0))
            L(nc.gpsimd.memset(ident[:], 0.0))
            L(nc.gpsimd.memset(causal[:], 0.0))
            sel = nc.gpsimd.affine_select
            L(sel(out=ident[:], in_=ident[:], compare_op=ALU.not_equal, fill=1.0, base=0, pattern=[[-1, P]],
                  channel_multiplier=1))
            L(sel(out=upper[:], in_=ones[:], compare_op=ALU.is_ge, fill=0.0, base=0, pattern=[[1, P]],
                  channel_multiplier=-1))
            L(sel(out=before[:], in_=ones[:], compare_op=ALU.is_gt, fill=0.0, base=0, pattern=[[1, P]],
                  channel_multiplier=-1))
            L(sel(out=later[:], in_=ones[:], compare_op=ALU.is_gt, fill=0.0, base=0, pattern=[[-1, P]],
                  channel_multiplier=1))
            L(sel(out=causal[:], in_=causal[:], compare_op=ALU.is_ge, fill=NEG, base=0, pattern=[[-1, P]],
                  channel_multiplier=1))
            for i in range(32):
                ins = nc.gpsimd.memset(freq[:, i:i + 1], float(np.float32(10000.0) ** np.float32(-2.0 * i / HD)))
            ins.then_inc(S["consts"], 1)
            for s in steps:
                kind_ = s["kind"]
                if kind_ == "ssd":
                    g = s["tag"]
                    for ch in range(NT):
                        wait(pool, S["seg_ps"], 4 * g + ch)
                        if g == 0 and ch == 0:
                            pool.wait_ge(S["dt_a"], 1)
                        nc.gpsimd.tensor_tensor(
                            ua[:], upper[:].unsqueeze(1).to_broadcast([P, GH, P]),
                            aa[:, ch, g * GH:(g + 1) * GH].unsqueeze(2).to_broadcast([P, GH, P]),
                            ALU.mult).then_inc(S["ua_ready"], 1)
                        pool.wait_ge(S["tr_ev"], 4 * g + 4)
                        wait(pool, S["y_ready"], 4 * g + ch)
                        nc.gpsimd.tensor_tensor(
                            skip[:].rearrange("p (h d) -> p h d", d=HP),
                            xs_rows[:, ch, :].rearrange("p (h d) -> p h d", d=HP),
                            dskip[:, g * GH:(g + 1) * GH].unsqueeze(2).to_broadcast([P, GH, HP]),
                            ALU.mult).then_inc(S["skipped"], 1)
                if s["kind"] == "branch" and s["tag"] == ("a", 1, 1):
                    pool.wait_ge(S["yT_lo"], HEADS)
                    for dst, j in ((g1b, 2), (sh2b, 3), (a2b, 4), (g2b, 5)):
                        pool.dma_start(dst[:], b_ada[0:1, j * D:(j + 1) * D].to_broadcast([P, D])).then_inc(
                            S["g_in"], 16)
                if s["kind"] == "col" and s["tag"] == ("ga", 1):
                    pool.wait_ge(S["stage_used"], 16)
                    pool.dma_start(gated_a, acc[:].rearrange("p k t -> p (k t)")).then_inc(S["spilled"], 16)
                if s["kind"] == "merge":
                    pool.wait_ge(S["proj_done"], out_index[("b", G4 - 1, 1)] + 4)
                    pool.wait_ge(S["spilled"], 16)
                    pool.dma_start(n2b[:], norm2_g.to_broadcast([P, D])).then_inc(S["ga_in"], 16)
                    pool.dma_start(ga_back[:].rearrange("p k t -> p (k t)"), gated_a).then_inc(S["ga_in"], 16)
                    for t in range(NT):
                        pool.dma_start(x2[:, t, :], x[0, t * P:(t + 1) * P, :]).then_inc(S["x2_in"], 16)
                    pool.dma_start(rbias[:], router_bias.to_broadcast([P, NE])).then_inc(S["rp_in"], 16)
                    L(nc.gpsimd.iota(farow[:, 0:NE], pattern=[[4, NE]], base=0, channel_multiplier=0))
                    L(nc.gpsimd.tensor_copy(e4[:], farow[:, 0:NE]))
                    L(nc.gpsimd.iota(tokid[:], pattern=[[P * TOPK, NT], [1, TOPK]], base=0, channel_multiplier=TOPK))
                    L(nc.gpsimd.memset(farow[:], FAR))
                    pool.dma_start(slot_table.rearrange("(p n) o -> p (n o)", p=P), farow[:]).then_inc(
                        S["table_far"], 16)
                    L(nc.gpsimd.memset(jlt[:], 1.0))
                    nc.gpsimd.affine_select(out=jlt[:], in_=jlt[:], compare_op=ALU.is_gt, fill=0.0, base=0,
                                            pattern=[[1, 8], [-1, 8]], channel_multiplier=0).then_inc(S["jlt_ready"], 1)
                if kind_ == "h2":
                    pool.wait_ge(S["m_lo"], KD)
                    pool.dma_start(wr[:], w_router[0].rearrange("(k p) n -> p k n", p=P)).then_inc(S["wr_in"], 16)
                    pool_route(pool, L)
            pool_moe(pool, L)

        @blk.scalar
        def _(act_e):
            a = act_e
            A = nc.scalar.activation
            L = line(a, S["act_line"])
            rs = [0]
            staged = [0]
            yt = [0]

            def inverse_root(n):
                rs[0] += 1
                a.wait_ge(S["rs_in"], rs[0])
                L(A(stat[:, 1, 0:n], stat[:, 0, 0:n], ACT.Ln))
                A(stat[:, 2, 0:n], stat[:, 1, 0:n], ACT.Exp, scale=-0.5).then_inc(S["rs_out"], 1)

            def split_hi(i):
                for u in ahead(i):
                    if "m" not in u:
                        continue
                    raw_wait(a, u)
                    free_split(a, u["m"])
                    A(hl[:, u["m"] % HL, 0, :], raw[:, u["n"] % RAW], ACT.Copy).then_inc(S["hi_done"], 1)

            def to_stage(src, func=ACT.Copy):
                n = staged[0]
                wait(a, S["stage_used"], n - 1)
                staged[0] += 1
                A(stage[:, n % 2], src, func).then_inc(S["proj_free"], 1)

            a.wait_ge(S["par_ev"], 2)
            A(silc[:], colp[:, 64:72], ACT.Silu).then_inc(S["silu_c"], 1)
            a.wait_ge(S["trig_in"], 1)
            for r in range(2):
                ins = A(trig[:, 3 + r], trig[:, r * 2], ACT.Sin)
            ins.then_inc(S["trig_out"], 1)
            a.wait_ge(S["trig_in"], 2)
            A(lam[:, 2:4], lam[:, 0:2], ACT.Exp).then_inc(S["trig_out"], 1)
            for t in range(NT):
                a.wait_ge(S["x_in"], 16 * NT)
                A(hsplit[:].rearrange("p a b -> p (a b)"), x_rows[:, t, :], ACT.Square,
                  accum_out=stat[:, 4, t:t + 1]).then_inc(S["sq_done"], 1)
                a.wait_ge(S["sq_done"], t + 1)
            inverse_root(NT)
            split_hi(-1)

            for i, s in enumerate(steps):
                split_hi(i)
                kind, tag, o0 = s["kind"], s["tag"], s["out0"]
                if kind == "h":
                    for k in range(KD):
                        a.wait_ge(S["h_tmp"], k + 1)
                        A(hT[:, k, 0, :], hsplit[:, k % 2], ACT.Copy).then_inc(S["h_hi"], 1)
                    a.wait_ge(S["params"], 16 * 16)
                    A(wdt_hl[:, :, 0, :], wdt[:], ACT.Copy).then_inc(S["wdt_hi"], 1)
                    a.wait_ge(S["dt_dve"], 1)
                    L(A(dwk[:, 2], dwk[:, 1], ACT.Exp))
                    A(dtb[:, 1], dtb[:, 1], ACT.Exp).then_inc(S["dt_exp"], 1)
                    a.wait_ge(S["dt_dve"], 2)
                    A(dwk[:, 4], dwk[:, 3], ACT.Ln).then_inc(S["dt_exp"], 1)
                    a.wait_ge(S["cum_ps"], 1)
                    A(expo[:].rearrange("p a t h -> p (a t h)"), psum[:, 5, 0:384], ACT.Exp).then_inc(S["cum_exp"], 1)
                elif kind in ("row", "col", "branch"):
                    for o in range(s["nout"]):
                        a.wait_ge(S["proj_done"], o0 + o + 1)
                        src = bank((o0 + o) % 4)
                        free = lambda ins: ins.then_inc(S["proj_free"], 1)
                        name = tag[0]
                        if name in "qk":
                            free(A(q_rows[:, "qk".index(name), o, :], src, ACT.Copy))
                        elif name == "v":
                            free(A(v_rows[:, o, :], src, ACT.Copy))
                        elif name in ("a", "b") and tag[1] == 0:
                            if name == "b":
                                a.wait_ge(S["spilled"], 16)
                            free(A(acc[:, tag[2] * 4 + o, :], src, ACT.Copy))
                        elif name in ("a", "b", "out", "sdn"):
                            to_stage(src)
                        elif name in ("ga", "gb"):
                            to_stage(src, ACT.Sigmoid)
                        elif name == "xs":
                            free(A(xbc[:, o, 3:], src, ACT.Copy))
                        elif name == "bc":
                            free(A(xbc[:, 4 + o, 3:], src, ACT.Copy))
                        elif name == "z":
                            free(A(z_rows[:, o, :], src, ACT.Silu))
                        elif name == "sgu":
                            A(sgu[:, o, 0:FE], src[:, 0:FE], ACT.Silu)
                            free(A(sgu[:, o, FE:], src[:, FE:], ACT.Copy))
                    if tag[0] in "qk" and len(tag[0]) == 1:
                        inverse_root(NT * 8)
                        if tag[0] == "k":
                            for n in range(2 * HALF):
                                c0 = tag[1] * 2 * HALF + n
                                a.wait_ge(S["qkT_ps"], c0 + 1)
                                A(qkT[:, n // HALF, n % HALF, :], bank(4 + n % 2), ACT.Copy).then_inc(S["qkT_ev"], 1)
                elif kind == "attn":
                    hf = tag
                    for n in range(4 * HALF + 1):
                        item = hf * 4 * HALF + n
                        if n < 4 * HALF:
                            j, qb = n // NT, n % NT
                            w_ = (qb + 1) * P
                            a.wait_ge(S["nmax"], item + 1)
                            wait(a, S["w_ready"], item - 1)
                            for m in range(2):
                                A(probs[:, n % 2, m, 0:w_], psum[:, (4, 0)[n % 2] + m, 0:w_], ACT.Exp,
                                  bias=sm[:, n % 2, m:m + 1], scale=0.125,
                                  accum_out=sm[:, n % 2, 2 + m:3 + m]).then_inc(S["p_exp"], 1)
                        if n >= 1:
                            item -= 1
                            n_ = n - 1
                            j, qb = n_ // NT, n_ % NT
                            w_ = (qb + 1) * P
                            a.wait_ge(S["wT_ps"], item + 1)
                            A(wT[:, 0:qb + 1, :].rearrange("p a b -> p (a b)"), psum[:, 6, 0:w_], ACT.Copy).then_inc(
                                S["wT_ev"], 1)
                            a.wait_ge(S["o_ps"], item + 1)
                            if qb == 0:
                                wait(a, S["yT_lo"], hf * HALF + j)
                            A(o_rows[:, qb, :], psum[:, (7, 3)[n_ % 2], 0:VD], ACT.Copy,
                              scale=sm[:, n_ % 2, 4:5]).then_inc(S["o_ev"], 1)
                            if qb == NT - 1:
                                inverse_root(NT)
                                h = hf * HALF + j
                                a.wait_ge(S["yT_ps"], h + 1)
                                A(ya_hl[:, j, 0, :], bank(2), ACT.Copy, scale=colp[:, 96:97]).then_inc(S["yT_hi"], 1)
                elif kind == "ssd":
                    g = tag

                    def square_sum(ch):
                        A(stage[:, 1], z_rows[:, ch, :], ACT.Square, accum_out=stat[:, 4, ch:ch + 1]).then_inc(
                            S["sq_done"], 1)
                        a.wait_ge(S["sq_done"], NT * (g + 1) + ch + 1)

                    for q in range(6):
                        a.wait_ge(S["conv_done"], 6 * g + q + 1)
                        A(cv[:, q], cv[:, q], ACT.Silu).then_inc(S["conv_silu"], 1)
                    for ch in range(NT):
                        a.wait_ge(S["tr_ps"], 4 * g + ch + 1)
                        A(xs_rows[:, ch, :], bank(ch % 2), ACT.Copy).then_inc(S["tr_ev"], 1)
                    a.wait_ge(S["cb_ps"], 2 * g + 1)
                    A(b_rows[:].rearrange("p a b -> p (a b)"), bank(2), ACT.Copy).then_inc(S["b_ev"], 1)
                    for ch in range(NT):
                        n = 4 * g + ch
                        a.wait_ge(S["seg_ps"], n + 1)
                        wait(a, S["ys_ps"], n)
                        A(lm[:].rearrange("p h l -> p (h l)"), psum[:, 4:6].rearrange("p b n -> p (b n)"),
                          ACT.Exp).then_inc(S["seg_exp"], 1)
                        if ch:
                            a.wait_ge(S["y_ready"], n)
                            square_sum(ch - 1)
                    a.wait_ge(S["y_ready"], 4 * g + 4)
                    square_sum(NT - 1)
                    inverse_root(NT)
                    for q in range(4):
                        h = HEADS + 4 * g + q
                        a.wait_ge(S["yT_ps"], h + 1)
                        A(yb_hl[:, q, 0, :], bank(q % 2), ACT.Copy, scale=colp[:, 97 + 4 * g + q:98 + 4 * g + q]).then_inc(
                            S["yT_hi"], 1)
                elif kind == "merge":
                    for k in range(KD):
                        a.wait_ge(S["merged"], k + 1)
                        A(hT[:, k, 0, :], acc[:, k, :], ACT.Copy).then_inc(S["m_hi"], 1)
                elif kind == "h2":
                    a.wait_ge(S["x2_ready"], 1)
                    for t in range(NT):
                        A(h2r[:, t, :], x2[:, t, :], ACT.Square, accum_out=stat[:, 4, t:t + 1]).then_inc(
                            S["sq_done"], 1)
                    inverse_root(NT)
                    a.wait_ge(S["wr_in"], 16)
                    A(wr_hl[:, :, 0, :], wr[:], ACT.Copy).then_inc(S["wr_hi"], 1)
                    for k in range(KD):
                        a.wait_ge(S["h2T_ps"], k + 1)
                        A(hT[:, k, 0, :], bank(4 + k % 2), ACT.Copy).then_inc(S["h2T_hi"], 1)
                    a.wait_ge(S["lg_ps"], 1)
                    A(rt[:, 0].rearrange("p t e -> p (t e)"), psum[:, 6, 0:NT * NE], ACT.Sigmoid).then_inc(S["lg_ev"], 1)
                elif kind == "sact":
                    for t in range(NT):
                        a.wait_ge(S["sT_ps"], t + 1)
                        A(sactT[:, :, 0, t * P:(t + 1) * P], psum[:, 4 + t % 2, 0:2 * P].rearrange(
                            "p (k t) -> p k t", t=P), ACT.Copy).then_inc(S["sT_hi"], 1)
            act_moe(a, A, L)

        @blk.tensor
        def _(pe):
            M = nc.tensor.matmul
            tr = nc.tensor.transpose

            def three(dst, lhs, rhs, first, last):
                M(dst, lhs(0), rhs(0), start=first, stop=False)
                M(dst, lhs(0), rhs(1), start=False, stop=False)
                return M(dst, lhs(1), rhs(0), start=False, stop=last)

            pe.wait_ge(S["params"], 16 * 16)
            pe.wait_ge(S["consts"], 1)
            tr(psum[:, 6, 0:113], pr1[0:113, :], ident[0:113, 0:113]).then_inc(S["par_T"], 1)
            tr(psum[:, 5, 0:96], pr2[0:96, :], ident[0:96, 0:96]).then_inc(S["par_T"], 1)

            for s in steps:
                kind, tag, o0 = s["kind"], s["tag"], s["out0"]
                if kind == "mod":
                    pe.wait_ge(S["mod_used"], 2 * (tag + 1))
                    wait(pe, S["mod_ev"], tag)
                    if tag < 4:
                        if tag == 0:
                            pe.wait_ge(S["par_ev"], 2)
                        for b in range(4):
                            ins = M(psum[:, 7, b:b + 1], modacc[:, b * P:(b + 1) * P], ones[:, 0:1],
                                    start=True, stop=True)
                    else:
                        ins = M(bank(7), ones[:], modacc[:], start=True, stop=True)
                    ins.then_inc(S["mod_ps"], 1)
                elif kind == "h":
                    pe.wait_ge(S["xr_ready"], NT)
                    for k in range(KD):
                        wait(pe, S["h_tmp"], k - 1)
                        for t in range(NT):
                            ins = tr(psum[:, 4 + k % 2, t * P:(t + 1) * P], x_rows[:, t, k * P:(k + 1) * P], ident[:])
                        ins.then_inc(S["xT_ps"], 1)
                    pe.wait_ge(S["wdt_lo"], 1)
                    pe.wait_ge(S["h_lo"], KD)
                    for t in range(NT):
                        for k in range(KD):
                            ins = three(psum[:, 6, t * 32:(t + 1) * 32],
                                        lambda q: hT[:, k, q, t * P:(t + 1) * P], lambda q: wdt_hl[:, k, q, :],
                                        k == 0, k == KD - 1)
                    ins.then_inc(S["dt_ps"], 1)
                    pe.wait_ge(S["dt_a"], 1)
                    for q, tri in enumerate((upper, later, ones)):
                        for t in range(NT):
                            ins = M(psum[:, 5, (q * NT + t) * 32:(q * NT + t + 1) * 32], tri[:], aa[:, t, :],
                                    start=True, stop=True)
                    ins.then_inc(S["cum_ps"], 1)
                elif kind in ("row", "col", "branch"):
                    name = tag[0]
                    nk = len(s["u"]) * s["ks"]
                    wide = UNIT // s["ks"]
                    if name == "a":
                        pe.wait_ge(S["yT_lo"], HALF * (tag[1] + 1))
                    elif name == "b":
                        pe.wait_ge(S["yT_lo"], HEADS + 4 * (tag[1] + 1))
                    elif name == "out":
                        pe.wait_ge(S["m_lo"], KD)
                    elif name == "sgu":
                        pe.wait_ge(S["h2T_lo"], KD)
                    elif name == "sdn":
                        pe.wait_ge(S["sT_lo"], NT)
                    for ui, u in enumerate(s["u"]):
                        pe.wait_ge(S["lo_done"], u["m"] + 1)
                        wv = [hl[:, u["m"] % HL, q, :].rearrange("p (k n) -> p k n", n=wide) for q in range(2)]
                        for o in range(s["nout"]):
                            dst = bank((o0 + o) % 4)
                            if ui == 0:
                                wait(pe, S["proj_free"], o0 + o - 3)
                            for kk in range(s["ks"]):
                                k = ui * s["ks"] + kk
                                if name == "sdn":
                                    t, half = o // 2, o % 2
                                    lhs = lambda q: sactT[:, k, q, t * P:(t + 1) * P]
                                    rhs = lambda q: wv[q][:, kk, half * 512:(half + 1) * 512]
                                elif kind == "row":
                                    lhs = lambda q: hT[:, k, q, o * P:(o + 1) * P]
                                    rhs = lambda q: wv[q][:, kk, :]
                                else:
                                    y = {"a": ya_hl, "b": yb_hl}.get(name, hT)
                                    lhs = lambda q: wv[q][:, kk, o * P:(o + 1) * P]
                                    rhs = lambda q: y[:, k, q, :]
                                ins = three(dst, lhs, rhs, k == 0, k == nk - 1)
                            if ui == len(s["u"]) - 1:
                                ins.then_inc(S["proj_done"], 1)
                            elif o == s["nout"] - 1:
                                ins.then_inc(S["half_done"], 1)
                    if len(name) == 1 and name in "qk":
                        x_ = "qk".index(name)
                        if name == "k":
                            for n in range(2 * HALF):
                                c0 = tag[1] * 2 * HALF + n
                                xx, j = n // HALF, n % HALF
                                pe.wait_ge(S["qk_ready"], 2 * tag[1] + xx + 1)
                                if n >= 2:
                                    pe.wait_ge(S["qkT_ev"], c0 - 1)
                                for t in range(NT):
                                    ins = tr(psum[:, 4 + n % 2, t * P:(t + 1) * P],
                                             q_rows[:, xx, t, j * P:(j + 1) * P], ident[:])
                                ins.then_inc(S["qkT_ps"], 1)
                elif kind == "attn":
                    hf = tag
                    pe.wait_ge(S["qkT_ev"], 2 * HALF * (hf + 1))
                    pe.wait_ge(S["proj_free"], out_index[("v", hf)] + 4)
                    for n in range(4 * HALF + 1):
                        item = hf * 4 * HALF + n
                        if n < 4 * HALF:
                            j, qb = n // NT, n % NT
                            w_ = (qb + 1) * P
                            wait(pe, S["p_exp"], 2 * (item - 1))
                            for m in range(2):
                                dst = psum[:, (4, 0)[n % 2] + m, :]
                                rows = slice(m * HD, (m + 1) * HD)
                                M(dst[:, 0:w_], qkT[rows, 0, j, qb * P:(qb + 1) * P], qkT[rows, 1, j, 0:w_],
                                  start=True, stop=False, skip_group_check=True)
                                ins = M(dst[:, qb * P:w_], ident[:], causal[:], start=False, stop=True,
                                        skip_group_check=True)
                            ins.then_inc(S["sc_ps"], 1)
                        if n >= 1:
                            item -= 1
                            n_ = n - 1
                            j, qb = n_ // NT, n_ % NT
                            pe.wait_ge(S["w_ready"], item + 1)
                            wait(pe, S["wT_ev"], item)
                            for b in range(qb + 1):
                                ins = tr(psum[:, 6, b * P:(b + 1) * P], wgt[:, n_ % 2, b * P:(b + 1) * P], ident[:])
                            ins.then_inc(S["wT_ps"], 1)
                            pe.wait_ge(S["wT_ev"], item + 1)
                            wait(pe, S["o_ev"], item - 1)
                            for b in range(qb + 1):
                                ins = M(psum[:, (7, 3)[n_ % 2], 0:VD], wT[:, b, :],
                                        v_rows[:, b, j * VD:(j + 1) * VD], start=(b == 0), stop=(b == qb))
                            ins.then_inc(S["o_ps"], 1)
                            if qb == NT - 1:
                                h = hf * HALF + j
                                pe.wait_ge(S["o_ready"], h + 1)
                                wait(pe, S["yT_lo"], h)
                                for t in range(NT):
                                    ins = tr(psum[:, 2, t * P:(t + 1) * P], o_rows[:, t, :], ident[:])
                                ins.then_inc(S["yT_ps"], 1)
                elif kind == "ssd":
                    g = tag
                    pe.wait_ge(S["proj_free"], out_index[("z", g)] + 4)
                    pe.wait_ge(S["conv_silu"], 6 * (g + 1))
                    for ch in range(NT):
                        wait(pe, S["tr_ev"], 4 * g + ch - 1 if ch >= 2 else 0)
                        for q in range(4):
                            ins = tr(psum[:, ch % 2, q * P:(q + 1) * P], cv[:, q, ch * P:(ch + 1) * P], ident[:])
                        ins.then_inc(S["tr_ps"], 1)
                    for ch in range(NT):
                        ins = tr(psum[:, 2, ch * P:(ch + 1) * P], cv[:, 4, ch * P:(ch + 1) * P], ident[:])
                    ins.then_inc(S["cb_ps"], 1)
                    for ch in range(NT):
                        cs = slice(ch * P, (ch + 1) * P)
                        ins = M(psum[:, 3, cs], cv[:, 4, cs], cv[:, 5, cs], start=True, stop=True)
                    ins.then_inc(S["cb_ps"], 1)
                    for ch in range(NT):
                        n = 4 * g + ch
                        pe.wait_ge(S["ua_ready"], n + 1)
                        wait(pe, S["seg_exp"], n)
                        for b in range(2):
                            ins = M(bank(4 + b), later[:], ua[:, 4 * b:4 * b + 4, :].rearrange("p h l -> p (h l)"),
                                    start=True, stop=True)
                        ins.then_inc(S["seg_ps"], 1)
                        pe.wait_ge(S["m_ready"], n + 1)
                        pe.wait_ge(S["xd_ready"], n + 1)
                        wait(pe, S["y_ready"], n)
                        for h in range(GH):
                            M(psum[:, 6, h * HP:(h + 1) * HP], lm[:, h, :], xdt[:, 0, h * HP:(h + 1) * HP],
                              start=True, stop=True)
                        pe.wait_ge(S["st_ready"], n + 1)
                        ins = M(bank(7), cv[:, 5, ch * P:(ch + 1) * P], state[:], start=True, stop=True)
                        if ch == 0:
                            pe.wait_ge(S["tr_ev"], 4 * g + 4)
                            pe.wait_ge(S["b_ev"], g + 1)
                        if ch < NT - 1:
                            ins = M(bank(ch % 2), b_rows[:, ch, :], xdt[:, 1, :], start=True, stop=True)
                        ins.then_inc(S["ys_ps"], 1)
                    pe.wait_ge(S["yn_ready"], g + 1)
                    for q in range(4):
                        h = HEADS + 4 * g + q
                        wait(pe, S["yT_lo"], h - 1 if q >= 2 else 0)
                        for t in range(NT):
                            ins = tr(psum[:, q % 2, t * P:(t + 1) * P], z_rows[:, t, q * P:(q + 1) * P], ident[:])
                        ins.then_inc(S["yT_ps"], 1)
                    pe.wait_ge(S["yT_lo"], HEADS + 4 * g + 4)
                elif kind == "h2":
                    pe.wait_ge(S["h2_row"], 1)
                    for k in range(KD):
                        wait(pe, S["h2T_lo"], k - 1)
                        for t in range(NT):
                            ins = tr(psum[:, 4 + k % 2, t * P:(t + 1) * P], h2r[:, t, k * P:(k + 1) * P], ident[:])
                        ins.then_inc(S["h2T_ps"], 1)
                    pe.wait_ge(S["wr_lo"], 1)
                    pe.wait_ge(S["h2T_lo"], KD)
                    for t in range(NT):
                        for k in range(KD):
                            ins = three(psum[:, 6, t * NE:(t + 1) * NE],
                                        lambda q: hT[:, k, q, t * P:(t + 1) * P], lambda q: wr_hl[:, k, q, :],
                                        k == 0, k == KD - 1)
                    ins.then_inc(S["lg_ps"], 1)
                elif kind == "sact":
                    pe.wait_ge(S["sel_ready"], NT)
                    for t in range(NT):
                        for j in range(t):
                            M(psum[:, 7, t * NE:(t + 1) * NE], ones[:], rt[:, 3, j, :], start=(j == 0), stop=False)
                        M(psum[:, 7, t * NE:(t + 1) * NE], before[:], rt[:, 3, t, :], start=(t == 0), stop=True)
                    for j in range(NT):
                        ins = M(psum[:, 7, NT * NE:(NT + 1) * NE], ones[:], rt[:, 3, j, :], start=(j == 0),
                                stop=(j == NT - 1))
                    ins.then_inc(S["pos_ps"], 1)
                    for t in range(NT):
                        pe.wait_ge(S["sa_ready"], t + 1)
                        wait(pe, S["sT_lo"], t - 1)
                        for k in range(2):
                            ins = tr(psum[:, 4 + t % 2, k * P:(k + 1) * P], sgu[:, t, k * P:(k + 1) * P], ident[:])
                        ins.then_inc(S["sT_ps"], 1)
            pe_moe(pe, M, tr, three)

        @blk.vector
        def _(v):
            V = nc.vector
            L = line(v, S["vec_line"])
            TS, TT, STT = V.tensor_scalar, V.tensor_tensor, V.scalar_tensor_tensor
            rs = [0]
            used = [0]
            taken = [0]

            def inverse_root(n):
                rs[0] += 1
                v.wait_ge(S["rs_out"], rs[0])
                L(TT(stat[:, 3, 0:n], stat[:, 2, 0:n], stat[:, 2, 0:n], ALU.mult))
                L(TT(stat[:, 3, 0:n], stat[:, 3, 0:n], stat[:, 0, 0:n], ALU.mult))
                L(TS(stat[:, 3, 0:n], stat[:, 3, 0:n], -0.5, 1.5, ALU.mult, ALU.add))
                L(TT(stat[:, 3, 0:n], stat[:, 3, 0:n], stat[:, 2, 0:n], ALU.mult))

            def mean_eps(src, n, width):
                TS(stat[:, 0, 0:n], src, 1.0 / width, EPS, ALU.mult, ALU.add).then_inc(S["rs_in"], 1)

            def take_mod(upto):
                while taken[0] < upto:
                    j = taken[0]
                    taken[0] += 1
                    v.wait_ge(S["mod_ps"], j + 1)
                    if j < 4:
                        TT(shT[:, j * 4:j * 4 + 4], psum[:, 7, 0:4], colp[:, j * 4:j * 4 + 4], ALU.add).then_inc(
                            S["mod_ev"], 1)
                    else:
                        v.wait_ge(S["g_in"], 64)
                        dst = {2: g1b, 3: sh2b, 4: a2b, 5: g2b}[j // 2][:, (j % 2) * 512:(j % 2 + 1) * 512]
                        TT(dst, dst, bank(7), ALU.add).then_inc(S["mod_ev"], 1)
                    v.wait_ge(S["mod_ev"], j + 1)

            def split_lo(i):
                for u in ahead(i):
                    r = raw[:, u["n"] % RAW]
                    if "m" in u:
                        v.wait_ge(S["hi_done"], u["m"] + 1)
                        h_ = hl[:, u["m"] % HL]
                        TT(h_[:, 1, :], r, h_[:, 0, :].bitcast(F32), ALU.subtract).then_inc(S["lo_done"], 1)
                        continue
                    raw_wait(v, u)
                    half = (u["mod"] - 1) % 2
                    if half == 0:
                        take_mod((u["mod"] - 1) // 2)
                    for kk in range(4):
                        k = half * 4 + kk
                        src = r.rearrange("p (k n) -> p k n", n=512)[:, kk, :]
                        if k == 0:
                            ins = TS(modacc[:], src, silc[:, 0:1], None, ALU.mult)
                        else:
                            ins = STT(out=modacc[:], in0=src, scalar=silc[:, k:k + 1], in1=modacc[:], op0=ALU.mult,
                                      op1=ALU.add)
                        if kk < 3:
                            L(ins)
                    ins.then_inc(S["mod_used"], 1)
                    v.wait_ge(S["mod_used"], u["mod"])

            def staged():
                used[0] += 1
                return stage[:, (used[0] - 1) % 2]

            v.wait_ge(S["par_T"], 1)
            V.tensor_copy(colp[:], psum[:, 6, 0:113]).then_inc(S["par_ev"], 1)
            v.wait_ge(S["par_T"], 2)
            V.tensor_copy(convw[:], psum[:, 5, 0:96]).then_inc(S["par_ev"], 1)
            v.wait_ge(S["par_ev"], 2)
            L(V.tensor_copy(posf[:], posi[:]))
            t32 = lambda n: trig[:, n].rearrange("p (t i) -> p t i", i=32)
            L(TT(t32(0), posf[:].unsqueeze(2).to_broadcast([P, NT, 32]), freq[:].unsqueeze(1).to_broadcast([P, NT, 32]),
                 ALU.mult))
            magic = 12582912.0
            L(TS(trig[:, 1], trig[:, 0], float(np.float32(1 / TWO_PI)), magic, ALU.mult, ALU.add))
            L(TS(trig[:, 1], trig[:, 1], magic, None, ALU.subtract))
            c1 = 6.28125
            c2 = float(np.float32(int((TWO_PI - c1) * 2 ** 20) / 2 ** 20))
            c3 = float(np.float32(TWO_PI - c1 - c2))
            for part in (c1, c2, c3):
                L(STT(out=trig[:, 0], in0=trig[:, 1], scalar=-part, in1=trig[:, 0], op0=ALU.mult, op1=ALU.add))
            L(TS(trig[:, 2], trig[:, 0], float(np.float32(np.pi / 2)), None, ALU.add))
            L(TS(trig[:, 1], trig[:, 2], float(np.float32(np.pi)), -TWO_PI, ALU.is_gt, ALU.mult))
            L(TT(trig[:, 2], trig[:, 2], trig[:, 1], ALU.add))
            L(TS(trig[:, 0], trig[:, 0], 3.1415925, -3.1415925, ALU.min, ALU.max))
            TS(trig[:, 2], trig[:, 2], 3.1415925, -3.1415925, ALU.min, ALU.max).then_inc(S["trig_in"], 1)
            prod = stage[:, 0, 0:2 * HD].rearrange("p (a d) -> p a d", d=HD)
            L(TT(prod, lamt[:, 0::2, :], lamt[:, 1::2, :], ALU.mult))
            V.tensor_reduce(lam[:, 0:2], prod, AX, ALU.add).then_inc(S["trig_in"], 1)
            v.wait_ge(S["trig_out"], 2)
            L(TT(lam[:, 4:5], lam[:, 3:4], lam[:, 2:3], ALU.subtract))
            L(TS(lam[:, 4:5], lam[:, 4:5], LAMBDA_INIT, None, ALU.subtract))
            for x_ in range(2):
                for half in range(2):
                    here = gqk[:, x_, half * 32:(half + 1) * 32].unsqueeze(1).to_broadcast([P, NT, 32])
                    other = gqk[:, x_, (1 - half) * 32:(2 - half) * 32].unsqueeze(1).to_broadcast([P, NT, 32])
                    L(TT(tabs[:, x_, 0, :, half * 32:(half + 1) * 32], t32(4), here, ALU.mult))
                    L(TT(tabs[:, x_, 1, :, half * 32:(half + 1) * 32], t32(3), other, ALU.mult))
                L(TS(tabs[:, x_, 1, :, 0:32], tabs[:, x_, 1, :, 0:32], -1.0, None, ALU.mult))
            v.wait_ge(S["sq_done"], NT)
            mean_eps(stat[:, 4, 0:NT], NT, D)
            inverse_root(NT)
            for t in range(NT):
                TS(x_rows[:, t, :], x_rows[:, t, :], stat[:, 3, t:t + 1], None, ALU.mult).then_inc(S["xr_ready"], 1)
            v.wait_ge(S["silu_c"], 1)
            split_lo(-1)

            for i, s in enumerate(steps):
                split_lo(i)
                kind, tag, o0 = s["kind"], s["tag"], s["out0"]
                name = tag[0] if isinstance(tag, tuple) else None
                if kind == "mod":
                    take_mod(tag + 1)
                elif kind == "h":
                    L(TS(a1T[:], shT[:, 8:16], 1.0, None, ALU.add))
                    L(TT(a1T[:], a1T[:], colp[:, 48:56], ALU.mult))
                    for k in range(KD):
                        v.wait_ge(S["xT_ps"], k + 1)
                        TS(hsplit[:, k % 2], bank(4 + k % 2), a1T[:, k:k + 1], shT[:, k:k + 1], ALU.mult,
                           ALU.add).then_inc(S["h_tmp"], 1)
                        v.wait_ge(S["h_tmp"], k + 1)
                        v.wait_ge(S["h_hi"], k + 1)
                        TT(hT[:, k, 1, :], hsplit[:, k % 2], hT[:, k, 0, :].bitcast(F32), ALU.subtract).then_inc(
                            S["h_lo"], 1)
                    v.wait_ge(S["wdt_hi"], 1)
                    TT(wdt_hl[:, :, 1, :], wdt[:], wdt_hl[:, :, 0, :].bitcast(F32), ALU.subtract).then_inc(S["wdt_lo"], 1)
                    th = lambda n: dwk[:, n].rearrange("p (t h) -> p t h", h=32)
                    over_h = lambda ap: ap.unsqueeze(1).to_broadcast([P, NT, 32])
                    v.wait_ge(S["dt_ps"], 1)
                    L(TT(th(0), psum[:, 6, 0:NT * 32].rearrange("p (t h) -> p t h", h=32), over_h(dtb[:, 0]), ALU.add))
                    L(TS(dwk[:, 5], dwk[:, 0], 0.0, None, ALU.max))
                    STT(out=dwk[:, 1], in0=dwk[:, 5], scalar=-2.0, in1=dwk[:, 0], op0=ALU.mult,
                        op1=ALU.add).then_inc(S["dt_dve"], 1)
                    v.wait_ge(S["dt_exp"], 1)
                    TS(dwk[:, 3], dwk[:, 2], 1.0, None, ALU.add).then_inc(S["dt_dve"], 1)
                    v.wait_ge(S["dt_dve"], 2)
                    L(TS(dwk[:, 1], dwk[:, 3], 1.0, 1e-30, ALU.subtract, ALU.max))
                    L(V.reciprocal(dwk[:, 1], dwk[:, 1]))
                    v.wait_ge(S["dt_exp"], 2)
                    L(TT(dwk[:, 2], dwk[:, 2], dwk[:, 1], ALU.mult))
                    L(TT(dwk[:, 2], dwk[:, 2], dwk[:, 4], ALU.mult))
                    dt_ = dtp[:].rearrange("p t h -> p (t h)")
                    L(TT(dt_, dwk[:, 2], dwk[:, 5], ALU.add))
                    L(TT(aa[:], dtp[:], over_h(dtb[:, 1]), ALU.mult))
                    TS(aa[:], aa[:], -1.0, None, ALU.mult).then_inc(S["dt_a"], 1)
                    v.wait_ge(S["cum_exp"], 1)
                    L(TT(dtdec[:], dtp[:], expo[:, 1], ALU.mult))
                elif name in ("q", "k"):
                    x_ = "qk".index(name)
                    vec = lambda ap: ap.rearrange("p (c d) -> p c d", d=HD)
                    for t in range(NT):
                        v.wait_ge(S["proj_free"], o0 + t + 1)
                        row = q_rows[:, x_, t, :]
                        L(TT(stage[:, 0], row, row, ALU.mult))
                        L(V.tensor_reduce(stat[:, 4, t * 8:(t + 1) * 8], vec(stage[:, 0]), AX, ALU.add))
                    mean_eps(stat[:, 4, 0:32], 32, HD)
                    for t in range(NT):
                        row = vec(q_rows[:, x_, t, :])
                        plain = tabs[:, x_, 0, t, :].unsqueeze(1).to_broadcast([P, 8, HD])
                        swap = lambda h_: tabs[:, x_, 1, t, h_ * 32:(h_ + 1) * 32].unsqueeze(1).to_broadcast([P, 8, 32])
                        s0, s1 = vec(stage[:, 0]), vec(stage[:, 1])
                        TT(s0[:, :, 0:32], row[:, :, 32:64], swap(0), ALU.mult)
                        L(TT(s0[:, :, 32:64], row[:, :, 0:32], swap(1), ALU.mult))
                        L(TT(s1, row, plain, ALU.mult))
                        L(TT(row, s0, s1, ALU.add))
                    inverse_root(32)
                    for t in range(NT):
                        row = vec(q_rows[:, x_, t, :])
                        ins = TT(row, row, stat[:, 3, t * 8:(t + 1) * 8].unsqueeze(2).to_broadcast([P, 8, HD]), ALU.mult)
                        if t < NT - 1:
                            L(ins)
                    ins.then_inc(S["qk_ready"], 1)
                    v.wait_ge(S["qk_ready"], 2 * tag[1] + x_ + 1)
                elif kind == "attn":
                    hf = tag

                    def weights(n):
                        item = hf * 4 * HALF + n
                        w_ = (n % NT + 1) * P
                        k = sm[:, n % 2]
                        v.wait_ge(S["p_exp"], 2 * (item + 1))
                        L(V.reciprocal(k[:, 4:6], k[:, 2:4]))
                        L(TT(k[:, 6:7], k[:, 2:3], k[:, 5:6], ALU.mult))
                        L(TT(k[:, 6:7], k[:, 6:7], lam[:, 4:5], ALU.mult))
                        wait(v, S["wT_ps"], item - 1)
                        STT(out=wgt[:, n % 2, 0:w_], in0=probs[:, n % 2, 1, 0:w_], scalar=k[:, 6:7],
                            in1=probs[:, n % 2, 0, 0:w_], op0=ALU.mult, op1=ALU.add).then_inc(S["w_ready"], 1)
                        v.wait_ge(S["w_ready"], item + 1)

                    for n in range(4 * HALF + 1):
                        item = hf * 4 * HALF + n
                        if n < 4 * HALF:
                            w_ = (n % NT + 1) * P
                            b0 = (4, 0)[n % 2]
                            v.wait_ge(S["sc_ps"], item + 1)
                            wait(v, S["o_ev"], item - 1)
                            L(V.tensor_reduce(sm[:, n % 2, 0:2], psum[:, b0:b0 + 2, 0:w_], AX, ALU.max))
                            TS(sm[:, n % 2, 0:2], sm[:, n % 2, 0:2], -0.125, None, ALU.mult).then_inc(S["nmax"], 1)
                            weights(n)
                        if n >= 1 and (n - 1) % NT == NT - 1:
                            j = (n - 1) // NT
                            h = hf * HALF + j
                            v.wait_ge(S["o_ev"], hf * 4 * HALF + n)
                            L(TT(o_sq[:], o_rows[:], o_rows[:], ALU.mult))
                            L(V.tensor_reduce(stat[:, 4, 0:NT], o_sq[:], AX, ALU.add))
                            mean_eps(stat[:, 4, 0:NT], NT, VD)
                            inverse_root(NT)
                            L(TS(stat[:, 3, 0:NT], stat[:, 3, 0:NT], 1.0 - LAMBDA_INIT, None, ALU.mult))
                            TT(o_rows[:], o_rows[:], stat[:, 3, 0:NT].unsqueeze(2).to_broadcast([P, NT, VD]),
                               ALU.mult).then_inc(S["o_ready"], 1)
                            v.wait_ge(S["yT_hi"], h + 1)
                            STT(out=ya_hl[:, j, 1, :], in0=bank(2), scalar=colp[:, 96:97],
                                in1=ya_hl[:, j, 0, :].bitcast(F32), op0=ALU.mult, op1=ALU.subtract).then_inc(S["yT_lo"], 1)
                elif name in ("a", "b") and kind == "branch" and tag[1] > 0:
                    for o in range(4):
                        v.wait_ge(S["proj_free"], o0 + o + 1)
                        dst = acc[:, tag[2] * 4 + o, :]
                        TT(dst, dst, staged(), ALU.add).then_inc(S["stage_used"], 1)
                        v.wait_ge(S["stage_used"], used[0])
                elif name in ("ga", "gb"):
                    for o in range(4):
                        v.wait_ge(S["proj_free"], o0 + o + 1)
                        dst = acc[:, tag[1] * 4 + o, :]
                        TT(dst, dst, staged(), ALU.mult).then_inc(S["stage_used"], 1)
                        v.wait_ge(S["stage_used"], used[0])
                elif kind == "ssd":
                    g = tag
                    hd = lambda ap: ap.rearrange("p (h d) -> p h d", d=HP)
                    per_h = lambda ap: ap[:, g * GH:(g + 1) * GH].unsqueeze(2).to_broadcast([P, GH, HP])
                    if g == 0:
                        L(V.memset(xbc[:, :, 0:3], 0.0))
                    for q in range(6):
                        ct = 4 * g + q if q < 4 else 16 + 4 * (q - 4) + g
                        v.wait_ge(S["proj_free"], (out_index[("xs", g)] + q if q < 4 else out_index[("bc", g)] + q - 4) + 1)
                        if q == 0 and g:
                            v.wait_ge(S["proj_done"], out_index[("b", g - 1, 1)] + 4)
                        tap = lambda k: convw[:, k * 24 + ct:k * 24 + ct + 1]
                        L(TS(cv[:, q], xbc[:, q, 0:T], tap(0), colp[:, 72 + ct:73 + ct], ALU.mult, ALU.add))
                        for k in range(1, 4):
                            ins = STT(out=cv[:, q], in0=xbc[:, q, k:k + T], scalar=tap(k), in1=cv[:, q], op0=ALU.mult,
                                      op1=ALU.add)
                            if k < 3:
                                L(ins)
                        ins.then_inc(S["conv_done"], 1)
                    v.wait_ge(S["cb_ps"], 2 * g + 2)
                    L(TT(cbm[:], bank(3).rearrange("p (c l) -> p c l", l=P),
                         upper[:].unsqueeze(1).to_broadcast([P, NT, P]), ALU.mult))
                    v.wait_ge(S["tr_ev"], 4 * g + 4)
                    V.memset(state[:], 0.0).then_inc(S["st_ready"], 1)
                    for ch in range(NT):
                        n = 4 * g + ch
                        L(TT(hd(xdt[:, 0]), hd(xs_rows[:, ch, :]), per_h(dtp[:, ch, :]), ALU.mult))
                        TT(hd(xdt[:, 1]), hd(xs_rows[:, ch, :]), per_h(dtdec[:, ch, :]), ALU.mult).then_inc(
                            S["xd_ready"], 1)
                        v.wait_ge(S["seg_exp"], n + 1)
                        TT(lm[:], lm[:], cbm[:, ch, :].unsqueeze(1).to_broadcast([P, GH, P]), ALU.mult).then_inc(
                            S["m_ready"], 1)
                        v.wait_ge(S["ys_ps"], n + 1)
                        tmp = stage[:, 0]
                        L(TT(hd(tmp), hd(bank(7)), per_h(expo[:, 0, ch, :]), ALU.mult))
                        L(TT(tmp, tmp, bank(6), ALU.add))
                        v.wait_ge(S["skipped"], n + 1)
                        L(TT(tmp, tmp, skip[:], ALU.add))
                        TT(z_rows[:, ch, :], z_rows[:, ch, :], tmp, ALU.mult).then_inc(S["y_ready"], 1)
                        if ch < NT - 1:
                            L(TT(hd(state[:]), hd(state[:]), per_h(expo[:, 2, ch, :]), ALU.mult))
                            TT(state[:], state[:], bank(ch % 2), ALU.add).then_inc(S["st_ready"], 1)
                            v.wait_ge(S["st_ready"], n + 2)
                    v.wait_ge(S["sq_done"], NT * (g + 2))
                    mean_eps(stat[:, 4, 0:NT], NT, 512)
                    inverse_root(NT)
                    for t in range(NT):
                        ins = TS(z_rows[:, t, :], z_rows[:, t, :], stat[:, 3, t:t + 1], None, ALU.mult)
                        if t < NT - 1:
                            L(ins)
                    ins.then_inc(S["yn_ready"], 1)
                    for q in range(4):
                        h = HEADS + 4 * g + q
                        v.wait_ge(S["yT_hi"], h + 1)
                        STT(out=yb_hl[:, q, 1, :], in0=bank(q % 2), scalar=colp[:, 97 + 4 * g + q:98 + 4 * g + q],
                            in1=yb_hl[:, q, 0, :].bitcast(F32), op0=ALU.mult, op1=ALU.subtract).then_inc(S["yT_lo"], 1)
                elif kind == "merge":
                    v.wait_ge(S["ga_in"], 32)
                    v.wait_ge(S["proj_done"], out_index[("gb", 1)] + 4)
                    for k in range(KD):
                        TT(acc[:, k, :], acc[:, k, :], ga_back[:, k, :], ALU.add).then_inc(S["merged"], 1)
                    for k in range(KD):
                        v.wait_ge(S["m_hi"], k + 1)
                        TT(hT[:, k, 1, :], acc[:, k, :], hT[:, k, 0, :].bitcast(F32), ALU.subtract).then_inc(S["m_lo"], 1)
                elif name in ("out", "sdn"):
                    v.wait_ge(S["x2_in"], 16 * NT)
                    for o in range(s["nout"]):
                        t, half = (o, tag[1]) if name == "out" else (o // 2, o % 2)
                        cols = slice(half * 512, (half + 1) * 512)
                        v.wait_ge(S["proj_free"], o0 + o + 1)
                        buf = staged()
                        L(TT(buf, buf, (g1b if name == "out" else g2b)[:, cols], ALU.mult))
                        TT(x2[:, t, cols], x2[:, t, cols], buf, ALU.add).then_inc(S["stage_used"], 1)
                        v.wait_ge(S["stage_used"], used[0])
                elif kind == "h2":
                    L(TS(a2b[:], a2b[:], 1.0, None, ALU.add))
                    TT(a2b[:], a2b[:], n2b[:], ALU.mult).then_inc(S["x2_ready"], 1)
                    v.wait_ge(S["x2_ready"], 1)
                    v.wait_ge(S["sq_done"], NT * (G4 + 2))
                    mean_eps(stat[:, 4, 0:NT], NT, D)
                    inverse_root(NT)
                    for t in range(NT):
                        L(STT(out=h2r[:, t, :], in0=x2[:, t, :], scalar=stat[:, 3, t:t + 1], in1=a2b[:], op0=ALU.mult,
                              op1=ALU.mult))
                        ins = TT(h2r[:, t, :], h2r[:, t, :], sh2b[:], ALU.add)
                        if t < NT - 1:
                            L(ins)
                    ins.then_inc(S["h2_row"], 1)
                    v.wait_ge(S["wr_hi"], 1)
                    TT(wr_hl[:, :, 1, :], wr[:], wr_hl[:, :, 0, :].bitcast(F32), ALU.subtract).then_inc(S["wr_lo"], 1)
                    for k in range(KD):
                        v.wait_ge(S["h2T_hi"], k + 1)
                        TT(hT[:, k, 1, :], bank(4 + k % 2), hT[:, k, 0, :].bitcast(F32), ALU.subtract).then_inc(
                            S["h2T_lo"], 1)
                    route(v, L)
                elif kind == "sact":
                    slots(v, L)
                    for t in range(NT):
                        v.wait_ge(S["proj_free"], out_index[("sgu", 0)] + t + 1)
                        TT(sgu[:, t, 0:FE], sgu[:, t, 0:FE], sgu[:, t, FE:], ALU.mult).then_inc(S["sa_ready"], 1)
                        v.wait_ge(S["sT_hi"], t + 1)
                        TT(sactT[:, :, 1, t * P:(t + 1) * P], psum[:, 4 + t % 2, 0:2 * P].rearrange(
                            "p (k t) -> p k t", t=P), sactT[:, :, 0, t * P:(t + 1) * P].bitcast(F32),
                            ALU.subtract).then_inc(S["sT_lo"], 1)
            vec_moe(v, L)


def kernel(x, c, positions, w_ada, b_ada, norm1_g, w_in, q_norm_g, k_norm_g, lambda_qk, subln_g,
           conv_w, conv_b, dt_bias, a_log, d_skip, ssd_norm_g, w_branch_a, w_branch_b, w_out,
           norm2_g, w_router, router_bias, w_exp_gate, w_exp_up, w_exp_down,
           w_sh_gate, w_sh_up, w_sh_down):
    import concourse.bacc as bacc
    from concourse.bass_utils import run_bass_kernel_spmd

    inputs = dict(locals())
    for name in ("bacc", "run_bass_kernel_spmd"):
        inputs.pop(name)
    nc = bacc.Bacc("TRN2", target_bir_lowering=False, num_devices=1)
    arrays, args = {}, {}
    for name, value in inputs.items():
        value = np.ascontiguousarray(value)
        arrays[f"in_{name}"] = value
        args[name] = nc.dram_tensor(f"in_{name}", value.shape, mybir.dt.from_np(value.dtype),
                                    kind="ExternalInput").ap()
    out = nc.dram_tensor("out", (1, T, D), F32, kind="ExternalOutput").ap()
    build(nc, out=out, **args)
    result = run_bass_kernel_spmd(nc, [arrays], core_ids=[0])
    return result.results[0]["out"]
```

```python
from contextlib import ExitStack

import numpy as np

import concourse.bass as bass
from concourse import mybir

F32 = mybir.dt.float32
F32R = mybir.dt.float32r
I32 = mybir.dt.int32
ALU = mybir.AluOpType
ACT = mybir.ActivationFunctionType
AX = mybir.AxisListType.X

P = 128
T = 512
NT = T // P
D = 1024
KD = D // P
HEADS, HD, VD = 8, 64, 128
HALF = 4
G4, GH, HP, NS = 4, 8, 64, 128
DI = 2048
NE, FE = 64, 256
TOPK, NG, PG = 8, 8, 8
EPS = 1e-6
LAMBDA_INIT = 0.2
ROUTED_SCALE = 2.5
OQ, OK, OV, OGA, OGB, OZ, OX = 0, 1024, 2048, 3072, 4096, 5120, 7168
OB = OX + DI
OC = OB + G4 * NS
ODT = OC + G4 * NS
UNIT = 2048
RAW, HL = 3, 3
FAR = 1 << 20
NEG = -1.0e30
TWO_PI = 2.0 * np.pi


def wait(eng, sem, value):
    if isinstance(value, int) and value <= 0:
        return
    eng.wait_ge(sem, value)


def line(eng, sem):
    n = [0]

    def run(ins):
        n[0] += 1
        ins.then_inc(sem, 1)
        eng.wait_ge(sem, n[0])
    run.count = n
    return run


class Map:

    def __init__(self, nc):
        self.nc = nc
        self.at = (nc.sbuf_base + 63) // 64 * 64
        self.end = nc.sbuf_usable_end

    def __call__(self, name, shape, dt=F32):
        size = int(np.prod(shape[1:])) * 4
        t = self.nc.alloc_sbuf_tensor_at(name, shape, dt, offset=self.at)
        self.at += (size + 31) // 32 * 32
        assert self.at <= self.end, (name, self.at, self.end)
        return t


def plan_steps(w):
    steps = []

    def cols(src, r0, nk, c0, n=512):
        return src[r0:r0 + nk * P, c0:c0 + n].rearrange("(k p) n -> p k n", p=P)

    def halves(src, c0):
        return [[(0, 512, 0, 4, cols(src, h * 512, 4, c0))] for h in range(2)]

    def add(kind, tag, units=(), nout=0, ks=4):
        steps.append(dict(kind=kind, tag=tag, units=list(units), nout=nout, ks=ks))

    for j in range(4):
        add("mod", j, halves(w["w_ada"], j * 512))
    add("h", 0)
    for hf in range(2):
        add("row", ("q", hf), halves(w["w_in"], OQ + hf * 512), 4)
        add("row", ("k", hf), halves(w["w_in"], OK + hf * 512), 4)
        add("row", ("v", hf), halves(w["w_in"], OV + hf * 512), 4)
        add("attn", hf)
        for b in range(2):
            add("branch", ("a", hf, b), [[(0, 512, 0, 4, cols(w["w_a"], hf * 512, 4, b * 512))]], 4)
    for b in range(2):
        add("col", ("ga", b), halves(w["w_in"], OGA + b * 512), 4)
    for g in range(G4):
        add("col", ("xs", g), halves(w["w_in"], OX + g * 512), 4)
        add("mod", 4 + 2 * g, halves(w["w_ada"], (4 + 2 * g) * 512))
        add("col", ("bc", g), [[(0, 128, 0, 8, cols(w["w_in"], 0, 8, OB + g * NS, NS)),
                               (128, 256, 0, 8, cols(w["w_in"], 0, 8, OC + g * NS, NS))]], 2, 8)
        add("mod", 5 + 2 * g, halves(w["w_ada"], (5 + 2 * g) * 512))
        add("row", ("z", g), halves(w["w_in"], OZ + g * 512), 4)
        add("ssd", g)
        for b in range(2):
            add("branch", ("b", g, b), [[(0, 512, 0, 4, cols(w["w_b"], g * 512, 4, b * 512))]], 4)
    for b in range(2):
        add("col", ("gb", b), halves(w["w_in"], OGB + b * 512), 4)
    add("merge", 0)
    for b in range(2):
        add("row", ("out", b), halves(w["w_out"], b * 512), 4)
    add("h2", 0)
    add("row", ("sgu", 0), [[(0, 256, 0, 4, cols(w["w_sg"], h * 512, 4, 0, 256)),
                            (256, 512, 0, 4, cols(w["w_su"], h * 512, 4, 0, 256))] for h in range(2)], 4)
    add("sact", 0)
    add("row", ("sdn", 0), [[(0, 1024, 0, 2, cols(w["w_sd"], 0, 2, 0, 1024))]], 8, 2)

    n = m = mods = outs = mids = 0
    for s in steps:
        s["out0"] = outs
        s["u"] = []
        for i, dmas in enumerate(s["units"]):
            u = dict(n=n, dmas=dmas)
            n += 1
            if s["kind"] == "mod":
                mods += 1
                u.update(mod=mods)
            else:
                u.update(m=m)
                m += 1
                if i == len(s["units"]) - 1:
                    u["freed"] = ("proj_done", outs + s["nout"])
                else:
                    mids += 1
                    u["freed"] = ("half_done", mids)
            s["u"].append(u)
        outs += s["nout"]
    return steps


def build(nc, x, c, positions, w_ada, b_ada, norm1_g, w_in, q_norm_g, k_norm_g, lambda_qk, subln_g,
          conv_w, conv_b, dt_bias, a_log, d_skip, ssd_norm_g, w_branch_a, w_branch_b, w_out,
          norm2_g, w_router, router_bias, w_exp_gate, w_exp_up, w_exp_down,
          w_sh_gate, w_sh_up, w_sh_down, out):
    w = dict(w_ada=w_ada[0], w_in=w_in[0], w_a=w_branch_a[0], w_b=w_branch_b[0], w_out=w_out[0],
             w_sg=w_sh_gate[0], w_su=w_sh_up[0], w_sd=w_sh_down[0])
    steps = plan_steps(w)
    units = [u for s in steps for u in s["u"]]
    splits = [u for u in units if "m" in u]
    landed, per = {}, [0] * RAW
    for u in units:
        per[u["n"] % RAW] += 16 * len(u["dmas"])
        landed[u["n"]] = per[u["n"] % RAW]

    def unit_view(buf, dma):
        c0, c1, k0, ks, src = dma
        width = UNIT // ks
        return buf.rearrange("p (k n) -> p k n", n=width)[:, :, c0:c1]

    dram = lambda n, s, dt=F32: nc.dram_tensor(n, s, dt, kind="Internal").ap()
    gated_a = dram("gated_a", (P, KD * T))
    h2_rows = dram("h2_rows", (T, D))
    y_rows = dram("y_rows", (T * TOPK, D))
    x2_dram = dram("x2_dram", (P, NT * D))
    g2_dram = dram("g2_dram", (P, D))
    slot_table = dram("slot_table", (P * NE * NT, 1), I32)

    sb = Map(nc)
    ident = sb("ident", [P, P])
    upper = sb("upper", [P, P])
    later = sb("later", [P, P])
    before = sb("before", [P, P])
    ones = sb("ones", [P, P])
    causal = sb("causal", [P, P])
    colp = sb("colp", [P, 113])
    convw = sb("convw", [P, 96])
    shT = sb("shT", [P, 16])
    a1T = sb("a1T", [P, KD])
    silc = sb("silc", [P, KD])
    stat = sb("stat", [P, 5, 32])
    modacc_at = sb.at
    modacc = sb("modacc", [P, T])
    tok_of = nc.alloc_sbuf_tensor_at("tok_of", [P, NE * NT], I32, offset=modacc_at)
    row_of = nc.alloc_sbuf_tensor_at("row_of", [P, NE * NT], I32, offset=modacc_at + NE * NT * 4)
    stage_at = sb.at
    stage = sb("stage", [P, 2, T])
    dtp = sb("dtp", [P, NT, 32])
    aa = sb("aa", [P, NT, 32])
    expo = sb("expo", [P, 3, NT, 32])
    dtdec = sb("dtdec", [P, NT, 32])
    dskip = sb("dskip", [P, 32])
    w8 = sb("w8", [P, NT, TOPK])
    cnt = sb("cnt", [P, 2, NE], I32)
    hT_at = sb.at
    hT = sb("hT", [P, KD, 2, T], F32R)
    rings = sb.at
    raw = sb("raw", [P, RAW, UNIT])
    hl = sb("hl", [P, HL, 2, UNIT], F32R)
    late = sb.at
    g1b = sb("g1b", [P, D])
    g2b = sb("g2b", [P, D])
    sh2b = sb("sh2b", [P, D])
    a2b = sb("a2b", [P, D])
    after_late = sb.at
    sb.at = late
    tabs = sb("tabs", [P, 2, 2, NT, HD])
    wT = sb("wT", [P, 2, NT, P])
    o_rows = sb("o_rows", [P, 2, NT, VD])
    o_sq = sb("o_sq", [P, VD])
    lamt = sb("lamt", [P, 4, HD])
    lam = sb("lam", [P, 8])
    sm = sb("sm", [P, 4, 8])
    gqk = sb("gqk", [P, 2, HD])
    assert sb.at <= after_late
    sb.at = after_late
    acc = sb("acc", [P, KD, T])
    work = sb.at
    x_rows = sb("x_rows", [P, NT, D])
    hsplit = sb("hsplit", [P, 2, T])
    pr1 = sb("pr1", [P, P])
    pr2 = sb("pr2", [P, P])
    wdt = sb("wdt", [P, KD, 32])
    wdt_hl = sb("wdt_hl", [P, KD, 2, 32], F32R)
    dtb = sb("dtb", [P, 2, 32])
    dwk = sb("dwk", [P, 6, NT * 32])
    trig = sb("trig", [P, 5, NT * 32])
    freq = sb("freq", [P, 32])
    posi = sb("posi", [P, NT], I32)
    posf = sb("posf", [P, NT])
    sb.at = work
    q_rows = sb("q_rows", [P, 2, NT, HALF * P])
    sb.at = work
    ya_hl = sb("ya_hl", [P, HALF, 2, T], F32R)
    v_rows = sb("v_rows", [P, NT, HALF * P])
    qkT = sb("qkT", [P, 2, HALF, T])
    probs = sb("probs", [P, 2, 2, T])
    wgt = sb("wgt", [P, 2, T])
    sb.at = work
    xbc = sb("xbc", [P, 6, T + 3])
    under = sb.at
    cv = sb("cv", [P, 6, T])
    b_rows = sb("b_rows", [P, NT, NS])
    cbm = sb("cbm", [P, NT, P])
    z_rows = sb("z_rows", [P, NT, 512])
    xs_rows = sb("xs_rows", [P, NT, 512])
    ua = sb("ua", [P, GH, P])
    lm = sb("lm", [P, 2, GH, P])
    xdt, state = cv[:, 0:2], cv[:, 2:4]
    sb.at = under
    yb_hl = sb("yb_hl", [P, 4, 2, T], F32R)
    sb.at = work
    ga_back = sb("ga_back", [P, KD, T])
    x2 = sb("x2", [P, NT, D])
    sb.at = work
    h2r = sb("h2r", [P, NT, D])
    sb.at = after_late
    wr = sb("wr", [P, KD, NE])
    wr_hl = sb("wr_hl", [P, KD, 2, NE], F32R)
    rt = sb("rt", [P, 6, NT, NE])
    assert sb.at <= work
    sb.at = work + 32768
    n2b = sb("n2b", [P, D])
    sb.at = work + 32768
    sgu = sb("sgu", [P, NT, T])
    sactT = sb("sactT", [P, 2, 2, T], F32R)
    rbias = sb("rbias", [P, NE])
    rk = sb("rk", [P, 3, 64])
    jlt = sb("jlt", [P, 8, 8])
    e4 = sb("e4", [P, NE])
    top = sb("top", [P, 16])
    grp = sb("grp", [P, NT, NG, 8])
    addr8 = sb("addr8", [P, NT, TOPK])
    addr8i = sb("addr8i", [P, NT, TOPK], I32)
    tokid = sb("tokid", [P, NT, TOPK], I32)
    eq8 = sb("eq8", [P, TOPK, NE])
    farow = sb("farow", [P, NE * NT], I32)
    sb.at = rings
    rawm = sb("rawm", [P, 6, UNIT])
    hlm = sb("hlm", [P, 6, 2, UNIT], F32R)
    yb = sb("yb", [P, 2, D])
    aT = sb("aT", [P, 2, 2, 2, P], F32R)
    sb.at = hT_at
    xT = sb("xT", [P, 2, KD, 2, P], F32R)
    xg = sb("xg", [P, 2, D])
    xo = sb("xo", [P, D])
    yo = sb("yo", [P, D])
    assert sb.at <= rings
    act = nc.alloc_sbuf_tensor_at("act", [P, 2, FE], F32, offset=stage_at)
    gix = nc.alloc_sbuf_tensor_at("gix", [P, 4], I32, offset=stage_at + 2048)
    oix = nc.alloc_sbuf_tensor_at("oix", [P, 2], I32, offset=stage_at + 2112)
    sb.at = rings
    ysum = sb("ysum", [P, TOPK // 2, 2, D])
    xfin = sb("xfin", [P, NT, D])
    g2f = sb("g2f", [P, D])
    ofin = sb("ofin", [P, 2, D])

    with ExitStack() as ctx:
        psum = ctx.enter_context(nc.psum_tensor("psum", [P, 8, 512], F32))
        S = {}

        def sem(*names):
            for n in names:
                S[n] = ctx.enter_context(nc.semaphore(n))
        sem("vec_line", "act_line", "pool_line", "consts", "params", "params_act", "row_ev", "x_in", "half_done", "proj_done",
            "proj_free", "hi_done", "lo_done", "mod_used", "mod_ps", "mod_ev", "par_T", "par_ev",
            "silu_c", "xr_ready", "xT_ps", "h_tmp", "h_hi", "h_lo", "wdt_hi", "wdt_lo", "dt_ps", "dtT_ps", "dtT_ev", "lgT_ps", "lgT_ev",
            "dt_exp", "dt_dve", "dt_a", "cum_ps", "cum_exp", "trig_in", "trig_out", "sq_done")
        sem(*[f"raw_in{i}" for i in range(RAW)])
        sem("qk_ready", "qkT_ps", "qkT_ev", "sc_ps", "nmax", "p_exp", "w_ready", "wT_ps", "wT_ev", "o_ps", "o_ev",
            "o_ready", "yT_ps", "yT_hi", "yT_lo", "stage_used")
        sem("conv_done", "conv_silu", "tr_ps", "tr_ev", "b_ev", "cb_ps", "ua_ready", "seg_ps", "u_ps", "yl_ps",
            "seg_exp", "m_ready", "xd_ready", "ys_ps", "st_ready", "y_ready", "yn_ready", "skipped",
            "g_in", "spilled", "ga_in", "x2_in", "merged", "m_hi", "m_lo")
        sem("x2_ready", "h2_row", "h2T_ps", "h2T_hi", "h2T_lo", "h2_out", "wr_in", "wr_hi", "wr_lo", "lg_ps", "lg_ev",
            "sel_ready", "pos_ps", "addr_ready", "table_far", "table_set", "table_in", "tok_ready",
            "sa_ready", "sT_ps", "sT_hi", "sT_lo", "x2_out", "cnt_ready", "rp_in", "jlt_ready")
        sem(*[f"m_raw{i}" for i in range(6)])
        sem("m_hi2", "m_lo2", "m_x0", "m_x1", "m_y0", "m_y1", "xt_ps", "xt_hi", "xt_lo", "gu_ps", "gu_silu", "act_ready",
            "at_ps", "at_hi", "at_lo", "dn_ps", "y_ev", "m_idx", "held")
        sem(*[f"more_{n}" for n in ("x", "t", "xh", "xl", "g", "sg", "act", "t2", "t2h", "t2l", "d", "y", "s", "idx")])
        sem("fin_x", *[f"fin_y{k}" for k in range(4)], "fin_used", "fin_out", "out_done0", "out_done1")
        blk = ctx.enter_context(nc.Block())
        bank = lambda b: psum[:, b]
        ring_rule = {}

        def free_split(eng, m):
            if m >= HL:
                name, value = splits[m - HL]["freed"]
                eng.wait_ge(S[name], value)

        def raw_wait(eng, u):
            eng.wait_ge(S[f"raw_in{u['n'] % RAW}"], landed[u["n"]])

        def ahead(i):
            if i not in ring_rule:
                done = 0
                for j in range(-1, len(steps)):
                    k = j + 1
                    while k < len(steps) and not (steps[k]["u"] and steps[k]["kind"] != "mod"):
                        k += 1
                    stop = steps[k]["u"][-1]["n"] + 1 if k < len(steps) else len(units)
                    ring_rule[j] = units[done:max(stop, done)]
                    done = max(stop, done)
            return ring_rule[i]

        out_index = {s["tag"]: s["out0"] for s in steps if s["nout"]}

        flat = lambda ap: ap.rearrange("p a b -> p (a b)")
        USED = sum(s["nout"] for s in steps if s["tag"] and isinstance(s["tag"], tuple) and (
            s["tag"][0] in ("out", "sdn", "ga", "gb") or (s["kind"] == "branch" and s["tag"][1] > 0)))
        OUTS = sum(s["nout"] for s in steps)
        x2_at = USED - 2 * NT - NT

        def route(v, L):
            V = nc.vector
            TS, TT, STT = V.tensor_scalar, V.tensor_tensor, V.scalar_tensor_tensor
            v.wait_ge(S["lg_ev"], 1)
            v.wait_ge(S["rp_in"], 16)
            over_t = lambda ap: ap.unsqueeze(1).to_broadcast([P, NT, NE])
            L(TT(rt[:, 1], rt[:, 0], over_t(rbias[:]), ALU.add))
            for t in range(NT):
                for g in range(NG):
                    ins = V.max(grp[:, t, g, :], rt[:, 1, t, g * PG:(g + 1) * PG])
            L(ins)
            gs = addr8
            L(TT(gs[:], grp[:, :, :, 0], grp[:, :, :, 1], ALU.add))
            v.wait_ge(S["jlt_ready"], 1)
            sq = lambda n: rk[:, n].rearrange("p (g j) -> p g j", j=8)
            for t in range(NT):
                as_j = gs[:, t, :].unsqueeze(1).to_broadcast([P, 8, 8])
                as_g = gs[:, t, :].unsqueeze(2).to_broadcast([P, 8, 8])
                L(TT(sq(0), as_j, as_g, ALU.is_gt))
                L(TT(sq(1), as_j, as_g, ALU.is_equal))
                L(TT(sq(1), sq(1), jlt[:], ALU.mult))
                L(TT(sq(0), sq(0), sq(1), ALU.add))
                L(V.tensor_reduce(top[:, 0:8], sq(0), AX, ALU.add))
                L(TS(top[:, 0:8], top[:, 0:8], 4.0, None, ALU.is_lt))
                L(TS(top[:, 8:16], top[:, 0:8], -NEG, NEG, ALU.mult, ALU.add))
                m = rt[:, 1, t, :]
                by_g = lambda ap: ap.rearrange("p (g e) -> p g e", e=PG)
                L(TT(by_g(m), by_g(m), top[:, 0:8].unsqueeze(2).to_broadcast([P, 8, 8]), ALU.mult))
                L(TT(by_g(m), by_g(m), top[:, 8:16].unsqueeze(2).to_broadcast([P, 8, 8]), ALU.add))
                L(V.max(top[:, 0:8], m))
                L(V.match_replace(rt[:, 2, t, :], top[:, 0:8], m, -3.0e38))
                TS(rt[:, 3, t, :], rt[:, 2, t, :], -2.0e30, None, ALU.is_lt).then_inc(S["sel_ready"], 1)
            v.wait_ge(S["sel_ready"], NT)
            L(TT(rt[:, 5], rt[:, 0], rt[:, 3], ALU.mult))
            L(V.tensor_reduce(top[:, 0:NT], rt[:, 5], AX, ALU.add))
            L(V.reciprocal(top[:, 0:NT], top[:, 0:NT]))
            L(TS(top[:, 0:NT], top[:, 0:NT], ROUTED_SCALE, None, ALU.mult))
            L(TT(rt[:, 5], rt[:, 5], top[:, 0:NT].unsqueeze(2).to_broadcast([P, NT, NE]), ALU.mult))

        def slots(v, L):
            V = nc.vector
            TS, TT, STT = V.tensor_scalar, V.tensor_tensor, V.scalar_tensor_tensor
            v.wait_ge(S["pos_ps"], 1)
            pos, j_ = flat(rt[:, 4]), flat(rt[:, 1])
            L(V.tensor_copy(pos, psum[:, 7, 0:NT * NE]))
            L(V.tensor_copy(rk[:, 2], psum[:, 7, NT * NE:(NT + 1) * NE]))
            L(TS(j_, pos, 128.0, None, ALU.is_ge))
            L(STT(out=j_, in0=pos, scalar=256.0, in1=j_, op0=ALU.is_ge, op1=ALU.add))
            L(STT(out=j_, in0=pos, scalar=384.0, in1=j_, op0=ALU.is_ge, op1=ALU.add))
            L(TS(pos, pos, 256.0, 1.0, ALU.mult, ALU.add))
            L(TT(rt[:, 4], rt[:, 4], e4[:].unsqueeze(1).to_broadcast([P, NT, NE]), ALU.add))
            L(STT(out=pos, in0=j_, scalar=-32767.0, in1=pos, op0=ALU.mult, op1=ALU.add))
            L(TT(pos, pos, flat(rt[:, 3]), ALU.mult))
            L(TS(pos, pos, 1.0, None, ALU.subtract))
            for t in range(NT):
                L(V.max(addr8[:, t, :], rt[:, 4, t, :]))
            V.tensor_copy(addr8i[:], addr8[:]).then_inc(S["addr_ready"], 1)

        def gates_and_counts(v, L):
            V = nc.vector
            TS, TT = V.tensor_scalar, V.tensor_tensor
            for t in range(NT):
                over_k = lambda ap: ap.unsqueeze(1).to_broadcast([P, TOPK, NE])
                L(TT(eq8[:], over_k(rt[:, 4, t, :]), addr8[:, t, :].unsqueeze(2).to_broadcast([P, TOPK, NE]),
                     ALU.is_equal))
                L(TT(eq8[:], eq8[:], over_k(rt[:, 5, t, :]), ALU.mult))
                L(V.tensor_reduce(w8[:, t, :], eq8[:], AX, ALU.add))
            L(V.tensor_copy(cnt[:, 0, :], rk[:, 2]))
            own = eq8[:, 0]
            L(TS(own, rk[:, 2], P + 0.5, None, ALU.is_gt))
            L(TS(eq8[:, 1], rk[:, 2], 2 * P + 0.5, 2.0, ALU.is_gt, ALU.mult))
            L(TT(own, own, eq8[:, 1], ALU.add))
            L(V.tensor_copy(eq8[:, 1], own))
            at = 1
            for step in (1, 2, 4, 8, 16, 32):
                nxt = 3 - at
                V.tensor_copy(eq8[:, nxt, 0:step], eq8[:, at, 0:step])
                L(TT(eq8[:, nxt, step:], eq8[:, at, step:], eq8[:, at, 0:NE - step], ALU.add))
                at = nxt
            L(TT(eq8[:, at], eq8[:, at], own, ALU.subtract))
            V.tensor_copy(cnt[:, 1, :], eq8[:, at]).then_inc(S["cnt_ready"], 1)

        def pool_route(pool, L):
            pool.wait_ge(S["h2_row"], 1)
            for t in range(NT):
                pool.dma_start(h2_rows[t * P:(t + 1) * P, :], h2r[:, t, :]).then_inc(S["h2_out"], 16)
            pool.wait_ge(S["table_far"], 16)
            pool.wait_ge(S["addr_ready"], 1)
            for t in range(NT):
                for k in range(TOPK):
                    pool.indirect_dma_start(slot_table, bass.IndirectOffsetOnAxis(ap=addr8i[:, t, k:k + 1], axis=0),
                                            tokid[:, t, k:k + 1], None).then_inc(S["table_set"], 16)
            pool.wait_ge(S["proj_done"], OUTS)
            L(nc.gpsimd.memset(xg[:], 0.0))
            L(nc.gpsimd.memset(xo[:], 0.0))
            pool.wait_ge(S["table_set"], 16 * NT * TOPK)
            pool.dma_start(row_of[:], slot_table.rearrange("(p n) o -> p (n o)", p=P)).then_inc(S["table_in"], 16)

        PAIRS = NE // 2

        def hold(eng, sem, value):
            eng.wait_ge(sem, value).then_inc(S["held"], 1)

        def read_counts(eng, e):
            return [eng.value_load(cnt[0:1, q, bass.ds(e, 1)], min_val=0, max_val=T) for q in range(2)]

        def extra(eng, e, body):
            count, n = read_counts(eng, e)
            with eng.If(count > P):
                body(1, n)
            with eng.If(count > 2 * P):
                for j in (2, 3):
                    body(j, n + (j - 1))

        def iterations(eng, it, last):
            for e in range(3):
                it(e, e % 2)
            with eng.Fori(0, PAIRS - 2) as i:
                it(i * 2 + 3, 1)
                it(i * 2 + 4, 0)
            for e in range(NE - 1, last):
                it(e, e % 2)

        def sp_moe(sp):
            gate = w_exp_gate[0].rearrange("e (k p) n -> e p k n", p=P)
            up = w_exp_up[0].rearrange("e (k p) n -> e p k n", p=P)
            down = w_exp_down[0].rearrange("e (k p) n -> e p k n", p=P)
            sp.wait_ge(S["proj_done"], OUTS)

            def load(e, par, first=False):
                at = bass.ds(e, 1)
                for u in range(3):
                    slot = 3 * par + u
                    if not first:
                        sp.wait_ge(S["m_lo2"], e * 3 + (u - 5))
                    buf = rawm[:, slot]
                    if u < 2:
                        b_ = buf.rearrange("p (k n) -> p k n", n=512)
                        for half, src in enumerate((gate, up)):
                            sp.dma_start(b_[:, :, half * FE:(half + 1) * FE],
                                         src[at, :, u * 4:u * 4 + 4, :].rearrange("o p k n -> (o p) k n")).then_inc(
                                S[f"m_raw{slot}"], 16)
                    else:
                        sp.dma_start(buf.rearrange("p (k n) -> p k n", n=D),
                                     down[at].rearrange("o p k n -> (o p) k n")).then_inc(S[f"m_raw{slot}"], 16)
            load(0, 0, True)
            sp.wait_ge(S["stage_used"], USED)
            sp.dma_start(x2_dram, flat(x2[:])).then_inc(S["x2_out"], 16)
            sp.dma_start(g2_dram, g2b[:]).then_inc(S["x2_out"], 16)
            sp.wait_ge(S["m_x0"], 16)
            sp.wait_ge(S["x2_out"], 32)
            load(1, 1, True)
            with sp.Fori(1, PAIRS) as i:
                load(i * 2, 0)
                load(i * 2 + 1, 1)
            for t in range(NT):
                sp.wait_ge(S["fin_out"], t + 1)
                sp.dma_start(out[0, t * P:(t + 1) * P, :], ofin[:, t % 2, :]).then_inc(S[f"out_done{t % 2}"], 16)
            sp.wait_ge(S["out_done0"], 16 * NT // 2)
            sp.wait_ge(S["out_done1"], 16 * NT // 2)

        def pool_moe(pool, L):
            pool.wait_ge(S["tok_ready"], 1)
            pool.wait_ge(S["x2_out"], 32)
            pool.wait_ge(S["h2_out"], 16 * NT)
            pool.wait_ge(S["cnt_ready"], 1)

            def gather(e, par, copies):
                nc.gpsimd.tensor_copy(gix[:, par:par + 1], tok_of[:, bass.ds(e * NT, 1)]).then_inc(S["m_idx"], 1)
                hold(pool, S["m_idx"], copies)
                pool.indirect_dma_start(xg[:, par, :], None, h2_rows,
                                        bass.IndirectOffsetOnAxis(ap=gix[:, par:par + 1], axis=0),
                                        bounds_check=T - 1, oob_is_err=False).then_inc(S[f"m_x{par}"], 16)

            def scatter(e, par, copies):
                nc.gpsimd.tensor_copy(gix[:, 2 + par:3 + par], row_of[:, bass.ds(e * NT, 1)]).then_inc(S["m_idx"], 1)
                hold(pool, S["m_idx"], copies)
                pool.indirect_dma_start(y_rows, bass.IndirectOffsetOnAxis(ap=gix[:, 2 + par:3 + par], axis=0),
                                        yb[:, par, :], None, bounds_check=T * TOPK - 1,
                                        oob_is_err=False).then_inc(S[f"m_y{par}"], 16)

            def more_rows(e, j, x_):
                nc.gpsimd.tensor_copy(oix[:, 0:1], tok_of[:, bass.ds(e * NT + j, 1)]).then_inc(S["more_idx"], 1)
                hold(pool, S["more_idx"], x_ * 2 + 1)
                pool.indirect_dma_start(xo[:], None, h2_rows, bass.IndirectOffsetOnAxis(ap=oix[:, 0:1], axis=0),
                                        bounds_check=T - 1, oob_is_err=False).then_inc(S["more_x"], 16)

            def more_ahead(e):
                count, n = read_counts(pool, e)
                with pool.If(count > P):
                    more_rows(e, 1, n)

            def more(e):
                def body(j, x_):
                    o = lambda n: S[f"more_{n}"]
                    if j > 1:
                        more_rows(e, j, x_)
                    nc.gpsimd.tensor_copy(oix[:, 1:2], row_of[:, bass.ds(e * NT + j, 1)]).then_inc(o("idx"), 1)
                    hold(pool, o("idx"), x_ * 2 + 2)
                    hold(pool, o("y"), x_ + 1)
                    pool.indirect_dma_start(y_rows, bass.IndirectOffsetOnAxis(ap=oix[:, 1:2], axis=0), yo[:], None,
                                            bounds_check=T * TOPK - 1, oob_is_err=False).then_inc(o("s"), 16)
                    hold(pool, o("s"), x_ * 16 + 16)
                extra(pool, e, body)

            def step(e, par, copies, last=False):
                if not isinstance(e, int) or e < NE:
                    more_ahead(e)
                if not isinstance(e, int) or e > 0:
                    hold(pool, S["y_ev"], e)
                    scatter(e - 1, 1 - par, copies + 1)
                    copies = copies + 1
                if not last:
                    hold(pool, S["xt_ps"], e + 1)
                    gather(e + 2, par, copies + 1)
                if not isinstance(e, int) or e < NE:
                    more(e)
            gather(0, 0, 1)
            gather(1, 1, 2)
            step(0, 0, 2)
            with pool.Fori(0, (NE - 4) // 2) as i:
                step(i * 2 + 1, 1, i * 4 + 3)
                step(i * 2 + 2, 0, i * 4 + 5)
            step(NE - 3, 1, 2 * NE - 5)
            step(NE - 2, 0, 2 * NE - 3, last=True)
            step(NE - 1, 1, 2 * NE - 2, last=True)
            step(NE, 0, 2 * NE - 1, last=True)
            fin_pool(pool)

        def pe_moe(pe, M, tr, three):
            xt_dst = lambda k: psum[:, k // 4, (k % 4) * P:(k % 4 + 1) * P]

            def to_T(src):
                for k in range(KD):
                    ins = tr(xt_dst(k), src[:, k * P:(k + 1) * P], ident[:])
                return ins

            def gate_up(par):
                for k in range(KD):
                    wv = lambda q: hlm[:, 3 * par + k // 4, q, :].rearrange("p (k n) -> p k n", n=512)[:, k % 4, :]
                    ins = three(bank(2 + par), lambda q: xT[:, par, k, q, :], wv, k == 0, k == KD - 1)
                return ins

            def act_to_T(src):
                for k in range(2):
                    ins = tr(psum[:, 4, k * P:(k + 1) * P], src[:, k * P:(k + 1) * P], ident[:])
                return ins

            def down_(par):
                wv = lambda q: hlm[:, 3 * par + 2, q, :].rearrange("p (k n) -> p k n", n=D)
                for half in range(2):
                    for k in range(2):
                        ins = three(bank(5 + half), lambda q: aT[:, par, k, q, :],
                                    lambda q: wv(q)[:, k, half * 512:(half + 1) * 512], k == 0, k == 1)
                return ins

            pe.wait_ge(S["cnt_ready"], 1)
            pe.wait_ge(S["stage_used"], USED)
            pe.wait_ge(S["m_x0"], 16)
            to_T(xg[:, 0, :]).then_inc(S["xt_ps"], 1)

            def it(e, par):
                whole = not isinstance(e, int) or e < NE
                if not isinstance(e, int) or e > 0:
                    pe.wait_ge(S["act_ready"], e)
                    wait(pe, S["at_lo"], e - 1)
                    act_to_T(act[:, 1 - par, :]).then_inc(S["at_ps"], 1)
                if whole:
                    pe.wait_ge(S["m_lo2"], e * 3 + 2)
                    pe.wait_ge(S["xt_lo"], e + 1)
                    wait(pe, S["act_ready"], e - 1)
                    gate_up(par).then_inc(S["gu_ps"], 1)
                if not isinstance(e, int) or e + 1 < NE:
                    pe.wait_ge(S[f"m_x{1 - par}"], (e + 1 - (1 - par)) * 8 + 16)
                    pe.wait_ge(S["xt_lo"], e + 1)
                    to_T(xg[:, 1 - par, :]).then_inc(S["xt_ps"], 1)
                if not isinstance(e, int) or e > 0:
                    pe.wait_ge(S["at_lo"], e)
                    pe.wait_ge(S["m_lo2"], e * 3)
                    wait(pe, S["y_ev"], e - 1)
                    down_(1 - par).then_inc(S["dn_ps"], 1)
                if whole:
                    def body(j, x_):
                        o = lambda n: S[f"more_{n}"]
                        pe.wait_ge(S["act_ready"], e + 1)
                        pe.wait_ge(S["m_lo2"], e * 3 + 3)
                        if not isinstance(e, int) or e > 0:
                            pe.wait_ge(S["y_ev"], e)
                        if not isinstance(e, int) or e + 1 < NE:
                            pe.wait_ge(S["xt_lo"], e + 2)
                        pe.wait_ge(o("x"), x_ * 16 + 16)
                        to_T(xo[:]).then_inc(o("t"), 1)
                        pe.wait_ge(o("xl"), x_ + 1)
                        gate_up(par).then_inc(o("g"), 1)
                        pe.wait_ge(o("act"), x_ + 1)
                        act_to_T(xo[:, 0:FE]).then_inc(o("t2"), 1)
                        pe.wait_ge(o("t2l"), x_ + 1)
                        down_(par).then_inc(o("d"), 1)
                        pe.wait_ge(o("y"), x_ + 1)
                    extra(pe, e, body)
            iterations(pe, it, NE + 1)

        def act_moe(a, A, L):
            a.wait_ge(S["x2_out"], 32)
            a.wait_ge(S["h2_out"], 16 * NT)
            a.wait_ge(S["cnt_ready"], 1)

            def split(e, par, us):
                for u in us:
                    slot = 3 * par + u
                    a.wait_ge(S[f"m_raw{slot}"], (e - par) * (16 if u < 2 else 8) + (32 if u < 2 else 16))
                    A(hlm[:, slot, 0, :], rawm[:, slot], ACT.Copy).then_inc(S["m_hi2"], 1)

            def x_hi(par):
                return A(xT[:, par, :, 0, :], psum[:, 0:2].rearrange("p b (k t) -> p (b k) t", t=P), ACT.Copy)

            def a_hi(par):
                return A(aT[:, par, :, 0, :], psum[:, 4, 0:2 * P].rearrange("p (k t) -> p k t", t=P), ACT.Copy)

            split(0, 0, range(3))
            a.wait_ge(S["tok_ready"], 1)
            a.wait_ge(S["xt_ps"], 1)
            x_hi(0).then_inc(S["xt_hi"], 1)

            def it(e, par):
                whole = not isinstance(e, int) or e < NE
                more_ = not isinstance(e, int) or e + 1 < NE
                prev = not isinstance(e, int) or e > 0
                if prev:
                    a.wait_ge(S["at_ps"], e)
                    wait(a, S["dn_ps"], e - 2)
                    a_hi(1 - par).then_inc(S["at_hi"], 1)
                    a.wait_ge(S["gu_ps"], e)
                if more_:
                    split(e + 1, 1 - par, range(2))
                if whole:
                    a.wait_ge(S["gu_ps"], e + 1)
                    wait(a, S["at_ps"], e - 1)
                    A(act[:, par, :], psum[:, 2 + par, 0:FE], ACT.Silu).then_inc(S["gu_silu"], 1)
                if more_:
                    a.wait_ge(S["xt_ps"], e + 2)
                    x_hi(1 - par).then_inc(S["xt_hi"], 1)
                if prev:
                    a.wait_ge(S["dn_ps"], e)
                    if not isinstance(e, int) or e > 2:
                        a.wait_ge(S[f"m_y{1 - par}"], (e - 1 - (1 - par)) * 8)
                    A(yb[:, 1 - par, :], psum[:, 5:7].rearrange("p b n -> p (b n)"), ACT.Copy).then_inc(S["y_ev"], 1)
                if more_:
                    split(e + 1, 1 - par, [2])
                if whole:
                    def body(j, x_):
                        o = lambda n: S[f"more_{n}"]
                        a.wait_ge(o("t"), x_ + 1)
                        x_hi(par).then_inc(o("xh"), 1)
                        a.wait_ge(o("g"), x_ + 1)
                        A(xo[:, 0:FE], psum[:, 2 + par, 0:FE], ACT.Silu).then_inc(o("sg"), 1)
                        a.wait_ge(o("t2"), x_ + 1)
                        a_hi(par).then_inc(o("t2h"), 1)
                        a.wait_ge(o("d"), x_ + 1)
                        A(yo[:], psum[:, 5:7].rearrange("p b n -> p (b n)"), ACT.Copy).then_inc(o("y"), 1)
                    extra(a, e, body)
            iterations(a, it, NE + 1)
            fin_act(a)

        def vec_moe(v, L):
            V = nc.vector
            TT = V.tensor_tensor
            v.wait_ge(S["table_in"], 16)
            V.tensor_single_scalar(tok_of[:], row_of[:], 3, ALU.arith_shift_right).then_inc(S["tok_ready"], 1)
            v.wait_ge(S["cnt_ready"], 1)

            def split(par, e, us):
                for u in us:
                    slot = 3 * par + u
                    v.wait_ge(S["m_hi2"], e * 3 + (u + 1))
                    TT(hlm[:, slot, 1, :], rawm[:, slot], hlm[:, slot, 0, :].bitcast(F32), ALU.subtract).then_inc(
                        S["m_lo2"], 1)

            def x_lo(par):
                return TT(xT[:, par, :, 1, :], psum[:, 0:2].rearrange("p b (k t) -> p (b k) t", t=P),
                          xT[:, par, :, 0, :].bitcast(F32), ALU.subtract)

            def a_lo(par):
                return TT(aT[:, par, :, 1, :], psum[:, 4, 0:2 * P].rearrange("p (k t) -> p k t", t=P),
                          aT[:, par, :, 0, :].bitcast(F32), ALU.subtract)

            split(0, 0, range(3))
            v.wait_ge(S["xt_hi"], 1)
            x_lo(0).then_inc(S["xt_lo"], 1)

            def it(e, par):
                whole = not isinstance(e, int) or e < NE
                more_ = not isinstance(e, int) or e + 1 < NE
                prev = not isinstance(e, int) or e > 0
                if prev:
                    v.wait_ge(S["at_hi"], e)
                    a_lo(1 - par).then_inc(S["at_lo"], 1)
                if more_:
                    split(1 - par, e + 1, range(2))
                if whole:
                    v.wait_ge(S["gu_silu"], e + 1)
                    TT(act[:, par, :], act[:, par, :], psum[:, 2 + par, FE:], ALU.mult).then_inc(S["act_ready"], 1)
                if more_:
                    v.wait_ge(S["xt_hi"], e + 2)
                    x_lo(1 - par).then_inc(S["xt_lo"], 1)
                    split(1 - par, e + 1, [2])
                if whole:
                    def body(j, x_):
                        o = lambda n: S[f"more_{n}"]
                        v.wait_ge(o("xh"), x_ + 1)
                        x_lo(par).then_inc(o("xl"), 1)
                        v.wait_ge(o("sg"), x_ + 1)
                        TT(xo[:, 0:FE], xo[:, 0:FE], psum[:, 2 + par, FE:], ALU.mult).then_inc(o("act"), 1)
                        v.wait_ge(o("t2h"), x_ + 1)
                        a_lo(par).then_inc(o("t2l"), 1)
                    extra(v, e, body)
            iterations(v, it, NE + 1)
            fin_vec(v)

        def fin_pool(pool):
            pool.wait_ge(S["m_y0"], 16 * NE // 2)
            pool.wait_ge(S["m_y1"], 16 * NE // 2)

        def fin_act(a):
            a.wait_ge(S["dn_ps"], NE)
            a.dma_start(g2f[:], g2_dram).then_inc(S["fin_x"], 16)
            a.wait_ge(S["m_y0"], 16 * NE // 2)
            a.wait_ge(S["m_y1"], 16 * NE // 2)
            ys = y_rows.rearrange("(t p k) d -> t p k d", p=P, k=TOPK)
            for t in range(NT):
                for pair in range(TOPK // 2):
                    wait(a, S["fin_used"], (t - 1) * (TOPK + 1) + 2 * pair + 2)
                    a.dma_start(ysum[:, pair], ys[t, :, 2 * pair:2 * pair + 2, :]).then_inc(S[f"fin_y{pair}"], 16)
                wait(a, S["fin_used"], t * (TOPK + 1))
                a.dma_start(xfin[:, t, :], x2_dram[:, t * D:(t + 1) * D]).then_inc(S["fin_x"], 16)

        def fin_vec(v):
            V = nc.vector
            for t in range(NT):
                o_ = ofin[:, t % 2, :]
                if t >= 2:
                    v.wait_ge(S[f"out_done{t % 2}"], 16 * (t // 2))
                for k in range(TOPK):
                    v.wait_ge(S[f"fin_y{k // 2}"], 16 * (t + 1))
                    if k == 0:
                        ins = V.tensor_scalar(o_, ysum[:, k // 2, k % 2, :], w8[:, t, k:k + 1], None, ALU.mult)
                    else:
                        ins = V.scalar_tensor_tensor(out=o_, in0=ysum[:, k // 2, k % 2, :], scalar=w8[:, t, k:k + 1], in1=o_,
                                                     op0=ALU.mult, op1=ALU.add)
                    ins.then_inc(S["fin_used"], 1)
                    v.wait_ge(S["fin_used"], t * (TOPK + 1) + k + 1)
                v.wait_ge(S["fin_x"], 16 * (t + 2))
                V.tensor_tensor(o_, o_, g2f[:], ALU.mult).then_inc(S["fin_used"], 1)
                v.wait_ge(S["fin_used"], (t + 1) * (TOPK + 1))
                V.tensor_tensor(o_, o_, xfin[:, t, :], ALU.add).then_inc(S["fin_out"], 1)

        @blk.sync
        def _(sp):
            for t in range(NT):
                sp.dma_start(x_rows[:, t, :], x[0, t * P:(t + 1) * P, :]).then_inc(S["x_in"], 16)
            for u in units:
                if u["n"] >= RAW:
                    old = units[u["n"] - RAW]
                    if "m" in old:
                        sp.wait_ge(S["lo_done"], old["m"] + 1)
                    else:
                        sp.wait_ge(S["mod_used"], old["mod"])
                for dma in u["dmas"]:
                    sp.dma_start(unit_view(raw[:, u["n"] % RAW], dma), dma[4]).then_inc(
                        S[f"raw_in{u['n'] % RAW}"], 16)
            sp_moe(sp)

        @blk.gpsimd
        def _(pool):
            L = line(pool, S["pool_line"])
            for dst, rows, src in (
                    (pr1, 0, b_ada[0].rearrange("(r p) -> r p", p=P)),
                    (pr1, 48, norm1_g[0].rearrange("(r p) -> r p", p=P)),
                    (pr1, 56, norm2_g[0].rearrange("(r p) -> r p", p=P)),
                    (pr1, 64, c[0].rearrange("(r p) -> r p", p=P)),
                    (pr1, 72, conv_b[0].rearrange("(r p) -> r p", p=P)),
                    (pr1, 96, subln_g[0].rearrange("(r p) -> r p", p=P)),
                    (pr1, 97, ssd_norm_g[0].rearrange("(r p) -> r p", p=P)),
                    (pr2, 0, conv_w[0].rearrange("k (r p) -> (k r) p", p=P))):
                pool.dma_start(dst[rows:rows + src.shape[0], :], src).then_inc(S["params"], 16)
            pool.dma_start(posi[:], positions.rearrange("o (t p) -> p (o t)", p=P),
                           allow_slow_non_contiguous=True).then_inc(S["params"], 16)
            L(nc.gpsimd.memset(ones[:], 1.0))
            L(nc.gpsimd.memset(ident[:], 0.0))
            L(nc.gpsimd.memset(causal[:], 0.0))
            sel = nc.gpsimd.affine_select
            L(sel(out=ident[:], in_=ident[:], compare_op=ALU.not_equal, fill=1.0, base=0, pattern=[[-1, P]],
                  channel_multiplier=1))
            L(sel(out=upper[:], in_=ones[:], compare_op=ALU.is_ge, fill=0.0, base=0, pattern=[[1, P]],
                  channel_multiplier=-1))
            L(sel(out=before[:], in_=ones[:], compare_op=ALU.is_gt, fill=0.0, base=0, pattern=[[1, P]],
                  channel_multiplier=-1))
            L(sel(out=later[:], in_=ones[:], compare_op=ALU.is_gt, fill=0.0, base=0, pattern=[[-1, P]],
                  channel_multiplier=1))
            L(sel(out=causal[:], in_=causal[:], compare_op=ALU.is_ge, fill=NEG, base=0, pattern=[[-1, P]],
                  channel_multiplier=1))
            for i in range(32):
                ins = nc.gpsimd.memset(freq[:, i:i + 1], float(np.float32(10000.0) ** np.float32(-2.0 * i / HD)))
            ins.then_inc(S["consts"], 1)
            for s in steps:
                kind_ = s["kind"]
                if kind_ == "ssd":
                    g = s["tag"]
                    for ch in range(NT + 1):
                        if ch < NT:
                            wait(pool, S["seg_ps"], 4 * g + ch)
                            if g == 0 and ch == 0:
                                pool.wait_ge(S["dt_a"], 1)
                                pool.wait_ge(S["params_act"], 16 * 7)
                            nc.gpsimd.tensor_tensor(
                                ua[:], upper[:].unsqueeze(1).to_broadcast([P, GH, P]),
                                aa[:, ch, g * GH:(g + 1) * GH].unsqueeze(2).to_broadcast([P, GH, P]),
                                ALU.mult).then_inc(S["ua_ready"], 1)
                        if ch:
                            pool.wait_ge(S["xd_ready"], 4 * g + ch)
                            rows = xs_rows[:, ch - 1, :].rearrange("p (h d) -> p h d", d=HP)
                            nc.gpsimd.tensor_tensor(
                                rows, rows, dskip[:, g * GH:(g + 1) * GH].unsqueeze(2).to_broadcast([P, GH, HP]),
                                ALU.mult).then_inc(S["skipped"], 1)
                if s["kind"] == "branch" and s["tag"] == ("a", 1, 1):
                    pool.wait_ge(S["yT_lo"], HEADS)
                    for dst, j in ((g1b, 2), (sh2b, 3), (a2b, 4), (g2b, 5)):
                        pool.dma_start(dst[:], b_ada[0:1, j * D:(j + 1) * D].to_broadcast([P, D])).then_inc(
                            S["g_in"], 16)
                if s["kind"] == "col" and s["tag"] == ("ga", 1):
                    pool.wait_ge(S["stage_used"], 16)
                    pool.dma_start(gated_a, acc[:].rearrange("p k t -> p (k t)")).then_inc(S["spilled"], 16)
                if s["kind"] == "merge":
                    pool.wait_ge(S["proj_done"], out_index[("b", G4 - 1, 1)] + 4)
                    pool.wait_ge(S["spilled"], 16)
                    pool.dma_start(n2b[:], norm2_g.to_broadcast([P, D])).then_inc(S["ga_in"], 16)
                    pool.dma_start(ga_back[:].rearrange("p k t -> p (k t)"), gated_a).then_inc(S["ga_in"], 16)
                    for t in range(NT):
                        pool.dma_start(x2[:, t, :], x[0, t * P:(t + 1) * P, :]).then_inc(S["x2_in"], 16)
                    pool.dma_start(rbias[:], router_bias.to_broadcast([P, NE])).then_inc(S["rp_in"], 16)
                    L(nc.gpsimd.iota(farow[:, 0:NE], pattern=[[4, NE]], base=0, channel_multiplier=0))
                    L(nc.gpsimd.tensor_copy(e4[:], farow[:, 0:NE]))
                    L(nc.gpsimd.iota(tokid[:], pattern=[[P * TOPK, NT], [1, TOPK]], base=0, channel_multiplier=TOPK))
                    L(nc.gpsimd.memset(farow[:], FAR))
                    pool.dma_start(slot_table.rearrange("(p n) o -> p (n o)", p=P), farow[:]).then_inc(
                        S["table_far"], 16)
                    L(nc.gpsimd.memset(jlt[:], 1.0))
                    nc.gpsimd.affine_select(out=jlt[:], in_=jlt[:], compare_op=ALU.is_gt, fill=0.0, base=0,
                                            pattern=[[1, 8], [-1, 8]], channel_multiplier=0).then_inc(S["jlt_ready"], 1)
                if kind_ == "h2":
                    pool.wait_ge(S["m_lo"], KD)
                    pool.dma_start(wr[:], w_router[0].rearrange("(k p) n -> p k n", p=P)).then_inc(S["wr_in"], 16)
                    pool_route(pool, L)
            pool_moe(pool, L)

        @blk.scalar
        def _(act_e):
            a = act_e
            A = nc.scalar.activation
            L = line(a, S["act_line"])
            staged = [0]
            yt = [0]

            def split_hi(i):
                for u in ahead(i):
                    if "m" not in u:
                        continue
                    raw_wait(a, u)
                    free_split(a, u["m"])
                    A(hl[:, u["m"] % HL, 0, :], raw[:, u["n"] % RAW], ACT.Copy).then_inc(S["hi_done"], 1)

            def to_stage(src, func=ACT.Copy):
                n = staged[0]
                wait(a, S["stage_used"], n - 1)
                staged[0] += 1
                A(stage[:, n % 2], src, func).then_inc(S["proj_free"], 1)

            for dst, src, n in ((gqk[:, 0], q_norm_g, HD), (gqk[:, 1], k_norm_g, HD), (dtb[:, 0], dt_bias, 32),
                                (dtb[:, 1], a_log, 32), (dskip[:], d_skip, 32),
                                (lamt.rearrange("p a d -> p (a d)"), lambda_qk.rearrange("o a d -> o (a d)"), 4 * HD)):
                a.dma_start(dst, src.to_broadcast([P, n])).then_inc(S["params_act"], 16)
            a.dma_start(wdt[:], w["w_in"][:, ODT:ODT + 32].rearrange("(k p) n -> p k n", p=P)).then_inc(S["params_act"], 16)
            a.wait_ge(S["par_ev"], 2)
            A(silc[:], colp[:, 64:72], ACT.Silu).then_inc(S["silu_c"], 1)
            a.wait_ge(S["trig_in"], 1)
            for r in range(2):
                ins = A(trig[:, 3 + r], trig[:, r * 2], ACT.Sin)
            ins.then_inc(S["trig_out"], 1)
            a.wait_ge(S["trig_in"], 2)
            A(lam[:, 2:4], lam[:, 0:2], ACT.Exp).then_inc(S["trig_out"], 1)
            for t in range(NT):
                a.wait_ge(S["x_in"], 16 * NT)
                A(hsplit[:].rearrange("p a b -> p (a b)"), x_rows[:, t, :], ACT.Square,
                  accum_out=stat[:, 4, t:t + 1]).then_inc(S["sq_done"], 1)
                a.wait_ge(S["sq_done"], t + 1)
            for j in range(4):
                a.wait_ge(S["mod_used"], 2 * j + 2)
                A(acc[0:1, j, :], psum[0:1, (7, 5)[j % 2], :], ACT.Copy).then_inc(S["row_ev"], 1)
            split_hi(-1)

            for i, s in enumerate(steps):
                split_hi(i)
                kind, tag, o0 = s["kind"], s["tag"], s["out0"]
                if kind == "h":
                    for k in range(KD):
                        a.wait_ge(S["h_tmp"], k + 1)
                        A(hT[:, k, 0, :], hsplit[:, k % 2], ACT.Copy).then_inc(S["h_hi"], 1)
                    a.wait_ge(S["params"], 16 * 9)
                    a.wait_ge(S["params_act"], 16 * 7)
                    A(wdt_hl[:, :, 0, :], wdt[:], ACT.Copy).then_inc(S["wdt_hi"], 1)
                    a.wait_ge(S["dtT_ps"], 1)
                    A(hsplit[0:32, 0, :], psum[0:32, 6, :], ACT.Copy).then_inc(S["dtT_ev"], 1)
                    a.wait_ge(S["dt_dve"], 1)
                    L(A(dwk[:, 2], dwk[:, 1], ACT.Exp))
                    A(dtb[:, 1], dtb[:, 1], ACT.Exp).then_inc(S["dt_exp"], 1)
                    a.wait_ge(S["dt_dve"], 2)
                    A(dwk[:, 4], dwk[:, 3], ACT.Ln).then_inc(S["dt_exp"], 1)
                    a.wait_ge(S["cum_ps"], 1)
                    A(expo[:].rearrange("p a t h -> p (a t h)"), psum[:, 5, 0:384], ACT.Exp).then_inc(S["cum_exp"], 1)
                elif kind in ("row", "col", "branch"):
                    for o in range(s["nout"]):
                        a.wait_ge(S["proj_done"], o0 + o + 1)
                        src = bank((o0 + o) % 4)
                        free = lambda ins: ins.then_inc(S["proj_free"], 1)
                        name = tag[0]
                        if name in "qk":
                            free(A(q_rows[:, "qk".index(name), o, :], src, ACT.Copy))
                        elif name == "v":
                            free(A(v_rows[:, o, :], src, ACT.Copy))
                        elif name in ("a", "b") and tag[1] == 0:
                            if name == "b":
                                a.wait_ge(S["spilled"], 16)
                            free(A(acc[:, tag[2] * 4 + o, :], src, ACT.Copy))
                        elif name in ("a", "b", "out", "sdn"):
                            to_stage(src)
                        elif name in ("ga", "gb"):
                            to_stage(src, ACT.Sigmoid)
                        elif name == "xs":
                            free(A(xbc[:, o, 3:], src, ACT.Copy))
                        elif name == "bc":
                            free(A(xbc[:, 4 + o, 3:], src, ACT.Copy))
                        elif name == "z":
                            free(A(z_rows[:, o, :], src, ACT.Silu))
                        elif name == "sgu":
                            A(sgu[:, o, 0:FE], src[:, 0:FE], ACT.Silu)
                            free(A(sgu[:, o, FE:], src[:, FE:], ACT.Copy))
                    if tag[0] == "v":
                        for n in range(2 * HALF):
                            c0 = tag[1] * 2 * HALF + n
                            a.wait_ge(S["qkT_ps"], c0 + 1)
                            A(qkT[:, n // HALF, n % HALF, :], bank(4 + n % 2), ACT.Copy).then_inc(S["qkT_ev"], 1)
                elif kind == "attn":
                    hf = tag
                    for n in range(4 * HALF + 4):
                        item = hf * 4 * HALF + n
                        if n < 4 * HALF:
                            j, qb = n // NT, n % NT
                            w_ = (qb + 1) * P
                            a.wait_ge(S["nmax"], item + 1)
                            wait(a, S["w_ready"], item - 1)
                            for m in range(2):
                                A(probs[:, n % 2, m, 0:w_], psum[:, (4, 0)[n % 2] + m, 0:w_], ACT.Exp,
                                  bias=sm[:, n % 4, m:m + 1], scale=0.125,
                                  accum_out=sm[:, n % 4, 2 + m:3 + m]).then_inc(S["p_exp"], 1)
                        if n >= 7 and n % NT == 3:
                            j = (n - 7) // NT
                            h = hf * HALF + j
                            a.wait_ge(S["yT_ps"], h + 1)
                            A(ya_hl[:, j, 0, :], bank(2), ACT.Copy, scale=colp[:, 96:97]).then_inc(S["yT_hi"], 1)
                        if 1 <= n <= 4 * HALF:
                            n_ = n - 1
                            qb = n_ % NT
                            a.wait_ge(S["wT_ps"], item)
                            wait(a, S["o_ps"], item - 2)
                            A(wT[:, n_ % 2, 0:qb + 1, :].rearrange("p a b -> p (a b)"), psum[:, 6, 0:(qb + 1) * P],
                              ACT.Copy).then_inc(S["wT_ev"], 1)
                        if 2 <= n <= 4 * HALF + 1:
                            n_ = n - 2
                            j, qb = n_ // NT, n_ % NT
                            a.wait_ge(S["o_ps"], item - 1)
                            if qb == 0:
                                wait(a, S["yT_ps"], hf * HALF + j - 1)
                            at = (j % 2) * NT + qb
                            A(o_rows[:, j % 2, qb, :], psum[:, (7, 3)[n_ % 2], 0:VD], ACT.Copy,
                              scale=sm[:, n_ % 4, 4:5])
                            A(o_sq[:], psum[:, (7, 3)[n_ % 2], 0:VD], ACT.Square, scale=sm[:, n_ % 4, 4:5],
                              accum_out=stat[:, 4, at:at + 1]).then_inc(S["o_ev"], 1)
                            a.wait_ge(S["o_ev"], item - 1)
                elif kind == "ssd":
                    g = tag

                    def square_sum(ch):
                        A(stage[:, 1], z_rows[:, ch, :], ACT.Square, accum_out=stat[:, 4, ch:ch + 1]).then_inc(
                            S["sq_done"], 1)
                        a.wait_ge(S["sq_done"], NT * (g + 1) + ch + 1)

                    for q in range(6):
                        a.wait_ge(S["conv_done"], 6 * g + q + 1)
                        A(cv[:, q], cv[:, q], ACT.Silu).then_inc(S["conv_silu"], 1)
                    for ch in range(NT):
                        a.wait_ge(S["tr_ps"], 4 * g + ch + 1)
                        A(xs_rows[:, ch, :], bank(ch % 2), ACT.Copy).then_inc(S["tr_ev"], 1)
                    a.wait_ge(S["cb_ps"], 2 * g + 1)
                    A(b_rows[:].rearrange("p a b -> p (a b)"), bank(2), ACT.Copy).then_inc(S["b_ev"], 1)
                    for ch in range(NT):
                        n = 4 * g + ch
                        a.wait_ge(S["seg_ps"], n + 1)
                        wait(a, S["yl_ps"], n - 1)
                        A(lm[:, ch % 2].rearrange("p h l -> p (h l)"), psum[:, 4:6].rearrange("p b n -> p (b n)"),
                          ACT.Exp).then_inc(S["seg_exp"], 1)
                        if ch >= 2:
                            a.wait_ge(S["y_ready"], n - 1)
                            square_sum(ch - 2)
                    for ch in (NT - 2, NT - 1):
                        a.wait_ge(S["y_ready"], 4 * g + ch + 1)
                        square_sum(ch)
                    for q in range(4):
                        h = HEADS + 4 * g + q
                        a.wait_ge(S["yT_ps"], h + 1)
                        A(yb_hl[:, q, 0, :], bank(q), ACT.Copy, scale=colp[:, 97 + 4 * g + q:98 + 4 * g + q]).then_inc(
                            S["yT_hi"], 1)
                elif kind == "merge":
                    for k in range(KD):
                        a.wait_ge(S["merged"], k + 1)
                        A(hT[:, k, 0, :], acc[:, k, :], ACT.Copy).then_inc(S["m_hi"], 1)
                elif kind == "h2":
                    for t in range(NT):
                        a.wait_ge(S["stage_used"], x2_at + t + 1)
                        A(h2r[:, t, :], x2[:, t, :], ACT.Square, accum_out=stat[:, 4, t:t + 1]).then_inc(
                            S["sq_done"], 1)
                    a.wait_ge(S["wr_in"], 16)
                    A(wr_hl[:, :, 0, :], wr[:], ACT.Copy).then_inc(S["wr_hi"], 1)
                    for k in range(KD):
                        a.wait_ge(S["h2T_ps"], k + 1)
                        A(hT[:, k, 0, :], bank(4 + k % 2), ACT.Copy).then_inc(S["h2T_hi"], 1)
                    a.wait_ge(S["lgT_ps"], 1)
                    A(stage[0:NE, 0, :], psum[0:NE, 6, :], ACT.Sigmoid).then_inc(S["lgT_ev"], 1)
                    a.wait_ge(S["lg_ps"], 1)
                    A(rt[:, 0].rearrange("p t e -> p (t e)"), psum[:, 4, 0:NT * NE], ACT.Copy).then_inc(S["lg_ev"], 1)
                elif kind == "sact":
                    for t in range(NT):
                        a.wait_ge(S["sT_ps"], t + 1)
                        A(sactT[:, :, 0, t * P:(t + 1) * P], psum[:, 4 + t % 2, 0:2 * P].rearrange(
                            "p (k t) -> p k t", t=P), ACT.Copy).then_inc(S["sT_hi"], 1)
            act_moe(a, A, L)

        @blk.tensor
        def _(pe):
            M = nc.tensor.matmul
            tr = nc.tensor.transpose

            def three(dst, lhs, rhs, first, last):
                M(dst, lhs(0), rhs(0), start=first, stop=False)
                M(dst, lhs(0), rhs(1), start=False, stop=False)
                return M(dst, lhs(1), rhs(0), start=False, stop=last)

            pe.wait_ge(S["params"], 16 * 9)
            pe.wait_ge(S["consts"], 1)
            tr(psum[:, 6, 0:113], pr1[0:113, :], ident[0:113, 0:113]).then_inc(S["par_T"], 1)
            tr(psum[:, 5, 0:96], pr2[0:96, :], ident[0:96, 0:96]).then_inc(S["par_T"], 1)

            for s in steps:
                kind, tag, o0 = s["kind"], s["tag"], s["out0"]
                if kind == "mod" and tag < 4:
                    if tag == 0:
                        pe.wait_ge(S["silu_c"], 1)
                    wait(pe, S["row_ev"], tag - 1)
                    for h, u in enumerate(s["u"]):
                        raw_wait(pe, u)
                        rows = raw[:, u["n"] % RAW].rearrange("p (k n) -> p k n", n=512)
                        for kk in range(4):
                            k = 4 * h + kk
                            ins = M(psum[0:1, (7, 5)[tag % 2], :], silc[:, k:k + 1], rows[:, kk, :], start=(k == 0),
                                    stop=(k == KD - 1))
                        ins.then_inc(S["mod_used"], 1)
                    for j in ((tag - 1,) if tag < 3 else (2, 3)):
                        if j < 0:
                            continue
                        pe.wait_ge(S["row_ev"], j + 1)
                        for b in range(4):
                            ins = M(psum[:, 6, 4 * j + b:4 * j + b + 1], acc[0:1, j, b * P:(b + 1) * P],
                                    ones[0:1, 0:1], start=True, stop=True)
                        ins.then_inc(S["mod_ps"], 1)
                elif kind == "mod":
                    pe.wait_ge(S["mod_used"], 2 * (tag + 1))
                    wait(pe, S["mod_ev"], tag)
                    M(bank(7), ones[:], modacc[:], start=True, stop=True).then_inc(S["mod_ps"], 1)
                elif kind == "h":
                    pe.wait_ge(S["xr_ready"], NT)
                    for k in range(KD):
                        wait(pe, S["h_tmp"], k - 1)
                        for t in range(NT):
                            ins = tr(psum[:, 4 + k % 2, t * P:(t + 1) * P], x_rows[:, t, k * P:(k + 1) * P], ident[:])
                        ins.then_inc(S["xT_ps"], 1)
                    pe.wait_ge(S["wdt_lo"], 1)
                    pe.wait_ge(S["h_lo"], KD)
                    for k in range(KD):
                        ins = three(psum[0:32, 6, :], lambda q: wdt_hl[:, k, q, :], lambda q: hT[:, k, q, :],
                                    k == 0, k == KD - 1)
                    ins.then_inc(S["dtT_ps"], 1)
                    pe.wait_ge(S["dtT_ev"], 1)
                    for t in range(NT):
                        ins = tr(psum[:, 4, t * 32:(t + 1) * 32], hsplit[0:32, 0, t * P:(t + 1) * P], ident[0:32, 0:32])
                    ins.then_inc(S["dt_ps"], 1)
                    pe.wait_ge(S["dt_a"], 1)
                    for q, tri in enumerate((upper, later, ones)):
                        for t in range(NT):
                            ins = M(psum[:, 5, (q * NT + t) * 32:(q * NT + t + 1) * 32], tri[:], aa[:, t, :],
                                    start=True, stop=True)
                    ins.then_inc(S["cum_ps"], 1)
                elif kind in ("row", "col", "branch"):
                    name = tag[0]
                    nk = len(s["u"]) * s["ks"]
                    wide = UNIT // s["ks"]
                    if name == "a":
                        pe.wait_ge(S["yT_lo"], HALF * (tag[1] + 1))
                    elif name == "b":
                        pe.wait_ge(S["yT_lo"], HEADS + 4 * (tag[1] + 1))
                    elif name == "out":
                        pe.wait_ge(S["m_lo"], KD)
                    elif name == "sgu":
                        pe.wait_ge(S["h2T_lo"], KD)
                    elif name == "sdn":
                        pe.wait_ge(S["sT_lo"], NT)
                    for ui, u in enumerate(s["u"]):
                        pe.wait_ge(S["lo_done"], u["m"] + 1)
                        wv = [hl[:, u["m"] % HL, q, :].rearrange("p (k n) -> p k n", n=wide) for q in range(2)]
                        for o in range(s["nout"]):
                            dst = bank((o0 + o) % 4)
                            if ui == 0:
                                wait(pe, S["proj_free"], o0 + o - 3)
                            for kk in range(s["ks"]):
                                k = ui * s["ks"] + kk
                                if name == "sdn":
                                    t, half = o // 2, o % 2
                                    lhs = lambda q: sactT[:, k, q, t * P:(t + 1) * P]
                                    rhs = lambda q: wv[q][:, kk, half * 512:(half + 1) * 512]
                                elif kind == "row":
                                    lhs = lambda q: hT[:, k, q, o * P:(o + 1) * P]
                                    rhs = lambda q: wv[q][:, kk, :]
                                else:
                                    y = {"a": ya_hl, "b": yb_hl}.get(name, hT)
                                    lhs = lambda q: wv[q][:, kk, o * P:(o + 1) * P]
                                    rhs = lambda q: y[:, k, q, :]
                                ins = three(dst, lhs, rhs, k == 0, k == nk - 1)
                            if ui == len(s["u"]) - 1:
                                ins.then_inc(S["proj_done"], 1)
                            elif o == s["nout"] - 1:
                                ins.then_inc(S["half_done"], 1)
                    if name == "v":
                        for n in range(2 * HALF):
                            c0 = tag[1] * 2 * HALF + n
                            xx, j = n // HALF, n % HALF
                            pe.wait_ge(S["qk_ready"], 2 * tag[1] + xx + 1)
                            if n >= 2:
                                pe.wait_ge(S["qkT_ev"], c0 - 1)
                            for t in range(NT):
                                ins = tr(psum[:, 4 + n % 2, t * P:(t + 1) * P],
                                         q_rows[:, xx, t, j * P:(j + 1) * P], ident[:])
                            ins.then_inc(S["qkT_ps"], 1)
                elif kind == "attn":
                    hf = tag
                    pe.wait_ge(S["qkT_ev"], 2 * HALF * (hf + 1))
                    pe.wait_ge(S["proj_free"], out_index[("v", hf)] + 4)
                    for n in range(4 * HALF + 4):
                        item = hf * 4 * HALF + n
                        if n < 4 * HALF:
                            j, qb = n // NT, n % NT
                            w_ = (qb + 1) * P
                            wait(pe, S["p_exp"], 2 * (item - 1))
                            for m in range(2):
                                dst = psum[:, (4, 0)[n % 2] + m, :]
                                rows = slice(m * HD, (m + 1) * HD)
                                M(dst[:, 0:w_], qkT[rows, 0, j, qb * P:(qb + 1) * P], qkT[rows, 1, j, 0:w_],
                                  start=True, stop=False, skip_group_check=True)
                                ins = M(dst[:, qb * P:w_], ident[:], causal[:], start=False, stop=True,
                                        skip_group_check=True)
                            ins.then_inc(S["sc_ps"], 1)
                        if n >= 7 and n % NT == 3:
                            j = (n - 7) // NT
                            h = hf * HALF + j
                            pe.wait_ge(S["o_ready"], h + 1)
                            wait(pe, S["yT_lo"], h)
                            for t in range(NT):
                                ins = tr(psum[:, 2, t * P:(t + 1) * P], o_rows[:, j % 2, t, :], ident[:])
                            ins.then_inc(S["yT_ps"], 1)
                        if 1 <= n <= 4 * HALF:
                            n_ = n - 1
                            pe.wait_ge(S["w_ready"], item)
                            wait(pe, S["wT_ev"], item - 1)
                            for b in range(n_ % NT + 1):
                                ins = tr(psum[:, 6, b * P:(b + 1) * P], wgt[:, n_ % 2, b * P:(b + 1) * P], ident[:])
                            ins.then_inc(S["wT_ps"], 1)
                        if 2 <= n <= 4 * HALF + 1:
                            n_ = n - 2
                            j, qb = n_ // NT, n_ % NT
                            pe.wait_ge(S["wT_ev"], item - 1)
                            wait(pe, S["o_ev"], item - 3)
                            for b in range(qb + 1):
                                ins = M(psum[:, (7, 3)[n_ % 2], 0:VD], wT[:, n_ % 2, b, :],
                                        v_rows[:, b, j * VD:(j + 1) * VD], start=(b == 0), stop=(b == qb))
                            ins.then_inc(S["o_ps"], 1)
                elif kind == "ssd":
                    g = tag
                    pe.wait_ge(S["proj_free"], out_index[("z", g)] + 4)
                    pe.wait_ge(S["conv_silu"], 6 * (g + 1))
                    for ch in range(NT):
                        wait(pe, S["tr_ev"], 4 * g + ch - 1 if ch >= 2 else 0)
                        for q in range(4):
                            ins = tr(psum[:, ch % 2, q * P:(q + 1) * P], cv[:, q, ch * P:(ch + 1) * P], ident[:])
                        ins.then_inc(S["tr_ps"], 1)
                    for ch in range(NT):
                        ins = tr(psum[:, 2, ch * P:(ch + 1) * P], cv[:, 4, ch * P:(ch + 1) * P], ident[:])
                    ins.then_inc(S["cb_ps"], 1)
                    for ch in range(NT):
                        cs = slice(ch * P, (ch + 1) * P)
                        ins = M(psum[:, 3, cs], cv[:, 4, cs], cv[:, 5, cs], start=True, stop=True)
                    ins.then_inc(S["cb_ps"], 1)

                    def segments(n):
                        pe.wait_ge(S["ua_ready"], n + 1)
                        wait(pe, S["seg_exp"], n)
                        for b in range(2):
                            ins = M(bank(4 + b), later[:], ua[:, 4 * b:4 * b + 4, :].rearrange("p h l -> p (h l)"),
                                    start=True, stop=True)
                        ins.then_inc(S["seg_ps"], 1)

                    segments(4 * g)
                    for ch in range(NT):
                        n = 4 * g + ch
                        pe.wait_ge(S["xd_ready"], n + 1)
                        if ch == 0:
                            pe.wait_ge(S["tr_ev"], 4 * g + 4)
                            pe.wait_ge(S["b_ev"], g + 1)
                        if ch < NT - 1:
                            if ch >= 2:
                                pe.wait_ge(S["st_ready"], n)
                            M(bank(ch % 2), b_rows[:, ch, :], xdt[:, 1, :], start=True, stop=True).then_inc(
                                S["u_ps"], 1)
                        pe.wait_ge(S["m_ready"], n + 1)
                        if ch >= 2:
                            pe.wait_ge(S["y_ready"], n - 1)
                        for h in range(GH):
                            ins = M(psum[:, (6, 3)[ch % 2], h * HP:(h + 1) * HP], lm[:, ch % 2, h, :],
                                    xdt[:, 0, h * HP:(h + 1) * HP], start=True, stop=True)
                        ins.then_inc(S["yl_ps"], 1)
                        if ch < NT - 1:
                            segments(n + 1)
                        pe.wait_ge(S["st_ready"], n + 1)
                        M(bank((7, 2)[ch % 2]), cv[:, 5, ch * P:(ch + 1) * P], state[:, ch % 2], start=True,
                          stop=True).then_inc(S["ys_ps"], 1)
                    pe.wait_ge(S["yn_ready"], g + 1)
                    for q in range(4):
                        for t in range(NT):
                            ins = tr(psum[:, q, t * P:(t + 1) * P], z_rows[:, t, q * P:(q + 1) * P], ident[:])
                        ins.then_inc(S["yT_ps"], 1)
                    pe.wait_ge(S["yT_lo"], HEADS + 4 * g + 4)
                elif kind == "h2":
                    pe.wait_ge(S["h2_row"], 1)
                    for k in range(KD):
                        wait(pe, S["h2T_lo"], k - 1)
                        for t in range(NT):
                            ins = tr(psum[:, 4 + k % 2, t * P:(t + 1) * P], h2r[:, t, k * P:(k + 1) * P], ident[:])
                        ins.then_inc(S["h2T_ps"], 1)
                    pe.wait_ge(S["wr_lo"], 1)
                    pe.wait_ge(S["h2T_lo"], KD)
                    for k in range(KD):
                        ins = three(psum[0:NE, 6, :], lambda q: wr_hl[:, k, q, :], lambda q: hT[:, k, q, :],
                                    k == 0, k == KD - 1)
                    ins.then_inc(S["lgT_ps"], 1)
                    pe.wait_ge(S["lgT_ev"], 1)
                    for t in range(NT):
                        ins = tr(psum[:, 4, t * NE:(t + 1) * NE], stage[0:NE, 0, t * P:(t + 1) * P], ident[0:NE, 0:NE])
                    ins.then_inc(S["lg_ps"], 1)
                elif kind == "sact":
                    pe.wait_ge(S["sel_ready"], NT)
                    for t in range(NT):
                        for j in range(t):
                            M(psum[:, 7, t * NE:(t + 1) * NE], ones[:], rt[:, 3, j, :], start=(j == 0), stop=False)
                        M(psum[:, 7, t * NE:(t + 1) * NE], before[:], rt[:, 3, t, :], start=(t == 0), stop=True)
                    for j in range(NT):
                        ins = M(psum[:, 7, NT * NE:(NT + 1) * NE], ones[:], rt[:, 3, j, :], start=(j == 0),
                                stop=(j == NT - 1))
                    ins.then_inc(S["pos_ps"], 1)
                    for t in range(NT):
                        pe.wait_ge(S["sa_ready"], t + 1)
                        wait(pe, S["sT_lo"], t - 1)
                        for k in range(2):
                            ins = tr(psum[:, 4 + t % 2, k * P:(k + 1) * P], sgu[:, t, k * P:(k + 1) * P], ident[:])
                        ins.then_inc(S["sT_ps"], 1)
            pe_moe(pe, M, tr, three)

        @blk.vector
        def _(v):
            V = nc.vector
            L = line(v, S["vec_line"])
            TS, TT, STT = V.tensor_scalar, V.tensor_tensor, V.scalar_tensor_tensor
            used = [0]
            taken = [0]

            def inverse_root(n):
                v_, h_, w_, y_ = (stat[:, q, 0:n] for q in range(4))
                V.tensor_single_scalar(w_.bitcast(I32), v_.bitcast(I32), 1, ALU.arith_shift_right)
                L(TS(h_, v_, -0.5, None, ALU.mult))
                L(TS(y_.bitcast(I32), w_.bitcast(I32), -1.0, float(0x5F3759DF), ALU.mult, ALU.add))
                for _ in range(3):
                    L(TT(w_, y_, y_, ALU.mult))
                    L(TT(w_, w_, h_, ALU.mult))
                    L(STT(out=y_, in0=w_, scalar=1.5, in1=y_, op0=ALU.add, op1=ALU.mult))

            def mean_eps(src, n, width, gain=1.0):
                L(TS(stat[:, 0, 0:n], src, 1.0 / (width * gain ** 2), EPS / gain ** 2, ALU.mult, ALU.add))

            def take_mod(upto):
                while taken[0] < upto:
                    j = taken[0]
                    taken[0] += 1
                    if j < 4:
                        v.wait_ge(S["mod_ps"], 4)
                        TT(shT[:, j * 4:j * 4 + 4], psum[:, 6, j * 4:j * 4 + 4], colp[:, j * 4:j * 4 + 4], ALU.add).then_inc(
                            S["mod_ev"], 1)
                    else:
                        v.wait_ge(S["mod_ps"], j + 1)
                        v.wait_ge(S["g_in"], 64)
                        dst = {2: g1b, 3: sh2b, 4: a2b, 5: g2b}[j // 2][:, (j % 2) * 512:(j % 2 + 1) * 512]
                        TT(dst, dst, bank(7), ALU.add).then_inc(S["mod_ev"], 1)
                    v.wait_ge(S["mod_ev"], j + 1)

            def split_lo(i):
                for u in ahead(i):
                    r = raw[:, u["n"] % RAW]
                    if "m" in u:
                        v.wait_ge(S["hi_done"], u["m"] + 1)
                        h_ = hl[:, u["m"] % HL]
                        TT(h_[:, 1, :], r, h_[:, 0, :].bitcast(F32), ALU.subtract).then_inc(S["lo_done"], 1)
                        continue
                    if u["mod"] <= 8:
                        continue
                    raw_wait(v, u)
                    half = (u["mod"] - 1) % 2
                    if half == 0:
                        take_mod((u["mod"] - 1) // 2)
                    for kk in range(4):
                        k = half * 4 + kk
                        src = r.rearrange("p (k n) -> p k n", n=512)[:, kk, :]
                        if k == 0:
                            ins = TS(modacc[:], src, silc[:, 0:1], None, ALU.mult)
                        else:
                            ins = STT(out=modacc[:], in0=src, scalar=silc[:, k:k + 1], in1=modacc[:], op0=ALU.mult,
                                      op1=ALU.add)
                        if kk < 3:
                            L(ins)
                    ins.then_inc(S["mod_used"], 1)
                    v.wait_ge(S["mod_used"], u["mod"])

            def staged():
                used[0] += 1
                return stage[:, (used[0] - 1) % 2]

            v.wait_ge(S["par_T"], 1)
            V.tensor_copy(colp[:], psum[:, 6, 0:113]).then_inc(S["par_ev"], 1)
            v.wait_ge(S["par_T"], 2)
            V.tensor_copy(convw[:], psum[:, 5, 0:96]).then_inc(S["par_ev"], 1)
            v.wait_ge(S["par_ev"], 2)
            v.wait_ge(S["params_act"], 16 * 7)
            L(V.tensor_copy(posf[:], posi[:]))
            t32 = lambda n: trig[:, n].rearrange("p (t i) -> p t i", i=32)
            L(TT(t32(0), posf[:].unsqueeze(2).to_broadcast([P, NT, 32]), freq[:].unsqueeze(1).to_broadcast([P, NT, 32]),
                 ALU.mult))
            magic = 12582912.0
            L(TS(trig[:, 1], trig[:, 0], float(np.float32(1 / TWO_PI)), magic, ALU.mult, ALU.add))
            L(TS(trig[:, 1], trig[:, 1], magic, None, ALU.subtract))
            c1 = 6.28125
            c2 = float(np.float32(int((TWO_PI - c1) * 2 ** 20) / 2 ** 20))
            c3 = float(np.float32(TWO_PI - c1 - c2))
            for part in (c1, c2, c3):
                L(STT(out=trig[:, 0], in0=trig[:, 1], scalar=-part, in1=trig[:, 0], op0=ALU.mult, op1=ALU.add))
            L(TS(trig[:, 2], trig[:, 0], float(np.float32(np.pi / 2)), None, ALU.add))
            L(TS(trig[:, 1], trig[:, 2], float(np.float32(np.pi)), -TWO_PI, ALU.is_gt, ALU.mult))
            L(TT(trig[:, 2], trig[:, 2], trig[:, 1], ALU.add))
            L(TS(trig[:, 0], trig[:, 0], 3.1415925, -3.1415925, ALU.min, ALU.max))
            TS(trig[:, 2], trig[:, 2], 3.1415925, -3.1415925, ALU.min, ALU.max).then_inc(S["trig_in"], 1)
            prod = stage[:, 0, 0:2 * HD].rearrange("p (a d) -> p a d", d=HD)
            L(TT(prod, lamt[:, 0::2, :], lamt[:, 1::2, :], ALU.mult))
            V.tensor_reduce(lam[:, 0:2], prod, AX, ALU.add).then_inc(S["trig_in"], 1)
            v.wait_ge(S["trig_out"], 2)
            L(TT(lam[:, 4:5], lam[:, 3:4], lam[:, 2:3], ALU.subtract))
            L(TS(lam[:, 4:5], lam[:, 4:5], LAMBDA_INIT, None, ALU.subtract))
            for x_ in range(2):
                for half in range(2):
                    here = gqk[:, x_, half * 32:(half + 1) * 32].unsqueeze(1).to_broadcast([P, NT, 32])
                    other = gqk[:, x_, (1 - half) * 32:(2 - half) * 32].unsqueeze(1).to_broadcast([P, NT, 32])
                    L(TT(tabs[:, x_, 0, :, half * 32:(half + 1) * 32], t32(4), here, ALU.mult))
                    L(TT(tabs[:, x_, 1, :, half * 32:(half + 1) * 32], t32(3), other, ALU.mult))
                L(TS(tabs[:, x_, 1, :, 0:32], tabs[:, x_, 1, :, 0:32], -1.0, None, ALU.mult))
            v.wait_ge(S["sq_done"], NT)
            mean_eps(stat[:, 4, 0:NT], NT, D)
            inverse_root(NT)
            for t in range(NT):
                TS(x_rows[:, t, :], x_rows[:, t, :], stat[:, 3, t:t + 1], None, ALU.mult).then_inc(S["xr_ready"], 1)
            v.wait_ge(S["silu_c"], 1)
            split_lo(-1)

            for i, s in enumerate(steps):
                split_lo(i)
                kind, tag, o0 = s["kind"], s["tag"], s["out0"]
                name = tag[0] if isinstance(tag, tuple) else None
                if kind == "mod":
                    take_mod(tag + 1)
                elif kind == "h":
                    L(TS(a1T[:], shT[:, 8:16], 1.0, None, ALU.add))
                    L(TT(a1T[:], a1T[:], colp[:, 48:56], ALU.mult))
                    for k in range(KD + 1):
                        if k < KD:
                            v.wait_ge(S["xT_ps"], k + 1)
                            wait(v, S["h_lo"], k - 1)
                            TS(hsplit[:, k % 2], bank(4 + k % 2), a1T[:, k:k + 1], shT[:, k:k + 1], ALU.mult,
                               ALU.add).then_inc(S["h_tmp"], 1)
                        if k:
                            v.wait_ge(S["h_tmp"], k)
                            v.wait_ge(S["h_hi"], k)
                            TT(hT[:, k - 1, 1, :], hsplit[:, (k - 1) % 2], hT[:, k - 1, 0, :].bitcast(F32),
                               ALU.subtract).then_inc(S["h_lo"], 1)
                    v.wait_ge(S["wdt_hi"], 1)
                    TT(wdt_hl[:, :, 1, :], wdt[:], wdt_hl[:, :, 0, :].bitcast(F32), ALU.subtract).then_inc(S["wdt_lo"], 1)
                    th = lambda n: dwk[:, n].rearrange("p (t h) -> p t h", h=32)
                    over_h = lambda ap: ap.unsqueeze(1).to_broadcast([P, NT, 32])
                    v.wait_ge(S["dt_ps"], 1)
                    L(TT(th(0), psum[:, 4, 0:NT * 32].rearrange("p (t h) -> p t h", h=32), over_h(dtb[:, 0]), ALU.add))
                    L(TS(dwk[:, 5], dwk[:, 0], 0.0, None, ALU.max))
                    STT(out=dwk[:, 1], in0=dwk[:, 5], scalar=-2.0, in1=dwk[:, 0], op0=ALU.mult,
                        op1=ALU.add).then_inc(S["dt_dve"], 1)
                    v.wait_ge(S["dt_exp"], 1)
                    TS(dwk[:, 3], dwk[:, 2], 1.0, None, ALU.add).then_inc(S["dt_dve"], 1)
                    v.wait_ge(S["dt_dve"], 2)
                    L(TS(dwk[:, 1], dwk[:, 3], 1.0, 1e-30, ALU.subtract, ALU.max))
                    L(V.reciprocal(dwk[:, 1], dwk[:, 1]))
                    v.wait_ge(S["dt_exp"], 2)
                    L(TT(dwk[:, 2], dwk[:, 2], dwk[:, 1], ALU.mult))
                    L(TT(dwk[:, 2], dwk[:, 2], dwk[:, 4], ALU.mult))
                    dt_ = dtp[:].rearrange("p t h -> p (t h)")
                    L(TT(dt_, dwk[:, 2], dwk[:, 5], ALU.add))
                    L(TT(aa[:], dtp[:], over_h(dtb[:, 1]), ALU.mult))
                    TS(aa[:], aa[:], -1.0, None, ALU.mult).then_inc(S["dt_a"], 1)
                    v.wait_ge(S["cum_exp"], 1)
                    L(TT(dtdec[:], dtp[:], expo[:, 1], ALU.mult))
                elif name in ("q", "k"):
                    x_ = "qk".index(name)
                    vec = lambda ap: ap.rearrange("p (c d) -> p c d", d=HD)
                    for t in range(NT):
                        v.wait_ge(S["proj_free"], o0 + t + 1)
                        row = q_rows[:, x_, t, :]
                        L(TT(stage[:, 0], row, row, ALU.mult))
                        L(V.tensor_reduce(stat[:, 4, t * 8:(t + 1) * 8], vec(stage[:, 0]), AX, ALU.add))
                    mean_eps(stat[:, 4, 0:32], 32, HD)
                    for t in range(NT):
                        row = vec(q_rows[:, x_, t, :])
                        plain = tabs[:, x_, 0, t, :].unsqueeze(1).to_broadcast([P, 8, HD])
                        swap = lambda h_: tabs[:, x_, 1, t, h_ * 32:(h_ + 1) * 32].unsqueeze(1).to_broadcast([P, 8, 32])
                        s0, s1 = vec(stage[:, 0]), vec(stage[:, 1])
                        TT(s0[:, :, 0:32], row[:, :, 32:64], swap(0), ALU.mult)
                        L(TT(s0[:, :, 32:64], row[:, :, 0:32], swap(1), ALU.mult))
                        L(TT(s1, row, plain, ALU.mult))
                        L(TT(row, s0, s1, ALU.add))
                    inverse_root(32)
                    for t in range(NT):
                        row = vec(q_rows[:, x_, t, :])
                        ins = TT(row, row, stat[:, 3, t * 8:(t + 1) * 8].unsqueeze(2).to_broadcast([P, 8, HD]), ALU.mult)
                        if t < NT - 1:
                            L(ins)
                    ins.then_inc(S["qk_ready"], 1)
                    v.wait_ge(S["qk_ready"], 2 * tag[1] + x_ + 1)
                elif kind == "attn":
                    hf = tag

                    def weights(n):
                        item = hf * 4 * HALF + n
                        w_ = (n % NT + 1) * P
                        k = sm[:, n % 4]
                        v.wait_ge(S["p_exp"], 2 * (item + 1))
                        L(V.reciprocal(k[:, 4:6], k[:, 2:4]))
                        L(TT(k[:, 6:7], k[:, 2:3], k[:, 5:6], ALU.mult))
                        L(TT(k[:, 6:7], k[:, 6:7], lam[:, 4:5], ALU.mult))
                        wait(v, S["wT_ps"], item - 1)
                        STT(out=wgt[:, n % 2, 0:w_], in0=probs[:, n % 2, 1, 0:w_], scalar=k[:, 6:7],
                            in1=probs[:, n % 2, 0, 0:w_], op0=ALU.mult, op1=ALU.add).then_inc(S["w_ready"], 1)
                        v.wait_ge(S["w_ready"], item + 1)

                    for n in range(4 * HALF + 4):
                        item = hf * 4 * HALF + n
                        if 1 <= n <= 4 * HALF:
                            weights(n - 1)
                        if n < 4 * HALF:
                            w_ = (n % NT + 1) * P
                            b0 = (4, 0)[n % 2]
                            v.wait_ge(S["sc_ps"], item + 1)
                            wait(v, S["o_ev"], item - 3)
                            L(V.tensor_reduce(sm[:, n % 4, 0:2], psum[:, b0:b0 + 2, 0:w_], AX, ALU.max))
                            TS(sm[:, n % 4, 0:2], sm[:, n % 4, 0:2], -0.125, None, ALU.mult).then_inc(S["nmax"], 1)
                        if n >= 6 and n % NT == 2:
                            j = (n - 6) // NT
                            rows = o_rows[:, j % 2]
                            v.wait_ge(S["o_ev"], item - 2)
                            at = (j % 2) * NT
                            mean_eps(stat[:, 4, at:at + NT], NT, VD, 1.0 - LAMBDA_INIT)
                            inverse_root(NT)
                            TT(rows, rows, stat[:, 3, 0:NT].unsqueeze(2).to_broadcast([P, NT, VD]),
                               ALU.mult).then_inc(S["o_ready"], 1)
                        if n >= 7 and n % NT == 3:
                            j = (n - 7) // NT
                            v.wait_ge(S["yT_hi"], hf * HALF + j + 1)
                            STT(out=ya_hl[:, j, 1, :], in0=bank(2), scalar=colp[:, 96:97],
                                in1=ya_hl[:, j, 0, :].bitcast(F32), op0=ALU.mult, op1=ALU.subtract).then_inc(S["yT_lo"], 1)
                elif name in ("a", "b") and kind == "branch" and tag[1] > 0:
                    for o in range(4):
                        v.wait_ge(S["proj_free"], o0 + o + 1)
                        dst = acc[:, tag[2] * 4 + o, :]
                        TT(dst, dst, staged(), ALU.add).then_inc(S["stage_used"], 1)
                        v.wait_ge(S["stage_used"], used[0])
                elif name in ("ga", "gb"):
                    for o in range(4):
                        v.wait_ge(S["proj_free"], o0 + o + 1)
                        dst = acc[:, tag[1] * 4 + o, :]
                        TT(dst, dst, staged(), ALU.mult).then_inc(S["stage_used"], 1)
                        v.wait_ge(S["stage_used"], used[0])
                elif kind == "ssd":
                    g = tag
                    hd = lambda ap: ap.rearrange("p (h d) -> p h d", d=HP)
                    per_h = lambda ap: ap[:, g * GH:(g + 1) * GH].unsqueeze(2).to_broadcast([P, GH, HP])
                    if g == 0:
                        L(V.memset(xbc[:, :, 0:3], 0.0))
                    for q in range(6):
                        ct = 4 * g + q if q < 4 else 16 + 4 * (q - 4) + g
                        v.wait_ge(S["proj_free"], (out_index[("xs", g)] + q if q < 4 else out_index[("bc", g)] + q - 4) + 1)
                        if q == 0 and g:
                            v.wait_ge(S["proj_done"], out_index[("b", g - 1, 1)] + 4)
                        tap = lambda k: convw[:, k * 24 + ct:k * 24 + ct + 1]
                        L(TS(cv[:, q], xbc[:, q, 0:T], tap(0), colp[:, 72 + ct:73 + ct], ALU.mult, ALU.add))
                        for k in range(1, 4):
                            ins = STT(out=cv[:, q], in0=xbc[:, q, k:k + T], scalar=tap(k), in1=cv[:, q], op0=ALU.mult,
                                      op1=ALU.add)
                            if k < 3:
                                L(ins)
                        ins.then_inc(S["conv_done"], 1)
                    v.wait_ge(S["cb_ps"], 2 * g + 2)
                    L(TT(cbm[:], bank(3).rearrange("p (c l) -> p c l", l=P),
                         upper[:].unsqueeze(1).to_broadcast([P, NT, P]), ALU.mult))
                    v.wait_ge(S["tr_ev"], 4 * g + 4)
                    V.memset(state[:, 0], 0.0).then_inc(S["st_ready"], 1)

                    def chunk_inputs(ch):
                        n = 4 * g + ch
                        wait(v, S["yl_ps"], n)
                        L(TT(hd(xdt[:, 0]), hd(xs_rows[:, ch, :]), per_h(dtp[:, ch, :]), ALU.mult))
                        TT(hd(xdt[:, 1]), hd(xs_rows[:, ch, :]), per_h(dtdec[:, ch, :]), ALU.mult).then_inc(
                            S["xd_ready"], 1)
                        v.wait_ge(S["seg_exp"], n + 1)
                        TT(lm[:, ch % 2], lm[:, ch % 2], cbm[:, ch, :].unsqueeze(1).to_broadcast([P, GH, P]),
                           ALU.mult).then_inc(S["m_ready"], 1)

                    chunk_inputs(0)
                    for ch in range(NT):
                        n = 4 * g + ch
                        if ch < NT - 1:
                            new, old = state[:, (ch + 1) % 2], state[:, ch % 2]
                            L(TT(hd(new), hd(old), per_h(expo[:, 2, ch, :]), ALU.mult))
                            v.wait_ge(S["u_ps"], (NT - 1) * g + ch + 1)
                            TT(new, new, bank(ch % 2), ALU.add).then_inc(S["st_ready"], 1)
                            v.wait_ge(S["st_ready"], n + 2)
                            chunk_inputs(ch + 1)
                        v.wait_ge(S["ys_ps"], n + 1)
                        wait(v, S["y_ready"], n)
                        tmp = stage[:, 0]
                        L(TT(hd(tmp), hd(bank((7, 2)[ch % 2])), per_h(expo[:, 0, ch, :]), ALU.mult))
                        L(TT(tmp, tmp, bank((6, 3)[ch % 2]), ALU.add))
                        v.wait_ge(S["skipped"], n + 1)
                        L(TT(tmp, tmp, xs_rows[:, ch, :], ALU.add))
                        TT(z_rows[:, ch, :], z_rows[:, ch, :], tmp, ALU.mult).then_inc(S["y_ready"], 1)
                    v.wait_ge(S["sq_done"], NT * (g + 2))
                    mean_eps(stat[:, 4, 0:NT], NT, 512)
                    inverse_root(NT)
                    for t in range(NT):
                        ins = TS(z_rows[:, t, :], z_rows[:, t, :], stat[:, 3, t:t + 1], None, ALU.mult)
                    ins.then_inc(S["yn_ready"], 1)
                    for q in range(4):
                        h = HEADS + 4 * g + q
                        v.wait_ge(S["yT_hi"], h + 1)
                        STT(out=yb_hl[:, q, 1, :], in0=bank(q), scalar=colp[:, 97 + 4 * g + q:98 + 4 * g + q],
                            in1=yb_hl[:, q, 0, :].bitcast(F32), op0=ALU.mult, op1=ALU.subtract).then_inc(S["yT_lo"], 1)
                elif kind == "merge":
                    v.wait_ge(S["ga_in"], 32)
                    v.wait_ge(S["proj_done"], out_index[("gb", 1)] + 4)
                    for k in range(KD):
                        TT(acc[:, k, :], acc[:, k, :], ga_back[:, k, :], ALU.add).then_inc(S["merged"], 1)
                    for k in range(KD):
                        v.wait_ge(S["m_hi"], k + 1)
                        TT(hT[:, k, 1, :], acc[:, k, :], hT[:, k, 0, :].bitcast(F32), ALU.subtract).then_inc(S["m_lo"], 1)
                elif name in ("out", "sdn"):
                    v.wait_ge(S["x2_in"], 16 * NT)
                    for o in range(s["nout"]):
                        t, half = (o, tag[1]) if name == "out" else (o // 2, o % 2)
                        cols = slice(half * 512, (half + 1) * 512)
                        v.wait_ge(S["proj_free"], o0 + o + 1)
                        buf = staged()
                        L(TT(buf, buf, (g1b if name == "out" else g2b)[:, cols], ALU.mult))
                        TT(x2[:, t, cols], x2[:, t, cols], buf, ALU.add).then_inc(S["stage_used"], 1)
                        v.wait_ge(S["stage_used"], used[0])
                elif kind == "h2":
                    L(TS(a2b[:], a2b[:], 1.0, None, ALU.add))
                    TT(a2b[:], a2b[:], n2b[:], ALU.mult).then_inc(S["x2_ready"], 1)
                    v.wait_ge(S["x2_ready"], 1)
                    v.wait_ge(S["sq_done"], NT * (G4 + 2))
                    mean_eps(stat[:, 4, 0:NT], NT, D)
                    inverse_root(NT)
                    for t in range(NT):
                        L(STT(out=h2r[:, t, :], in0=x2[:, t, :], scalar=stat[:, 3, t:t + 1], in1=a2b[:], op0=ALU.mult,
                              op1=ALU.mult))
                        ins = TT(h2r[:, t, :], h2r[:, t, :], sh2b[:], ALU.add)
                        if t < NT - 1:
                            L(ins)
                    ins.then_inc(S["h2_row"], 1)
                    v.wait_ge(S["wr_hi"], 1)
                    TT(wr_hl[:, :, 1, :], wr[:], wr_hl[:, :, 0, :].bitcast(F32), ALU.subtract).then_inc(S["wr_lo"], 1)
                    for k in range(KD):
                        v.wait_ge(S["h2T_hi"], k + 1)
                        TT(hT[:, k, 1, :], bank(4 + k % 2), hT[:, k, 0, :].bitcast(F32), ALU.subtract).then_inc(
                            S["h2T_lo"], 1)
                    route(v, L)
                elif kind == "sact":
                    slots(v, L)
                    for t in range(NT):
                        v.wait_ge(S["proj_free"], out_index[("sgu", 0)] + t + 1)
                        TT(sgu[:, t, 0:FE], sgu[:, t, 0:FE], sgu[:, t, FE:], ALU.mult).then_inc(S["sa_ready"], 1)
                        v.wait_ge(S["sT_hi"], t + 1)
                        TT(sactT[:, :, 1, t * P:(t + 1) * P], psum[:, 4 + t % 2, 0:2 * P].rearrange(
                            "p (k t) -> p k t", t=P), sactT[:, :, 0, t * P:(t + 1) * P].bitcast(F32),
                            ALU.subtract).then_inc(S["sT_lo"], 1)
                    gates_and_counts(v, L)
            vec_moe(v, L)


def kernel(x, c, positions, w_ada, b_ada, norm1_g, w_in, q_norm_g, k_norm_g, lambda_qk, subln_g,
           conv_w, conv_b, dt_bias, a_log, d_skip, ssd_norm_g, w_branch_a, w_branch_b, w_out,
           norm2_g, w_router, router_bias, w_exp_gate, w_exp_up, w_exp_down,
           w_sh_gate, w_sh_up, w_sh_down):
    import concourse.bacc as bacc
    from concourse.bass_utils import run_bass_kernel_spmd

    inputs = dict(locals())
    for name in ("bacc", "run_bass_kernel_spmd"):
        inputs.pop(name)
    nc = bacc.Bacc("TRN2", target_bir_lowering=False, num_devices=1)
    arrays, args = {}, {}
    for name, value in inputs.items():
        value = np.ascontiguousarray(value)
        arrays[f"in_{name}"] = value
        args[name] = nc.dram_tensor(f"in_{name}", value.shape, mybir.dt.from_np(value.dtype),
                                    kind="ExternalInput").ap()
    out = nc.dram_tensor("out", (1, T, D), F32, kind="ExternalOutput").ap()
    build(nc, out=out, **args)
    result = run_bass_kernel_spmd(nc, [arrays], core_ids=[0])
    return result.results[0]["out"]
```
